# Optimizing a Trainium2 kernel written in Bass

```python
import jax, jax.numpy as jnp
from jax import lax
import numpy as np

D_MODEL = 1024
BATCH = 1
SEQ = 256
DEPTH = 2

GRID_W = 64
CTX_LEN = 256

RWKV_HEADS = 8
RWKV_HEAD_DIM = 64
RWKV_WIDTH = RWKV_HEADS * RWKV_HEAD_DIM
DECAY_LORA = 64
AAA_LORA = 64
GATE_LORA = 128
N_DIR = 2
GN_EPS = 64e-5

MLA_HEADS = 8
QK_NOPE = 64
QK_ROPE = 32
QK_HEAD = QK_NOPE + QK_ROPE
V_HEAD = 64
MLA_WIDTH = MLA_HEADS * V_HEAD
Q_LORA = 384
KV_LORA = 128
ROPE_AXIS = QK_ROPE // 2
ROPE_THETA = 10000.0
Q_BLOCK = 128

FNO_GROUPS = 8
FNO_GROUP_DIM = 64
FNO_WIDTH = FNO_GROUPS * FNO_GROUP_DIM

N_BRANCH = 3
N_RWKV_IN = 3 * RWKV_WIDTH + N_DIR * DECAY_LORA + N_DIR * AAA_LORA + GATE_LORA
N_MLA_IN = Q_LORA + KV_LORA + QK_ROPE
N_IN = N_RWKV_IN + N_MLA_IN + FNO_WIDTH + N_BRANCH * D_MODEL
IN_SPLITS = (N_RWKV_IN, N_RWKV_IN + N_MLA_IN, N_RWKV_IN + N_MLA_IN + FNO_WIDTH)
RWKV_SPLITS = (RWKV_WIDTH, 2 * RWKV_WIDTH, 3 * RWKV_WIDTH,
               3 * RWKV_WIDTH + N_DIR * DECAY_LORA,
               3 * RWKV_WIDTH + N_DIR * DECAY_LORA + N_DIR * AAA_LORA)

FFN_HIDDEN = ((8 * D_MODEL + 3 * 256 - 1) // (3 * 256)) * 256
RMS_EPS = 1e-6

kernel_name = "hybrid_rwkv7_mla_fnet_dit_block"

def rms_norm(x, g):
    xf = x.astype(jnp.float32)
    y = xf * lax.rsqrt(jnp.mean(xf * xf, axis=-1, keepdims=True) + RMS_EPS)
    return (y * g.astype(jnp.float32)).astype(x.dtype)

def modulate(h, shift, scale):
    return h * (1.0 + scale) + shift

def centred_shift_mix(z, mu_prev, mu_next):
    z_prev = jnp.pad(z, ((0, 0), (1, 0), (0, 0)))[:, :-1]
    z_next = jnp.pad(z, ((0, 0), (0, 1), (0, 0)))[:, 1:]
    return z + (z_prev - z) * mu_prev + (z_next - z) * mu_next

def rwkv_features(z, p):
    z = centred_shift_mix(z, p["mu_prev"], p["mu_next"])
    B, T, _ = z.shape
    r, k, v, zw, za, zg = jnp.split(z, RWKV_SPLITS, axis=-1)
    heads = lambda t: t.reshape(B, T, RWKV_HEADS, RWKV_HEAD_DIM)
    dir_heads = lambda t: t.reshape(B, T, N_DIR, RWKV_HEADS, RWKV_HEAD_DIM)
    zw = jnp.tanh(zw.reshape(B, T, N_DIR, DECAY_LORA))
    w_log = -jax.nn.softplus(-(p["w0"] + jnp.einsum("btdr,drc->btdc", zw, p["w2"]))) - 0.5
    decay = jnp.exp(-jnp.exp(w_log.astype(jnp.float32)))
    a = jax.nn.sigmoid(p["a0"] + jnp.einsum("btdr,drc->btdc", za.reshape(B, T, N_DIR, AAA_LORA), p["a2"]))
    g = jax.nn.sigmoid(zg) @ p["g2"]
    kk = heads(k * p["k_k"]).astype(jnp.float32)
    kk = kk / jnp.maximum(jnp.sqrt(jnp.sum(kk * kk, axis=-1, keepdims=True)), 1e-12)
    k_dir = k[:, :, None, :] * (1.0 + (a - 1.0) * p["k_a"])
    b_dir = kk[:, :, None] * dir_heads(a).astype(jnp.float32)
    return dict(r=heads(r), v=heads(v), kk=kk, g=g, decay=dir_heads(decay), k=dir_heads(k_dir), b=b_dir)

def rwkv_scan(state0, f, d, reverse):
    seq = (f["r"], f["decay"][:, :, d], f["k"][:, :, d], f["v"], f["kk"], f["b"][:, :, d])
    xs = tuple(jnp.moveaxis(t.astype(jnp.float32), 1, 0) for t in seq)

    def step(S, inp):
        r_t, w_t, k_t, v_t, kk_t, b_t = inp
        sa = -jnp.einsum("bhvk,bhk->bhv", S, kk_t)
        S = S * w_t[:, :, None, :] + sa[..., None] * b_t[:, :, None, :] + v_t[..., None] * k_t[:, :, None, :]
        return S, jnp.einsum("bhvk,bhk->bhv", S, r_t)

    S, ys = lax.scan(step, state0, xs, reverse=reverse)
    return S, jnp.moveaxis(ys, 0, 1)

def rwkv_output(y, f, p):
    B, T = y.shape[:2]
    mu = jnp.mean(y, axis=-1, keepdims=True)
    var = jnp.mean(jnp.square(y - mu), axis=-1, keepdims=True)
    yn = ((y - mu) * lax.rsqrt(var + GN_EPS)).reshape(B, T, RWKV_WIDTH) * p["gn_w"] + p["gn_b"]
    k_sum = f["k"].sum(axis=2)
    bonus = jnp.sum(f["r"] * p["r_k"] * k_sum, axis=-1, keepdims=True) * f["v"]
    o = (yn + bonus.reshape(B, T, RWKV_WIDTH)) * f["g"]
    return o.astype(f["g"].dtype) @ p["w_rwkv_o"]

def axial_rope_angles(n_tokens):
    rows = n_tokens // GRID_W
    row = jnp.broadcast_to(jnp.arange(rows)[:, None], (rows, GRID_W)).reshape(-1).astype(jnp.float32)
    col = jnp.broadcast_to(jnp.arange(GRID_W)[None, :], (rows, GRID_W)).reshape(-1).astype(jnp.float32)
    inv_freq = ROPE_THETA ** (-jnp.arange(0, ROPE_AXIS, 2, dtype=jnp.float32) / ROPE_AXIS)
    return row[:, None] * inv_freq, col[:, None] * inv_freq

def rotate_half(t, ang):
    t1, t2 = jnp.split(t, 2, axis=-1)
    cos = jnp.cos(ang)[:, None, :].astype(t.dtype)
    sin = jnp.sin(ang)[:, None, :].astype(t.dtype)
    return jnp.concatenate([t1 * cos - t2 * sin, t2 * cos + t1 * sin], axis=-1)

def apply_axial_rope(t, angles):
    ang_row, ang_col = angles
    t_nope, t_row, t_col = jnp.split(t, (QK_NOPE, QK_NOPE + ROPE_AXIS), axis=-1)
    return jnp.concatenate([t_nope, rotate_half(t_row, ang_row), rotate_half(t_col, ang_col)], axis=-1)

def mla_qkv(z, p, angles):
    B, T, _ = z.shape
    c_q, c_kv, k_rope = jnp.split(z, (Q_LORA, Q_LORA + KV_LORA), axis=-1)
    q = (rms_norm(c_q, p["g_cq"]) @ p["w_uq"]).reshape(B, T, MLA_HEADS, QK_HEAD)
    kv = (rms_norm(c_kv, p["g_ckv"]) @ p["w_ukv"]).reshape(B, T, MLA_HEADS, QK_NOPE + V_HEAD)
    k_nope, v = jnp.split(kv, (QK_NOPE,), axis=-1)
    k = jnp.concatenate([k_nope, jnp.broadcast_to(k_rope[:, :, None, :], (B, T, MLA_HEADS, QK_ROPE))], axis=-1)
    q = rms_norm(q, p["g_qn"])
    k = rms_norm(k, p["g_kn"])
    if angles is not None:
        q = apply_axial_rope(q, angles)
        k = apply_axial_rope(k, angles)
    return q, k, v

def block_attention(q, k, v):
    B, T, H, Dk = q.shape
    scale = Dk ** -0.5
    qb = q.reshape(B, T // Q_BLOCK, Q_BLOCK, H, Dk).transpose(1, 0, 2, 3, 4)

    def one_block(q_blk):
        s = jnp.einsum("bqhd,bkhd->bhqk", q_blk, k).astype(jnp.float32) * scale
        pr = jax.nn.softmax(s, axis=-1)
        return jnp.einsum("bhqk,bkhd->bqhd", pr.astype(v.dtype), v)

    o = lax.map(one_block, qb)
    return o.transpose(1, 0, 2, 3, 4).reshape(B, T, H * v.shape[-1])

def fourier_mix(z):
    B, T, _ = z.shape
    zg = z.astype(jnp.float32).reshape(B, T, FNO_GROUPS, FNO_GROUP_DIM)
    y = jnp.fft.fft2(zg, axes=(1, 3), norm="ortho").real
    return y.reshape(B, T, FNO_WIDTH).astype(z.dtype)

def merge_branches(z_gate, a_o, b_o, c_o, w_out):
    B, T, _ = z_gate.shape
    g = jax.nn.sigmoid(z_gate.reshape(B, T, N_BRANCH, D_MODEL))
    return (g[:, :, 0] * a_o + g[:, :, 1] * b_o + g[:, :, 2] * c_o) @ w_out

def swiglu(h, w_in, w_out):
    gate, up = jnp.split(h @ w_in, 2, axis=-1)
    return (jax.nn.silu(gate) * up) @ w_out

def setup_inputs(seed: int = 0) -> dict:
    key = jax.random.key(seed)
    ks = iter(jax.random.split(key, 64))
    L, D = DEPTH, D_MODEL
    f32 = jnp.float32
    nrm = lambda shape, s: jax.random.normal(next(ks), shape, f32) * s
    uni = lambda shape, lo, hi: jax.random.uniform(next(ks), shape, f32, lo, hi)
    return {
        "x": nrm((BATCH, SEQ, D), 1.0),
        "c": nrm((BATCH, D), 1.0),
        "ctx": nrm((BATCH, CTX_LEN, D), 1.0),
        "c_ctx": nrm((D,), 1.0),
        "w_mod": nrm((L, D, 6 * D), 0.02),
        "b_mod": nrm((L, 6 * D), 0.01),
        "g_norm1": 1.0 + nrm((L, D), 0.02),
        "w_in": nrm((L, D, N_IN), D ** -0.5),
        "mu_prev": uni((L, N_RWKV_IN), 0.0, 0.5),
        "mu_next": uni((L, N_RWKV_IN), 0.0, 0.5),
        "w0": uni((L, N_DIR, RWKV_WIDTH), -5.0, 1.0),
        "w2": nrm((L, N_DIR, DECAY_LORA, RWKV_WIDTH), 0.1 * DECAY_LORA ** -0.5),
        "a0": nrm((L, N_DIR, RWKV_WIDTH), 0.1),
        "a2": nrm((L, N_DIR, AAA_LORA, RWKV_WIDTH), 0.5 * AAA_LORA ** -0.5),
        "k_k": 0.85 + nrm((L, RWKV_WIDTH), 0.02),
        "k_a": 1.0 + nrm((L, RWKV_WIDTH), 0.02),
        "r_k": nrm((L, RWKV_HEADS, RWKV_HEAD_DIM), 0.1),
        "g2": nrm((L, GATE_LORA, RWKV_WIDTH), GATE_LORA ** -0.5),
        "gn_w": 1.0 + nrm((L, RWKV_WIDTH), 0.02),
        "gn_b": nrm((L, RWKV_WIDTH), 0.02),
        "w_rwkv_o": nrm((L, RWKV_WIDTH, D), RWKV_WIDTH ** -0.5),
        "g_cq": 1.0 + nrm((L, Q_LORA), 0.02),
        "g_ckv": 1.0 + nrm((L, KV_LORA), 0.02),
        "w_uq": nrm((L, Q_LORA, MLA_HEADS * QK_HEAD), Q_LORA ** -0.5),
        "w_ukv": nrm((L, KV_LORA, MLA_HEADS * (QK_NOPE + V_HEAD)), KV_LORA ** -0.5),
        "g_qn": 1.0 + nrm((L, QK_HEAD), 0.02),
        "g_kn": 1.0 + nrm((L, QK_HEAD), 0.02),
        "w_mla_o": nrm((L, MLA_WIDTH, D), MLA_WIDTH ** -0.5),
        "w_fno": nrm((L, FNO_WIDTH, D), FNO_WIDTH ** -0.5),
        "w_out": nrm((L, D, D), D ** -0.5),
        "g_norm2": 1.0 + nrm((L, D), 0.02),
        "w_ffn_in": nrm((L, D, 2 * FFN_HIDDEN), D ** -0.5),
        "w_ffn_out": nrm((L, FFN_HIDDEN, D), FFN_HIDDEN ** -0.5),
    }

def reference(x, c, ctx, c_ctx, w_mod, b_mod, g_norm1, w_in, mu_prev, mu_next, w0, w2, a0, a2,
              k_k, k_a, r_k, g2, gn_w, gn_b, w_rwkv_o, g_cq, g_ckv, w_uq, w_ukv, g_qn, g_kn,
              w_mla_o, w_fno, w_out, g_norm2, w_ffn_in, w_ffn_out):
    layer_params = dict(w_mod=w_mod, b_mod=b_mod, g_norm1=g_norm1, w_in=w_in, mu_prev=mu_prev,
                        mu_next=mu_next, w0=w0, w2=w2, a0=a0, a2=a2, k_k=k_k, k_a=k_a, r_k=r_k,
                        g2=g2, gn_w=gn_w, gn_b=gn_b, w_rwkv_o=w_rwkv_o, g_cq=g_cq, g_ckv=g_ckv,
                        w_uq=w_uq, w_ukv=w_ukv, g_qn=g_qn, g_kn=g_kn, w_mla_o=w_mla_o, w_fno=w_fno,
                        w_out=w_out, g_norm2=g_norm2, w_ffn_in=w_ffn_in, w_ffn_out=w_ffn_out)
    B, S, _ = x.shape
    angles = axial_rope_angles(S)
    zero_state = jnp.zeros((B, RWKV_HEADS, RWKV_HEAD_DIM, RWKV_HEAD_DIM), jnp.float32)
    cs = ctx
    for layer in range(DEPTH):
        p = {name: arr[layer] for name, arr in layer_params.items()}
        last = layer == DEPTH - 1
        mod_x = [m[:, None, :] for m in jnp.split(jax.nn.silu(c) @ p["w_mod"] + p["b_mod"], 6, axis=-1)]
        mod_c = jnp.split(jax.nn.silu(c_ctx) @ p["w_mod"] + p["b_mod"], 6, axis=-1)

        hc = modulate(rms_norm(cs, p["g_norm1"]), mod_c[0], mod_c[1])
        hx = modulate(rms_norm(x, p["g_norm1"]), mod_x[0], mod_x[1])
        zr_c, zm_c, zf_c, zg_c = jnp.split(hc @ p["w_in"], IN_SPLITS, axis=-1)
        zr_x, zm_x, zf_x, zg_x = jnp.split(hx @ p["w_in"], IN_SPLITS, axis=-1)

        fc = rwkv_features(zr_c, p)
        fx = rwkv_features(zr_x, p)
        s_fwd_c, y_fwd_c = rwkv_scan(zero_state, fc, 0, reverse=False)
        s_bwd_c, y_bwd_c = rwkv_scan(zero_state, fc, 1, reverse=True)
        _, y_fwd_x = rwkv_scan(s_fwd_c, fx, 0, reverse=False)
        _, y_bwd_x = rwkv_scan(s_bwd_c, fx, 1, reverse=True)
        a_x = rwkv_output(y_fwd_x + y_bwd_x, fx, p)

        q_c, k_c, v_c = mla_qkv(zm_c, p, None)
        q_x, k_x, v_x = mla_qkv(zm_x, p, angles)
        b_x = block_attention(q_x, jnp.concatenate([k_c, k_x], axis=1),
                              jnp.concatenate([v_c, v_x], axis=1)) @ p["w_mla_o"]

        f_x = fourier_mix(zf_x) @ p["w_fno"]

        x_mid = x + mod_x[2] * merge_branches(zg_x, a_x, b_x, f_x, p["w_out"])
        hx2 = modulate(rms_norm(x_mid, p["g_norm2"]), mod_x[3], mod_x[4])
        x_new = x_mid + mod_x[5] * swiglu(hx2, p["w_ffn_in"], p["w_ffn_out"])

        if not last:
            a_c = rwkv_output(y_fwd_c + y_bwd_c, fc, p)
            b_c = block_attention(q_c, k_c, v_c) @ p["w_mla_o"]
            f_c = fourier_mix(zf_c) @ p["w_fno"]
            c_mid = cs + mod_c[2] * merge_branches(zg_c, a_c, b_c, f_c, p["w_out"])
            hc2 = modulate(rms_norm(c_mid, p["g_norm2"]), mod_c[3], mod_c[4])
            cs = c_mid + mod_c[5] * swiglu(hc2, p["w_ffn_in"], p["w_ffn_out"])
        x = x_new
    return x


_drawn_inputs = setup_inputs


def setup_inputs(seed=0):
    import zlib

    import numpy as np

    out = dict(_drawn_inputs(seed))
    spreads = {}
    factors = {'b_mod': 3.442,
     'g_norm1': 7.346,
     'w2': 64.0,
     'a0': 8.0,
     'k_k': 62.512,
     'k_a': 7.254,
     'gn_w': 64.0,
     'gn_b': 64.0,
     'g_cq': 64.0,
     'g_ckv': 64.0,
     'g_qn': 64.0,
     'g_kn': 64.0,
     'g_norm2': 38.656,
     'w0': 3.517}
    for name, (base, spread) in spreads.items():
        noise = np.random.default_rng([zlib.crc32(name.encode()), seed]).standard_normal(out[name].shape)
        drawn = base * np.exp(spread * noise) if base else spread * noise
        out[name] = __import__('jax').numpy.asarray(drawn.astype(out[name].dtype))
    for name, factor in factors.items():
        out[name] = (out[name] * factor).astype(out[name].dtype)
    return out
```

```python
from contextlib import ExitStack

import concourse.bass as bass
import numpy as np
from concourse import mybir

FP32 = mybir.dt.float32
ACT = mybir.ActivationFunctionType
ALU = mybir.AluOpType
AX = mybir.AxisListType

P = 128
D = 1024
DT = D // P
SEQ = 256
CTX = 256
TOK = CTX + SEQ
DEPTH = 2
GRID_W = 64

HEADS = 8
HD = 64
PAIRS = HEADS // 2
WIDTH = HEADS * HD
NDIR = 2
Z_R, Z_K, Z_V, Z_W, Z_A, Z_G = 0, 4, 8, 12, 13, 14
Z_TILES = 15
N_RWKV_IN = Z_TILES * P

QK_NOPE, QK_ROPE = 64, 32
QK = QK_NOPE + QK_ROPE
VH = 64
Q_LORA, KV_LORA = 384, 128
ROPE_AXIS = QK_ROPE // 2
N_MLA_IN = Q_LORA + KV_LORA + QK_ROPE
C_MLA = N_RWKV_IN
C_FNO = C_MLA + N_MLA_IN
C_GATE = C_FNO + WIDTH
N_IN = C_GATE + 3 * D

FFN = ((8 * D + 3 * 256 - 1) // (3 * 256)) * 256
FT = FFN // P

RMS_EPS = 1e-6
GN_EPS = 64e-5
KAPPA = float(np.exp(-0.5))

CHUNK = 64
SEG_CHUNKS = SEQ // CHUNK
LEVELS = 6

SLOTS = 4
SLOT = 2048

VEC_ROWS = [("g_norm1", 8), ("g_norm2", 8), ("mu_prev", 15), ("mu_next", 15), ("w0", 8), ("a0", 8),
            ("k_k", 4), ("k_a", 4), ("r_k", 4), ("gn_w", 4), ("gn_b", 4), ("g_cq", 3), ("g_ckv", 1)]
VEC_AT = {}
_n = 0
for _name, _k in VEC_ROWS:
    VEC_AT[_name] = (_n, _k)
    _n += _k
N_VEC = _n
N_BMOD = 6 * DT


def shape_constants():
    f = np.float32
    out = {}
    out["ident"] = np.eye(P, dtype=f)
    out["head_ones"] = np.kron(np.eye(2), np.ones((HD, HD))).astype(f)
    n = np.arange(HD)
    ang = 2 * np.pi * ((n[:, None] * n[None, :]) % HD) / HD
    out["dft_feature"] = np.concatenate([np.kron(np.eye(2), np.cos(ang)), np.kron(np.eye(2), np.sin(ang))],
                                        axis=1).astype(f)
    t = np.arange(SEQ)
    ang = 2 * np.pi * ((t[:, None] * t[None, :]) % SEQ) / SEQ
    norm = 1.0 / np.sqrt(SEQ * HD)
    out["dft_token"] = np.concatenate([np.cos(ang) * norm, -np.sin(ang) * norm], axis=1).astype(f)
    inv = 10000.0 ** (-np.arange(0, ROPE_AXIS, 2, dtype=np.float64) / ROPE_AXIS)
    cos, sin = np.ones((QK, SEQ)), np.zeros((QK, SEQ))
    rot = np.zeros((QK, QK))
    h = ROPE_AXIS // 2
    for axis, pos in enumerate((t // GRID_W, t % GRID_W)):
        a = pos[None, :] * inv[:, None]
        lo = QK_NOPE + axis * ROPE_AXIS
        for part in (0, h):
            cos[lo + part:lo + part + h] = np.cos(a)
            sin[lo + part:lo + part + h] = np.sin(a)
        for i in range(h):
            rot[lo + h + i, lo + i] = -1.0
            rot[lo + i, lo + h + i] = 1.0
    out["rope"] = np.concatenate([cos, sin, rot], axis=1).astype(f)
    r, c = np.arange(HD)[:, None], np.arange(HD)[None, :]
    stack = lambda m: np.concatenate([m, m], axis=0)
    masks = []
    for d in range(NDIR):
        earlier = (lambda a, b: a < b) if d == 0 else (lambda a, b: a > b)
        level = []
        for l in range(LEVELS):
            b = 1 << l
            same = (r // (2 * b) == c // (2 * b)) & (r // b != c // b)
            level.append(same & earlier(r, c))
        strict_t = earlier(r, c)
        incl_t = strict_t | (r == c)
        parts = [-(level[0].T.astype(f)), -(level[0].astype(f))] + [m.astype(f) for m in level[1:]]
        parts += [strict_t.astype(f), incl_t.astype(f)]
        masks.append(np.concatenate([stack(m) for m in parts], axis=1))
    out["masks"] = np.concatenate(masks, axis=1).astype(f)
    out["eye_heads"] = stack(np.eye(HD)).astype(f)
    return out


class Signal:

    trips = 1
    every = []

    def __init__(self, ctx, nc, name):
        self.sem = ctx.enter_context(nc.semaphore(name))
        self.base = 0
        self.made = 0
        Signal.every.append(self)

    def mark(self, ins):
        self.made += Signal.trips
        return ins.then_inc(self.sem, 1)

    def __call__(self, k):
        return self.sem, self.base + k

    @staticmethod
    def end_stage():
        for s in Signal.every:
            s.base += s.made
            s.made = 0


def build(nc, ins, out):
    Signal.every = []
    Signal.trips = 1
    with ExitStack() as ctx:
        ctx.enter_context(nc.allow_non_contiguous_dma(reason="two norm vectors as columns"))
        build_in(ctx, nc, ins, out)


def build_in(ctx, nc, ins, out):
    def sb(name, shape):
        return ctx.enter_context(nc.sbuf_tensor(name, shape, FP32))

    def sig(name):
        return Signal(ctx, nc, name)

    X = sb("X", [P, DT, TOK])
    H = sb("H", [P, DT, TOK])
    RING = sb("RING", [P, SLOTS, SLOT])
    WORK_N = 27648
    WORK = sb("WORK", [P, WORK_N])
    ident = sb("ident", [P, P])
    ones = sb("ones", [P, P])
    head_ones = sb("head_ones", [P, P])
    eye_heads = sb("eye_heads", [P, HD])
    dft_feature = sb("dft_feature", [P, 2 * P])
    dft_token = sb("dft_token", [P, 2, 2 * SEQ])
    rope = sb("rope", [QK, 2 * SEQ + QK])
    masks = sb("masks", [P, NDIR, LEVELS + 3, HD])
    chunk_start = sb("chunk_start", [P, TOK])
    vec_rows = sb("vec_rows", [P, 2, P])
    vec = sb("vec", [P, N_VEC])
    bmod = sb("bmod", [P, N_BMOD])
    c_rows = sb("c_rows", [2 * DT, P])
    silu_c = sb("silu_c", [P, DT, 2])
    mod = sb("mod", [P, 6, DT, 2])
    scale_1 = sb("scale_1", [P, DT, 2])
    scale_2 = sb("scale_2", [P, DT, 2])
    mu_self = sb("mu_self", [P, Z_TILES])
    ka_rest = sb("ka_rest", [P, PAIRS])
    g_head = sb("g_head", [QK, 2])
    w2_sb = sb("w2_sb", [P, WIDTH])
    a2_sb = sb("a2_sb", [P, WIDTH])
    g2_sb = sb("g2_sb", [P, WIDTH])
    BANK = ctx.enter_context(nc.psum_tensor("BANK", [P, 8, 512], FP32))

    def carve(mem, at, *shape):
        n = 1
        for s in shape:
            n *= s
        flat = mem[:, at:at + n]
        if len(shape) == 1:
            return flat
        names = "abcd"[:len(shape)]
        return flat.rearrange(f"p ({' '.join(names)}) -> p {' '.join(names)}",
                              **{k: s for k, s in zip(names[1:], shape[1:])})

    def v(name, i):
        at = VEC_AT[name][0] + i
        return vec[:, at:at + 1]

    slot_full = [ctx.enter_context(nc.semaphore(f"slot_full_{s}")) for s in range(SLOTS)]
    slot_used = sig("slot_used")
    ring = {"next": 0}

    class Loads:

        def __init__(self, sources):
            self.sources = sources
            self.first = ring["next"]
            ring["next"] += len(sources)

        def issue(self, sp, used=None):
            for i, src in enumerate(self.sources):
                n = self.first + i
                if i >= SLOTS:
                    sp.wait_ge(*used(i - SLOTS))
                sp.dma_start(self.view(i), src).then_inc(slot_full[n % SLOTS], 16)

        def view(self, i):
            src = self.sources[i]
            k, w = src.shape[1], src.shape[2]
            s = (self.first + i) % SLOTS
            return RING[:, s, 0:k * w].rearrange("p (k w) -> p k w", k=k)

        def arrived(self, pe, i):
            n = self.first + i
            pe.wait_ge(slot_full[n % SLOTS], 16 * (n // SLOTS + 1))
            return self.view(i)

    def k_tiles(dram, c0, c1):
        return dram[:, c0:c1].rearrange("(k p) n -> p k n", p=P)

    consts_in = ctx.enter_context(nc.semaphore("consts_in"))
    rows_in = ctx.enter_context(nc.semaphore("rows_in"))
    small_in = ctx.enter_context(nc.semaphore("small_in"))
    out_stored = ctx.enter_context(nc.semaphore("out_stored"))
    pe_sig, act_sig, dve_sig, pool_sig = sig("pe_step"), sig("act_step"), sig("dve_step"), sig("pool_step")
    rows_turned = sig("rows_turned")
    turned_out = sig("turned_out")
    squares = sig("squares")
    sums = sig("sums")
    inverse_rms = sig("inverse_rms")
    scaled = sig("scaled")
    h_ready = sig("h_ready")
    product = sig("product")
    evacuated = sig("evacuated")
    first_cut = sig("first_cut")
    gate_ready = sig("gate_ready")
    merged = sig("merged")

    def stage():
        return nc.Block()

    waits_passed = {e: ctx.enter_context(nc.semaphore(f"waits_passed_{e}")) for e in ("pe", "dve", "pool")}

    def hold(eng, name="pe"):
        eng.sem_inc(waits_passed[name], 1)

    rows_loaded = {"n": 0}

    tokens_in = carve(WORK, 0, 4, D)
    with stage() as block:
        @block.sync
        def _(sp):
            sp.dma_start(tokens_in[:, 0:2], ins["ctx"][0].rearrange("(t p) d -> p t d", p=P)).then_inc(consts_in, 16)
            sp.dma_start(tokens_in[:, 2:4], ins["x"][0].rearrange("(t p) d -> p t d", p=P)).then_inc(consts_in, 16)
            sp.dma_start(ident[:], ins["ident"]).then_inc(consts_in, 16)
            sp.dma_start(head_ones[:], ins["head_ones"]).then_inc(consts_in, 16)
            sp.dma_start(eye_heads[:], ins["eye_heads"]).then_inc(consts_in, 16)
            sp.dma_start(dft_feature[:], ins["dft_feature"]).then_inc(consts_in, 16)
            sp.dma_start(dft_token[:], ins["dft_token"].rearrange("(t p) n -> p t n", p=P)).then_inc(consts_in, 16)
            sp.dma_start(rope[:], ins["rope"]).then_inc(consts_in, 16)
            sp.dma_start(masks[:].rearrange("p d m n -> p (d m n)"), ins["masks"]).then_inc(consts_in, 16)
            sp.dma_start(c_rows[0:DT, :], ins["c_ctx"].rearrange("(k p) -> k p", p=P)).then_inc(consts_in, 16)
            sp.dma_start(c_rows[DT:2 * DT, :], ins["c"][0].rearrange("(k p) -> k p", p=P)).then_inc(consts_in, 16)

        @block.gpsimd
        def _(pool):
            nc.gpsimd.memset(ones[:], 1.0)
            nc.gpsimd.memset(chunk_start[:], 1.0).then_inc(pool_sig.sem, 1)
            pool_sig.made += 1
            pool.wait_ge(*pool_sig(1))
            nc.gpsimd.memset(chunk_start[:].rearrange("p (c t) -> p c t", t=CHUNK)[:, :, 0:1], 0.0)

        @block.tensor
        def _(pe):
            pe.wait_ge(consts_in, 16 * 11)
            for k in range(DT):
                for t in range(4):
                    last = nc.tensor.transpose(BANK[:, k, t * P:(t + 1) * P], tokens_in[:, t, k * P:(k + 1) * P], ident[:])
                rows_turned.mark(last)
            pe.wait_ge(*turned_out(1))
            rows_turned.mark(nc.tensor.transpose(BANK[:, 0, 0:2 * DT], c_rows[:], ident[0:2 * DT, 0:2 * DT]))

        @block.vector
        def _(dve):
            for k in range(DT):
                dve.wait_ge(*rows_turned(k + 1))
                turned_out.mark(nc.vector.tensor_copy(X[:, k], BANK[:, k]))

        @block.scalar
        def _(act):
            act.wait_ge(*rows_turned(DT + 1))
            nc.scalar.activation(silu_c[:].rearrange("p k s -> p s k"),
                                 BANK[:, 0, 0:2 * DT].rearrange("p (s k) -> p s k", s=2), ACT.Silu)
    Signal.end_stage()

    def modulation(l):
        loads = Loads([k_tiles(ins["w_mod"][l], c, c + 2 * P) for c in range(0, 6 * D, 2 * P)])
        n0 = rows_loaded["n"]
        rows_loaded["n"] += len(VEC_ROWS) + 1
        with stage() as block:
            @block.sync
            def _(sp):
                loads.issue(sp, lambda i: slot_used(i + 1))

            @block.gpsimd
            def _(pool):
                pool.dma_start(vec_rows[0:N_BMOD, 0, :], ins["b_mod"][l].rearrange("(k p) -> k p", p=P)).then_inc(rows_in, 16)
                for name, k in VEC_ROWS:
                    at = VEC_AT[name][0]
                    src = ins[name][l]
                    if len(src.shape) == 2:
                        src = src.rearrange("a b -> (a b)")
                    pool.dma_start(vec_rows[at:at + k, 1, :], src.rearrange("(k p) -> k p", p=P)).then_inc(rows_in, 16)
                pool.dma_start(w2_sb[:], ins["w2"][l].rearrange("d r c -> (d r) c")).then_inc(small_in, 16)
                pool.dma_start(a2_sb[:], ins["a2"][l].rearrange("d r c -> (d r) c")).then_inc(small_in, 16)
                pool.dma_start(g2_sb[:], ins["g2"][l]).then_inc(small_in, 16)
                pool.dma_start(g_head[:, 0:1], ins["g_qn"][l].rearrange("(a b) -> a b", b=1)).then_inc(small_in, 16)
                pool.dma_start(g_head[:, 1:2], ins["g_kn"][l].rearrange("(a b) -> a b", b=1)).then_inc(small_in, 16)
                pool.wait_ge(small_in, 16 * 5 * (l + 1))

            @block.tensor
            def _(pe):
                pe.wait_ge(rows_in, 16 * (n0 + len(VEC_ROWS) + 1))
                rows_turned.mark(nc.tensor.transpose(BANK[:, 0, 0:N_BMOD], vec_rows[0:N_BMOD, 0, :], ident[0:N_BMOD, 0:N_BMOD]))
                rows_turned.mark(nc.tensor.transpose(BANK[:, 1, 0:N_VEC], vec_rows[0:N_VEC, 1, :], ident[0:N_VEC, 0:N_VEC]))
                for i in range(3 * DT):
                    w = loads.arrived(pe, i)
                    for m in (2 * i, 2 * i + 1):
                        for k in range(DT):
                            last = nc.tensor.matmul(BANK[:, 2, 2 * m:2 * m + 2], w[:, k, (m % 2) * P:(m % 2 + 1) * P],
                                                    silu_c[:, k], start=(k == 0), stop=(k == DT - 1))
                    slot_used.mark(last)

            @block.vector
            def _(dve):
                dve.wait_ge(*rows_turned(1))
                dve_sig.mark(nc.vector.tensor_copy(bmod[:], BANK[:, 0, 0:N_BMOD]))
                dve.wait_ge(*rows_turned(2))
                dve_sig.mark(nc.vector.tensor_copy(vec[:], BANK[:, 1, 0:N_VEC]))
                dve.wait_ge(*dve_sig(2))
                mp, mn = VEC_AT["mu_prev"][0], VEC_AT["mu_next"][0]
                dve_sig.mark(nc.vector.tensor_tensor(mu_self[:], vec[:, mp:mp + Z_TILES], vec[:, mn:mn + Z_TILES], ALU.add))
                ka = VEC_AT["k_a"][0]
                dve_sig.mark(nc.vector.tensor_scalar(ka_rest[:], vec[:, ka:ka + PAIRS], -1.0, 1.0, ALU.mult, ALU.add))
                dve.wait_ge(*dve_sig(4))
                nc.vector.tensor_scalar(mu_self[:], mu_self[:], -1.0, 1.0, ALU.mult, ALU.add)
                dve.wait_ge(*slot_used(3 * DT))
                flat = mod[:].rearrange("p q k s -> p (q k) s")
                dve_sig.mark(nc.vector.tensor_tensor(flat, BANK[:, 2, 0:2 * N_BMOD].rearrange("p (m s) -> p m s", s=2),
                                                     bmod[:].unsqueeze(2).to_broadcast([P, N_BMOD, 2]), ALU.add))
                dve.wait_ge(*dve_sig(5))
                for which, dst, g in ((1, scale_1, "g_norm1"), (4, scale_2, "g_norm2")):
                    at = VEC_AT[g][0]
                    dve_sig.mark(nc.vector.tensor_scalar(dst[:], mod[:, which], 1.0, None, ALU.add))
                    dve.wait_ge(*dve_sig(6 if which == 1 else 7))
                    nc.vector.tensor_tensor(dst[:], dst[:], vec[:, at:at + DT].unsqueeze(2).to_broadcast([P, DT, 2]), ALU.mult)
        Signal.end_stage()

    def norm(scale, shift, t0, work_at=0):
        n = TOK - t0
        sq = carve(WORK, work_at, DT, TOK)
        rms = carve(WORK, work_at + DT * TOK, TOK)
        segs = [s for s in range(2) if s * CTX >= t0]
        with stage() as block:
            @block.scalar
            def _(act):
                for k in range(DT):
                    squares.mark(nc.scalar.activation(sq[:, k, t0:], X[:, k, t0:], ACT.Square))
                act.wait_ge(*dve_sig(2))
                inverse_rms.mark(nc.scalar.activation(rms[:, t0:], rms[:, t0:], ACT.Sqrt))
                i = 0
                for k in range(DT):
                    for s in segs:
                        i += 1
                        act.wait_ge(*scaled(i))
                        nc.scalar.activation(H[:, k, s * CTX:(s + 1) * CTX], H[:, k, s * CTX:(s + 1) * CTX],
                                             ACT.Identity, bias=shift[:, k, s:s + 1])

            @block.tensor
            def _(pe):
                for k in range(DT):
                    pe.wait_ge(*squares(k + 1))
                    last = nc.tensor.matmul(BANK[:, 0, 0:n], ones[:], sq[:, k, t0:], start=(k == 0), stop=(k == DT - 1))
                sums.mark(last)

            @block.vector
            def _(dve):
                dve.wait_ge(*sums(1))
                dve_sig.mark(nc.vector.tensor_scalar(rms[:, t0:], BANK[:, 0, 0:n], 1.0 / D, RMS_EPS, ALU.mult, ALU.add))
                dve.wait_ge(*dve_sig(1))
                dve_sig.mark(nc.vector.reciprocal(rms[:, t0:], rms[:, t0:]))
                dve.wait_ge(*inverse_rms(1))
                for k in range(DT):
                    for s in segs:
                        a, b = s * CTX, (s + 1) * CTX
                        scaled.mark(nc.vector.scalar_tensor_tensor(H[:, k, a:b], X[:, k, a:b], scale[:, k, s:s + 1],
                                                                   rms[:, a:b], ALU.mult, ALU.mult))
        Signal.end_stage()

    Z = carve(WORK, 0, Z_TILES, TOK)

    def project_rwkv(l):
        loads = Loads([k_tiles(ins["w_in"][l], c, min(c + 2 * P, N_RWKV_IN)) for c in range(0, N_RWKV_IN, 2 * P)])
        with stage() as block:
            @block.sync
            def _(sp):
                loads.issue(sp, lambda i: product(2 * i + 2))

            @block.tensor
            def _(pe):
                for m in range(Z_TILES):
                    if m % 2 == 0:
                        w = loads.arrived(pe, m // 2)
                    if m >= 4:
                        pe.wait_ge(*evacuated(m - 3))
                    for k in range(DT):
                        last = nc.tensor.matmul(BANK[:, m % 4], w[:, k, (m % 2) * P:(m % 2 + 1) * P], H[:, k],
                                                start=(k == 0), stop=(k == DT - 1))
                    product.mark(last)

            @block.scalar
            def _(act):
                for m in range(Z_TILES):
                    act.wait_ge(*product(m + 1))
                    first_cut.mark(nc.scalar.activation(Z[:, m], BANK[:, m % 4], ACT.Copy, scale=mu_self[:, m:m + 1]))

            @block.vector
            def _(dve):
                for m in range(Z_TILES):
                    z = Z[:, m].rearrange("p (s t) -> p s t", s=2)
                    raw = BANK[:, m % 4].rearrange("p (s t) -> p s t", s=2)
                    dve.wait_ge(*first_cut(m + 1))
                    dve_sig.mark(nc.vector.scalar_tensor_tensor(z[:, :, 1:], raw[:, :, :SEQ - 1], v("mu_prev", m), z[:, :, 1:],
                                                                ALU.mult, ALU.add))
                    dve.wait_ge(*dve_sig(m + 1))
                    evacuated.mark(nc.vector.scalar_tensor_tensor(z[:, :, :SEQ - 1], raw[:, :, 1:], v("mu_next", m),
                                                                  z[:, :, :SEQ - 1], ALU.mult, ALU.add))
        Signal.end_stage()

    F0 = Z_TILES * TOK
    KK = carve(WORK, F0, PAIRS, TOK)
    KD = [carve(WORK, F0 + (1 + d) * WIDTH * 4, PAIRS, TOK) for d in range(NDIR)]
    BB = [carve(WORK, F0 + (3 + d) * WIDTH * 4, PAIRS, TOK) for d in range(NDIR)]
    INCL = [carve(WORK, F0 + (5 + d) * WIDTH * 4, PAIRS, TOK) for d in range(NDIR)]
    EXCL = [carve(WORK, F0 + (7 + d) * WIDTH * 4, PAIRS, TOK) for d in range(NDIR)]
    WORK_USED = F0 + 9 * WIDTH * 4
    Y = carve(WORK, Z_K * TOK, PAIRS, TOK)

    def features():
        sqk = carve(RING.rearrange("p s n -> p (s n)"), 0, PAIRS, TOK)
        inv = carve(RING.rearrange("p s n -> p (s n)"), PAIRS * TOK, PAIRS, TOK)
        with stage() as block:
            @block.scalar
            def _(act):
                act_sig.mark(nc.scalar.activation(Z[:, Z_W], Z[:, Z_W], ACT.Tanh))
                act_sig.mark(nc.scalar.activation(Z[:, Z_G], Z[:, Z_G], ACT.Sigmoid))
                n = 0
                for d in range(NDIR):
                    for j in range(PAIRS):
                        n += 1
                        act.wait_ge(*product(n))
                        gate_ready.mark(nc.scalar.activation(EXCL[d][:, j], BANK[:, n % 4], ACT.Sigmoid, bias=v("w0", d * PAIRS + j)))
                for d in range(NDIR):
                    for j in range(PAIRS):
                        n += 1
                        act.wait_ge(*product(n))
                        gate_ready.mark(nc.scalar.activation(BB[d][:, j], BANK[:, n % 4], ACT.Sigmoid, bias=v("a0", d * PAIRS + j)))
                for j in range(PAIRS):
                    act.wait_ge(*scaled(j + 1))
                    squares.mark(nc.scalar.activation(sqk[:, j], KK[:, j], ACT.Square))
                for j in range(PAIRS):
                    act.wait_ge(*sums(j + 1))
                    evacuated.mark(nc.scalar.activation(inv[:, j], BANK[:, 4 + j], ACT.Sqrt))

            @block.tensor
            def _(pe):
                n = 0
                for w, z in ((w2_sb, Z_W), (a2_sb, Z_A)):
                    for d in range(NDIR):
                        for j in range(PAIRS):
                            n += 1
                            if n == 1:
                                pe.wait_ge(*act_sig(1))
                            if n > 4:
                                pe.wait_ge(*gate_ready(n - 4))
                            product.mark(nc.tensor.matmul(BANK[:, n % 4], w[d * 64:(d + 1) * 64, j * P:(j + 1) * P],
                                                          Z[d * 64:(d + 1) * 64, z], start=True, stop=True))
                for j in range(PAIRS):
                    pe.wait_ge(*squares(j + 1))
                    sums.mark(nc.tensor.matmul(BANK[:, 4 + j], head_ones[:], sqk[:, j], start=True, stop=True))

            @block.vector
            def _(dve):
                c = 0
                for j in range(PAIRS):
                    scaled.mark(nc.vector.tensor_scalar(KK[:, j], Z[:, Z_K + j], v("k_k", j), None, ALU.mult))
                for d in range(NDIR):
                    for j in range(PAIRS):
                        dve.wait_ge(*gate_ready(d * PAIRS + j + 1))
                        c += 1
                        dve_sig.mark(nc.vector.tensor_tensor_scan(INCL[d][:, j], chunk_start[:], EXCL[d][:, j], 0.0, ALU.mult, ALU.add))
                    dve.wait_ge(*dve_sig(c))
                    nc.vector.tensor_tensor(EXCL[d], INCL[d], EXCL[d], ALU.subtract)
                for d in range(NDIR):
                    for j in range(PAIRS):
                        dve.wait_ge(*gate_ready((NDIR + d) * PAIRS + j + 1))
                        c += 1
                        dve_sig.mark(nc.vector.tensor_scalar(KD[d][:, j], BB[d][:, j], v("k_a", j), ka_rest[:, j:j + 1], ALU.mult, ALU.add))
                    dve.wait_ge(*dve_sig(c))
                    nc.vector.tensor_tensor(KD[d], KD[d], Z[:, Z_K:Z_K + PAIRS], ALU.mult)
                for j in range(PAIRS):
                    dve.wait_ge(*evacuated(j + 1))
                    c += 1
                    dve_sig.mark(nc.vector.tensor_scalar(inv[:, j], inv[:, j], 1e-12, None, ALU.max))
                dve.wait_ge(*dve_sig(c))
                c += 1
                dve_sig.mark(nc.vector.reciprocal(inv, inv))
                dve.wait_ge(*dve_sig(c))
                c += 1
                dve_sig.mark(nc.vector.tensor_tensor(KK, KK, inv, ALU.mult))
                dve.wait_ge(*dve_sig(c))
                for d in range(NDIR):
                    nc.vector.tensor_tensor(BB[d], BB[d], KK, ALU.mult)
                nc.vector.memset(Y, 0.0)
        Signal.end_stage()

    h_flat = H[:].rearrange("p k t -> p (k t)")
    r_flat = RING[:].rearrange("p s n -> p (s n)")
    HALF = PAIRS * HD
    free = [(r_flat, 0, SLOTS * SLOT), (h_flat, 0, DT * TOK), (WORK[:], Z_W * TOK, Z_G * TOK),
            (WORK[:], WORK_USED, WORK_N)]

    def scratch(*shape):
        n = 1
        for s in shape:
            n *= s
        for i, (mem, at, end) in enumerate(free):
            if at + n <= end:
                free[i] = (mem, at + n, end)
                return carve(mem, at, *shape)
        raise ValueError(f"no room for {shape}: {[(a, e) for _, a, e in free]}")

    QR = [scratch(PAIRS, 2, HD) for _ in range(NDIR)]
    QR2 = [scratch(PAIRS, 2, HD) for _ in range(NDIR)]
    GA = [scratch(PAIRS, 2, HD) for _ in range(NDIR)]
    T2 = [scratch(2, PAIRS, HD) for _ in range(NDIR)]
    BT = [scratch(PAIRS, HD) for _ in range(NDIR)]
    KT = [scratch(PAIRS, HD) for _ in range(NDIR)]
    BH = [scratch(PAIRS, HD) for _ in range(NDIR)]
    KH = [scratch(PAIRS, HD) for _ in range(NDIR)]
    VF = [scratch(PAIRS, HD) for _ in range(NDIR)]
    VB_TOK = [scratch(2, PAIRS, HD) for _ in range(NDIR)]
    KH_TOK = [scratch(PAIRS, HD) for _ in range(NDIR)]
    EXPO = [scratch(3, PAIRS, HD) for _ in range(1)]
    EXPS = [scratch(4, PAIRS, HD) for _ in range(1)]
    LTS = [scratch(PAIRS, HD) for _ in range(NDIR)]
    LM = [scratch(PAIRS, HD) for _ in range(NDIR)]
    ARB = [scratch(PAIRS, HD) for _ in range(NDIR)]
    X1 = [scratch(PAIRS, HD) for _ in range(NDIR)]
    WS = [scratch(PAIRS, HD) for _ in range(NDIR)]
    SA = [scratch(PAIRS, HD) for _ in range(NDIR)]
    ST = [scratch(PAIRS, HD) for _ in range(NDIR)]
    SD = [scratch(PAIRS, HD) for _ in range(NDIR)]
    DEC = [sb(f"decay_{d}", [P, PAIRS]) for d in range(NDIR)]

    s_expo = sig("exponents_ready")
    s_exp = sig("exps_ready")
    s_exp_used = [sig(f"exps_used_{i}") for i in range(2)]
    s_qr = [sig(f"qr_ready_{d}") for d in range(NDIR)]
    s_ops = [sig(f"operands_ready_{d}") for d in range(NDIR)]
    s_qr2 = [sig(f"qr_kept_{d}") for d in range(NDIR)]
    s_gram = [sig(f"gram_{d}") for d in range(NDIR)]
    s_lts = [sig(f"lt_kept_{d}") for d in range(NDIR)]
    s_gram_out = [sig(f"gram_out_{d}") for d in range(NDIR)]
    s_tok_out = [sig(f"token_major_out_{d}") for d in range(NDIR)]
    s_lm = [sig(f"level_mask_{d}") for d in range(NDIR)]
    s_x1 = [sig(f"x1_product_{d}") for d in range(NDIR)]
    s_x1_out = [sig(f"x1_out_{d}") for d in range(NDIR)]
    s_tx = [sig(f"merge_product_{d}") for d in range(NDIR)]
    s_t = [sig(f"inverse_merged_{d}") for d in range(NDIR)]
    s_w = [sig(f"w_product_{d}") for d in range(NDIR)]
    s_w_out = [sig(f"w_out_{d}") for d in range(NDIR)]
    s_sa = [sig(f"sa_product_{d}") for d in range(NDIR)]
    s_sa_out = [sig(f"sa_out_{d}") for d in range(NDIR)]
    s_y = [sig(f"y_product_{d}") for d in range(NDIR)]
    s_ds = [sig(f"state_product_{d}") for d in range(NDIR)]
    s_y_out = [sig(f"y_added_{d}") for d in range(NDIR)]
    s_sd = [sig(f"state_decayed_{d}") for d in range(NDIR)]
    s_st = [sig(f"state_new_{d}") for d in range(NDIR)]
    s_init = sig("state_cleared")
    s_first = [sig(f"first_level_{d}") for d in range(NDIR)]

    scan_signals = [s_expo, s_exp, s_init, *s_qr, *s_ops, *s_qr2, *s_gram, *s_lts, *s_gram_out, *s_tok_out, *s_lm, *s_x1, *s_x1_out,
                    *s_tx, *s_t, *s_w, *s_w_out, *s_sa, *s_sa_out, *s_y, *s_ds, *s_y_out, *s_sd, *s_st, *s_first]
    with stage() as block:
        @block.sync
        def _(sp):
            for s in scan_signals:
                sp.sem_inc(s.sem, 1)
                s.made += 1
    Signal.end_stage()

    NL = LEVELS - 1
    N = SEG_CHUNKS

    def lanes(mask):
        return mask.unsqueeze(1).to_broadcast([P, PAIRS, HD])

    def scan(seg, need_y, clear):
        t_base = seg * SEQ

        def chunk_of(d, i):
            return t_base + i * CHUNK if d == 0 else t_base + (N - 1) * CHUNK - i * CHUNK

        def level_mask(d, l):
            return masks[:, d, 1 + l]

        B_L, B_LT, B_G, B_V = 0, 1, 2, 3
        Signal.trips = N
        with stage() as block:
            @block.gpsimd
            def _(pool):
                with pool.Fori(0, N) as i:
                    for d in range(NDIR):
                        t = pool.snap(chunk_of(d, i), min_val=t_base, max_val=t_base + (N - 1) * CHUNK)
                        at = bass.ds(t, CHUNK)
                        e = EXPS[0]
                        pool.wait_ge(s_gram[d].sem, s_gram[d].base + 4 * i)
                        hold(pool, "pool")
                        nc.gpsimd.tensor_copy(VF[d], Z[:, Z_V:Z_V + PAIRS, at])
                        pool.wait_ge(s_exp.sem, s_exp.base + 2 * i + d + 1)
                        hold(pool, "pool")
                        nc.gpsimd.tensor_tensor(BH[d], BB[d][:, :, at], e[:, 3], ALU.mult)
                        nc.gpsimd.tensor_tensor(KH[d], KD[d][:, :, at], e[:, 3], ALU.mult)
                        s_ops[d].mark(nc.gpsimd.tensor_tensor(KT[d], KD[d][:, :, at], e[:, 2], ALU.mult))
                    for l in range(1, LEVELS):
                        for d in range(NDIR):
                            pool.wait_ge(s_lts[d].sem, s_lts[d].base + i + 1)
                            if l > 1:
                                pool.wait_ge(s_x1[d].sem, s_x1[d].base + NL * i + l - 1)
                            else:
                                pool.wait_ge(s_x1[d].sem, s_x1[d].base + NL * i)
                            s_lm[d].mark(nc.gpsimd.tensor_tensor(LM[d], LTS[d], lanes(level_mask(d, l)), ALU.mult))
                    for d in range(NDIR):
                        pool.wait_ge(s_st[d].sem, s_st[d].base + i)
                        if seg == 0 or clear:
                            pool.wait_ge(*s_init(1))
                        s_sd[d].mark(nc.gpsimd.tensor_tensor(SD[d], ST[d], DEC[d][:].unsqueeze(2).to_broadcast([P, PAIRS, HD]), ALU.mult))

            @block.scalar
            def _(act):
                with act.Fori(0, N) as i:
                    for d in range(NDIR):
                        act.wait_ge(s_expo.sem, s_expo.base + 2 * i + d + 1)
                        if d == 0:
                            act.wait_ge(s_ops[1].sem, s_ops[1].base + i)
                            act.wait_ge(s_qr2[1].sem, s_qr2[1].base + i)
                        else:
                            act.wait_ge(s_ops[0].sem, s_ops[0].base + i + 1)
                            act.wait_ge(s_qr2[0].sem, s_qr2[0].base + i + 1)
                        t = act.snap(chunk_of(d, i), min_val=t_base, max_val=t_base + (N - 1) * CHUNK)
                        at = bass.ds(t, CHUNK)
                        x, e = EXPO[0], EXPS[0]
                        excl = EXCL[0][:, :, at] if d == 0 else x[:, 1]
                        incl = INCL[0][:, :, at] if d == 0 else x[:, 0]
                        rest = x[:, 2] if d == 0 else EXCL[1][:, :, at]
                        nc.scalar.activation(e[:, 0], excl, ACT.Exp, scale=-KAPPA)
                        nc.scalar.activation(e[:, 1], incl, ACT.Exp, scale=-KAPPA)
                        nc.scalar.activation(e[:, 2], incl, ACT.Exp, scale=KAPPA)
                        nc.scalar.activation(e[:, 3], rest, ACT.Exp, scale=-KAPPA)
                        act.wait_ge(s_sd[d].sem, s_sd[d].base + i)
                        s_exp.mark(nc.scalar.activation(DEC[d][:].unsqueeze(2), INCL[d][:, :, bass.ds(t + (CHUNK - 1), 1)],
                                                        ACT.Exp, scale=-KAPPA))
                    for d in range(NDIR):
                        act.wait_ge(s_gram[d].sem, s_gram[d].base + 4 * i + 1)
                        act.wait_ge(s_lm[d].sem, s_lm[d].base + NL * i)
                        s_lts[d].mark(nc.scalar.activation(LTS[d], BANK[:, 4 * d + B_LT].rearrange("p (j q t) -> p j q t", j=PAIRS, q=2)[:, :, 0], ACT.Copy))
                    for d in range(NDIR):
                        act.wait_ge(s_gram[d].sem, s_gram[d].base + 4 * i + 2)
                        act.wait_ge(s_ds[d].sem, s_ds[d].base + i)
                        s_tok_out[d].mark(nc.scalar.activation(KH_TOK[d], BANK[:, 4 * d + B_L, HALF:].rearrange("p (j t) -> p j t", j=PAIRS), ACT.Copy))
                        act.wait_ge(s_gram[d].sem, s_gram[d].base + 4 * i + 3)
                        s_tok_out[d].mark(nc.scalar.activation(VB_TOK[d].rearrange("p q j t -> p (q j t)"), BANK[:, 4 * d + B_V], ACT.Copy))
                    for l in range(1, LEVELS):
                        for d in range(NDIR):
                            act.wait_ge(s_x1[d].sem, s_x1[d].base + NL * i + l)
                            s_x1_out[d].mark(nc.scalar.activation(X1[d], BANK[:, 4 * d + B_L, 0:HALF].rearrange("p (j t) -> p j t", j=PAIRS), ACT.Copy))
                    for d in range(NDIR):
                        act.wait_ge(s_w[d].sem, s_w[d].base + i + 1)
                        s_w_out[d].mark(nc.scalar.activation(WS[d], BANK[:, 4 * d + B_L, 0:HALF].rearrange("p (j t) -> p j t", j=PAIRS), ACT.Copy))
                    for d in range(NDIR):
                        act.wait_ge(s_sa[d].sem, s_sa[d].base + i + 1)
                        s_sa_out[d].mark(nc.scalar.activation(SA[d], BANK[:, 4 * d + B_LT, 0:HALF].rearrange("p (j t) -> p j t", j=PAIRS), ACT.Copy, scale=-1.0))

            @block.vector
            def _(dve):
                if clear:
                    nc.vector.memset(ST[0], 0.0)
                    s_init.mark(nc.vector.memset(ST[1], 0.0))
                    s_init.made = 1
                with dve.Fori(0, N) as i:
                    for d in range(NDIR):
                        t = dve.snap(chunk_of(d, i), min_val=t_base, max_val=t_base + (N - 1) * CHUNK)
                        at = bass.ds(t, CHUNK)
                        whole = INCL[d][:, :, bass.ds(t + (CHUNK - 1), 1)].to_broadcast([P, PAIRS, CHUNK])
                        x, e = EXPO[0], EXPS[0]
                        dve.wait_ge(s_exp.sem, s_exp.base + 2 * i + d)
                        hold(dve, "dve")
                        if d == 0:
                            s_expo.mark(nc.vector.tensor_tensor(x[:, 2], whole, INCL[0][:, :, at], ALU.subtract))
                        else:
                            nc.vector.tensor_tensor(x[:, 0], whole, EXCL[1][:, :, at], ALU.subtract)
                            s_expo.mark(nc.vector.tensor_tensor(x[:, 1], whole, INCL[1][:, :, at], ALU.subtract))
                        dve.wait_ge(s_exp.sem, s_exp.base + 2 * i + d + 1)
                        dve.wait_ge(s_gram[d].sem, s_gram[d].base + 4 * i)
                        nc.vector.tensor_tensor(BT[d], BB[d][:, :, at], e[:, 2], ALU.mult)
                        nc.vector.tensor_tensor(QR[d][:, :, 0], KK[:, :, at], e[:, 0], ALU.mult)
                        s_qr[d].mark(nc.vector.tensor_tensor(QR[d][:, :, 1], Z[:, Z_R:Z_R + PAIRS, at], e[:, 1], ALU.mult))
                        dve.wait_ge(s_ds[d].sem, s_ds[d].base + i)
                        dve.wait_ge(s_qr[d].sem, s_qr[d].base + i + 1)
                        s_qr2[d].mark(nc.vector.tensor_copy(QR2[d], QR[d]))
                    for d in range(NDIR):
                        lt = BANK[:, 4 * d + B_LT].rearrange("p (j q t) -> p j q t", j=PAIRS, q=2)
                        dve.wait_ge(s_lts[d].sem, s_lts[d].base + i + 1)
                        nc.vector.tensor_tensor(ARB[d], lt[:, :, 1], lanes(masks[:, d, LEVELS + 2]), ALU.mult)
                        dve.wait_ge(s_tok_out[d].sem, s_tok_out[d].base + 2 * i + 1)
                        nc.vector.tensor_tensor(T2[d][:, 0], BANK[:, 4 * d + B_L, 0:HALF].rearrange("p (j t) -> p j t", j=PAIRS),
                                                lanes(masks[:, d, 0]), ALU.mult)
                        s_first[d].mark(nc.vector.tensor_tensor(T2[d][:, 1], LTS[d], lanes(masks[:, d, 1]), ALU.mult))
                        dve.wait_ge(s_first[d].sem, s_first[d].base + i + 1)
                        s_t[d].mark(nc.vector.tensor_tensor(T2[d].rearrange("p q j t -> p (q j) t"), T2[d].rearrange("p q j t -> p (q j) t"),
                                                            eye_heads[:].unsqueeze(1).to_broadcast([P, 2 * PAIRS, HD]), ALU.add))
                        dve.wait_ge(s_gram[d].sem, s_gram[d].base + 4 * i + 4)
                        s_gram_out[d].mark(nc.vector.tensor_tensor(
                            GA[d].rearrange("p j q t -> p j (q t)"),
                            BANK[:, 4 * d + B_G].rearrange("p (j n) -> p j n", j=PAIRS),
                            masks[:, d, LEVELS + 1:LEVELS + 3].rearrange("p q t -> p (q t)").unsqueeze(1).to_broadcast([P, PAIRS, 2 * HD]),
                            ALU.mult))
                    for l in range(1, LEVELS):
                        for d in range(NDIR):
                            dve.wait_ge(s_tx[d].sem, s_tx[d].base + NL * i + l)
                            dve.wait_ge(s_t[d].sem, s_t[d].base + LEVELS * i + l)
                            tx = BANK[:, 4 * d + B_LT].rearrange("p (q j t) -> p q j t", q=2, j=PAIRS)
                            if l < LEVELS - 1:
                                s_t[d].mark(nc.vector.tensor_tensor(T2[d].rearrange("p q j t -> p (q j t)"), T2[d].rearrange("p q j t -> p (q j t)"),
                                                                    BANK[:, 4 * d + B_LT], ALU.subtract))
                            else:
                                s_t[d].mark(nc.vector.tensor_tensor(T2[d][:, 1], T2[d][:, 1], tx[:, 1], ALU.subtract))
                    if need_y:
                        for d in range(NDIR):
                            t = dve.snap(chunk_of(d, i), min_val=t_base, max_val=t_base + (N - 1) * CHUNK)
                            at = bass.ds(t, CHUNK)
                            dve.wait_ge(s_y[d].sem, s_y[d].base + i + 1)
                            o = s_y_out[1 - d]
                            dve.wait_ge(o.sem, o.base + i + d)
                            s_y_out[d].mark(nc.vector.tensor_tensor(Y[:, :, at], Y[:, :, at],
                                                                    BANK[:, 4 * d + B_G, 0:HALF].rearrange("p (j t) -> p j t", j=PAIRS), ALU.add))
                    for d in range(NDIR):
                        dve.wait_ge(s_sd[d].sem, s_sd[d].base + i + 1)
                        dve.wait_ge(s_ds[d].sem, s_ds[d].base + i + 1)
                        s_st[d].mark(nc.vector.tensor_tensor(ST[d], SD[d], BANK[:, 4 * d + B_V, 0:HALF].rearrange("p (j t) -> p j t", j=PAIRS), ALU.add))

            @block.tensor
            def _(pe):
                def each(bank, at, width, *terms):
                    for j in range(PAIRS):
                        for h in range(2):
                            rows = slice(h * HD, (h + 1) * HD)
                            for n, (lhs, rhs) in enumerate(terms):
                                last = nc.tensor.matmul(BANK[rows, bank, at + j * width:at + (j + 1) * width],
                                                        lhs(j)[rows], rhs(j)[rows], start=(n == 0), stop=(n == len(terms) - 1))
                    return last

                with pe.Fori(0, N) as i:
                    for d in range(NDIR):
                        bank = 4 * d
                        q = lambda j: QR[d][:, j, 0]
                        qr = lambda j: QR[d][:, j].rearrange("p q t -> p (q t)")
                        pe.wait_ge(s_qr[d].sem, s_qr[d].base + i + 1)
                        pe.wait_ge(s_ops[d].sem, s_ops[d].base + i + 1)
                        pe.wait_ge(s_sa_out[d].sem, s_sa_out[d].base + i)
                        hold(pe)
                        s_gram[d].mark(each(bank + B_LT, 0, 2 * HD, (lambda j: BT[d][:, j], qr)))
                        each(bank + B_L, 0, HD, (q, lambda j: BT[d][:, j]))
                        s_gram[d].mark(each(bank + B_L, HALF, HD, (lambda j: KH[d][:, j], lambda j: eye_heads[:])))
                        pe.wait_ge(s_st[d].sem, s_st[d].base + i)
                        hold(pe)
                        each(bank + B_V, 0, HD, (lambda j: VF[d][:, j], lambda j: eye_heads[:]))
                        s_gram[d].mark(each(bank + B_V, HALF, HD, (lambda j: BH[d][:, j], lambda j: eye_heads[:])))
                        if need_y:
                            pe.wait_ge(s_y_out[d].sem, s_y_out[d].base + i)
                        hold(pe)
                        s_gram[d].mark(each(bank + B_G, 0, 2 * HD, (lambda j: KT[d][:, j], qr)))
                    for l in range(1, LEVELS):
                        for d in range(NDIR):
                            pe.wait_ge(s_t[d].sem, s_t[d].base + LEVELS * i + l)
                            pe.wait_ge(s_lm[d].sem, s_lm[d].base + NL * i + l)
                            hold(pe)
                            s_x1[d].mark(each(4 * d + B_L, 0, HD, (lambda j: LM[d][:, j], lambda j: T2[d][:, 0, j])))
                        for d in range(NDIR):
                            pe.wait_ge(s_x1_out[d].sem, s_x1_out[d].base + NL * i + l)
                            hold(pe)
                            if l < LEVELS - 1:
                                each(4 * d + B_LT, 0, HD, (lambda j: T2[d][:, 1, j], lambda j: X1[d][:, j]))
                            s_tx[d].mark(each(4 * d + B_LT, HALF, HD, (lambda j: X1[d][:, j], lambda j: T2[d][:, 1, j])))
                    for d in range(NDIR):
                        pe.wait_ge(s_gram_out[d].sem, s_gram_out[d].base + i + 1)
                        pe.wait_ge(s_qr2[d].sem, s_qr2[d].base + i + 1)
                        pe.wait_ge(s_tok_out[d].sem, s_tok_out[d].base + 2 * i + 2)
                        if clear:
                            pe.wait_ge(*s_init(1))
                        hold(pe)
                        s_w[d].mark(each(4 * d + B_L, 0, HD, (lambda j: QR2[d][:, j, 0], lambda j: ST[d][:, j]),
                                         (lambda j: GA[d][:, j, 0], lambda j: VB_TOK[d][:, 0, j])))
                    for d in range(NDIR):
                        pe.wait_ge(s_w_out[d].sem, s_w_out[d].base + i + 1)
                        pe.wait_ge(s_t[d].sem, s_t[d].base + LEVELS * i + LEVELS)
                        hold(pe)
                        s_sa[d].mark(each(4 * d + B_LT, 0, HD, (lambda j: T2[d][:, 1, j], lambda j: WS[d][:, j])))
                    for d in range(NDIR):
                        pe.wait_ge(s_sa_out[d].sem, s_sa_out[d].base + i + 1)
                        hold(pe)
                        if need_y:
                            s_y[d].mark(each(4 * d + B_G, 0, HD, (lambda j: ST[d][:, j], lambda j: QR2[d][:, j, 1]),
                                             (lambda j: SA[d][:, j], lambda j: ARB[d][:, j]),
                                             (lambda j: VB_TOK[d][:, 0, j], lambda j: GA[d][:, j, 1])))
                        s_ds[d].mark(each(4 * d + B_V, 0, HD, (lambda j: VB_TOK[d][:, 1, j], lambda j: SA[d][:, j]),
                                          (lambda j: KH_TOK[d][:, j], lambda j: VB_TOK[d][:, 0, j])))
        Signal.trips = 1
        Signal.end_stage()

    O_R = carve(WORK, F0 + 9 * WIDTH * 4 - WIDTH * 4, PAIRS, TOK)

    def rwkv_output(t0):
        n = TOK - t0
        A1 = carve(WORK, F0 + 5 * WIDTH * 4, PAIRS, TOK)
        A2 = carve(WORK, F0 + 6 * WIDTH * 4, PAIRS, TOK)
        with stage() as block:
            @block.tensor
            def _(pe):
                for j in range(PAIRS):
                    sums.mark(nc.tensor.matmul(BANK[:, j, 0:n], head_ones[:], Y[:, j, t0:], start=True, stop=True))
                for j in range(PAIRS):
                    pe.wait_ge(*scaled(j + 1))
                    product.mark(nc.tensor.matmul(BANK[:, 4 + j, 0:n], head_ones[:], A1[:, j, t0:], start=True, stop=True))
                for j in range(PAIRS):
                    pe.wait_ge(*squares(j + 1))
                    pe.wait_ge(*dve_sig(3 * j + 3))
                    sums.mark(nc.tensor.matmul(BANK[:, j, 0:n], head_ones[:], A2[:, j, t0:], start=True, stop=True))
                for j in range(PAIRS):
                    pe.wait_ge(*evacuated(j + 1))
                    product.mark(nc.tensor.matmul(BANK[:, 4 + j, 0:n], g2_sb[:, j * P:(j + 1) * P], Z[:, Z_G, t0:], start=True, stop=True))

            @block.scalar
            def _(act):
                for j in range(PAIRS):
                    act.wait_ge(*dve_sig(3 * j + 3))
                    squares.mark(nc.scalar.activation(A2[:, j, t0:], Y[:, j, t0:], ACT.Square))
                for j in range(PAIRS):
                    act.wait_ge(*merged(j + 1))
                    inverse_rms.mark(nc.scalar.activation(A2[:, j, t0:], A2[:, j, t0:], ACT.Sqrt))

            @block.vector
            def _(dve):
                c = 0
                for j in range(PAIRS):
                    dve_sig.mark(nc.vector.tensor_tensor(A1[:, j, t0:], KD[0][:, j, t0:], KD[1][:, j, t0:], ALU.add))
                    dve.wait_ge(*dve_sig(3 * j + 1))
                    dve_sig.mark(nc.vector.tensor_scalar(A1[:, j, t0:], A1[:, j, t0:], v("r_k", j), None, ALU.mult))
                    dve.wait_ge(*dve_sig(3 * j + 2))
                    scaled.mark(nc.vector.tensor_tensor(A1[:, j, t0:], A1[:, j, t0:], Z[:, Z_R + j, t0:], ALU.mult))
                    dve.wait_ge(*sums(j + 1))
                    dve_sig.mark(nc.vector.scalar_tensor_tensor(Y[:, j, t0:], BANK[:, j, 0:n], -1.0 / HD, Y[:, j, t0:], ALU.mult, ALU.add))
                c = 3 * PAIRS
                for j in range(PAIRS):
                    dve.wait_ge(*product(j + 1))
                    evacuated.mark(nc.vector.tensor_tensor(O_R[:, j, t0:], BANK[:, 4 + j, 0:n], Z[:, Z_V + j, t0:], ALU.mult))
                for j in range(PAIRS):
                    dve.wait_ge(*sums(PAIRS + j + 1))
                    c += 1
                    dve_sig.mark(nc.vector.tensor_scalar(A2[:, j, t0:], BANK[:, j, 0:n], 1.0 / HD, GN_EPS, ALU.mult, ALU.add))
                    dve.wait_ge(*dve_sig(c))
                    merged.mark(nc.vector.reciprocal(A2[:, j, t0:], A2[:, j, t0:]))
                for j in range(PAIRS):
                    dve.wait_ge(*inverse_rms(j + 1))
                    c += 1
                    dve_sig.mark(nc.vector.scalar_tensor_tensor(Y[:, j, t0:], Y[:, j, t0:], v("gn_w", j), A2[:, j, t0:], ALU.mult, ALU.mult))
                    dve.wait_ge(*dve_sig(c))
                    c += 1
                    dve_sig.mark(nc.vector.scalar_tensor_tensor(Y[:, j, t0:], Y[:, j, t0:], v("gn_b", j), O_R[:, j, t0:], ALU.add, ALU.add))
                    dve.wait_ge(*dve_sig(c))
                    dve.wait_ge(*product(PAIRS + j + 1))
                    nc.vector.tensor_tensor(O_R[:, j, t0:], Y[:, j, t0:], BANK[:, 4 + j, 0:n], ALU.mult)
        Signal.end_stage()

    O_M = carve(WORK, 0, PAIRS, TOK)
    M0 = PAIRS * TOK
    ZM = carve(WORK, M0, 5, TOK)
    QH = carve(WORK, M0 + 5 * TOK, HEADS, TOK)
    KHD = carve(WORK, M0 + (5 + HEADS) * TOK, HEADS, TOK)
    VT = carve(WORK, M0 + (5 + 2 * HEADS) * TOK, 4, WIDTH)
    M1 = M0 + (9 + 2 * HEADS) * TOK
    MT = carve(WORK, M1, 8, TOK)
    assert M1 + 8 * TOK <= F0 + 8 * WIDTH * 4

    def mla_project(l, tq):
        w = ins["w_in"][l]
        loads = Loads([k_tiles(w, C_MLA, C_MLA + 256), k_tiles(w, C_MLA + 256, C_MLA + 512), k_tiles(w, C_MLA + 512, C_FNO)])
        groups = ((0, 3, Q_LORA, "g_cq"), (3, 4, KV_LORA, "g_ckv"))
        with stage() as block:
            @block.sync
            def _(sp):
                loads.issue(sp)

            @block.tensor
            def _(pe):
                for m in range(5):
                    if m % 2 == 0:
                        wt = loads.arrived(pe, m // 2)
                    rows = P if m < 4 else QK_ROPE
                    for k in range(DT):
                        last = nc.tensor.matmul(BANK[0:rows, m], wt[:, k, (m % 2) * P:(m % 2) * P + rows], H[:, k],
                                                start=(k == 0), stop=(k == DT - 1))
                    product.mark(last)
                for g, (m0, m1, _, _) in enumerate(groups):
                    for m in range(m0, m1):
                        pe.wait_ge(*squares(m + 1))
                        last = nc.tensor.matmul(BANK[:, 5 + g], ones[:], MT[:, m], start=(m == m0), stop=(m == m1 - 1))
                    sums.mark(last)

            @block.scalar
            def _(act):
                for m in range(5):
                    rows = P if m < 4 else QK_ROPE
                    act.wait_ge(*product(m + 1))
                    evacuated.mark(nc.scalar.activation(ZM[0:rows, m], BANK[0:rows, m], ACT.Copy))
                    if m < 4:
                        squares.mark(nc.scalar.activation(MT[:, m], BANK[:, m], ACT.Square))
                for g in range(2):
                    act.wait_ge(*merged(g + 1))
                    inverse_rms.mark(nc.scalar.activation(MT[:, 4 + g], MT[:, 4 + g], ACT.Sqrt))

            @block.vector
            def _(dve):
                for g, (m0, m1, width, gname) in enumerate(groups):
                    dve.wait_ge(*sums(g + 1))
                    dve_sig.mark(nc.vector.tensor_scalar(MT[:, 4 + g], BANK[:, 5 + g], 1.0 / width, RMS_EPS, ALU.mult, ALU.add))
                    dve.wait_ge(*dve_sig(g + 1))
                    merged.mark(nc.vector.reciprocal(MT[:, 4 + g], MT[:, 4 + g]))
                for g, (m0, m1, width, gname) in enumerate(groups):
                    dve.wait_ge(*inverse_rms(g + 1))
                    for m in range(m0, m1):
                        dve.wait_ge(*evacuated(m + 1))
                        nc.vector.scalar_tensor_tensor(ZM[:, m], ZM[:, m], v(gname, m - m0), MT[:, 4 + g], ALU.mult, ALU.mult)
        Signal.end_stage()

    def mla_heads(l, tq):
        wq = ins["w_uq"][l].rearrange("(k p) n -> p k n", p=P)
        loads = Loads([wq[:, :, 0:4 * QK], wq[:, :, 4 * QK:8 * QK], ins["w_ukv"][l].rearrange("(k p) n -> p k n", p=P)])
        units = [("q", h, tq) for h in range(HEADS)] + [("k", h, 0) for h in range(HEADS)]
        U = len(units)
        cos, sin = rope[:, 0:SEQ], rope[:, SEQ:2 * SEQ]
        rotate = rope[:, 2 * SEQ:]
        dst = lambda u: (QH if units[u][0] == "q" else KHD)[0:QK, units[u][1]]
        sq = lambda u: MT[0:QK, u % 2]
        rs = lambda u: MT[0:QK, 2 + u % 2]
        tmp = lambda u: MT[0:QK, 4 + u % 2, 0:SEQ]
        with stage() as block:
            @block.sync
            def _(sp):
                loads.issue(sp)

            @block.tensor
            def _(pe):
                for u in range(U + 2):
                    if u < U:
                        kind, h, t = units[u]
                        if u >= 2:
                            pe.wait_ge(*scaled(u - 1))
                        if kind == "q":
                            w = loads.arrived(pe, h // 4)
                            for k in range(3):
                                last = nc.tensor.matmul(BANK[0:QK, u % 2, 0:TOK - t], w[:, k, (h % 4) * QK:(h % 4 + 1) * QK], ZM[:, k, t:],
                                                        start=(k == 0), stop=(k == 2))
                        else:
                            w = loads.arrived(pe, 2)
                            nc.tensor.matmul(BANK[0:QK_NOPE, u % 2], w[:, 0, h * P:h * P + QK_NOPE], ZM[:, 3], start=True, stop=True)
                            last = nc.tensor.matmul(BANK[QK_NOPE:QK, u % 2], ident[0:QK_ROPE, 0:QK_ROPE], ZM[0:QK_ROPE, 4], start=True, stop=True)
                        product.mark(last)
                    if 1 <= u <= U:
                        n = TOK - units[u - 1][2]
                        pe.wait_ge(*squares(u))
                        if u >= 3:
                            pe.wait_ge(*dve_sig(2 * (u - 3) + 1))
                        sums.mark(nc.tensor.matmul(BANK[0:QK, 2 + (u - 1) % 2, 0:n], ones[0:QK, 0:QK], sq(u - 1)[:, 0:n], start=True, stop=True))
                    if u >= 2:
                        pe.wait_ge(*scaled(u - 1))
                        if u >= 4:
                            pe.wait_ge(*gate_ready(u - 3))
                        turned_out.mark(nc.tensor.matmul(BANK[0:QK, 4 + u % 2, 0:SEQ], rotate, dst(u - 2)[:, CTX:], start=True, stop=True))
                w = loads.arrived(pe, 2)
                wv = w[:, 0].rearrange("p (h n) -> p h n", h=HEADS)[:, :, QK_NOPE:]
                for t in range(4):
                    pe.wait_ge(*gate_ready(U))
                    product.mark(nc.tensor.matmul(BANK[:, t].rearrange("p (h n) -> p h n", h=HEADS), ZM[:, 3, t * P:(t + 1) * P], wv, start=True, stop=True))

            @block.scalar
            def _(act):
                for u in range(U + 1):
                    if u < U:
                        n = TOK - units[u][2]
                        act.wait_ge(*product(u + 1))
                        if u >= 2:
                            act.wait_ge(*sums(u - 1))
                        squares.mark(nc.scalar.activation(sq(u)[:, 0:n], BANK[0:QK, u % 2, 0:n], ACT.Square))
                    if u >= 1:
                        n = TOK - units[u - 1][2]
                        act.wait_ge(*dve_sig(2 * (u - 1) + 2))
                        inverse_rms.mark(nc.scalar.activation(rs(u - 1)[:, 0:n], rs(u - 1)[:, 0:n], ACT.Sqrt))
                for t in range(4):
                    act.wait_ge(*product(U + t + 1))
                    nc.scalar.activation(VT[:, t], BANK[:, t], ACT.Copy)

            @block.vector
            def _(dve):
                for u in range(U + 2):
                    if 1 <= u <= U:
                        t = units[u - 1][2]
                        n = TOK - t
                        g = 0 if units[u - 1][0] == "q" else 1
                        dve.wait_ge(*sums(u))
                        dve_sig.mark(nc.vector.tensor_scalar(rs(u - 1)[:, 0:n], BANK[0:QK, 2 + (u - 1) % 2, 0:n], 1.0 / QK, RMS_EPS, ALU.mult, ALU.add))
                        dve.wait_ge(*dve_sig(2 * (u - 1) + 1))
                        dve_sig.mark(nc.vector.reciprocal(rs(u - 1)[:, 0:n], rs(u - 1)[:, 0:n]))
                        dve.wait_ge(*inverse_rms(u))
                        scaled.mark(nc.vector.scalar_tensor_tensor(dst(u - 1)[:, t:], BANK[0:QK, (u - 1) % 2, 0:n], g_head[:, g:g + 1],
                                                                   rs(u - 1)[:, 0:n], ALU.mult, ALU.mult))
                    if u >= 2:
                        dve.wait_ge(*turned_out(u - 1))
                        if u >= 4:
                            dve.wait_ge(*pool_sig(2 * (u - 4) + 2))
                        gate_ready.mark(nc.vector.tensor_tensor(tmp(u), BANK[0:QK, 4 + u % 2, 0:SEQ], sin, ALU.mult))

            @block.gpsimd
            def _(pool):
                for u in range(U):
                    pool.wait_ge(*gate_ready(u + 1))
                    pool_sig.mark(nc.gpsimd.tensor_tensor(dst(u)[:, CTX:], dst(u)[:, CTX:], cos, ALU.mult))
                    pool.wait_ge(*pool_sig(2 * u + 1))
                    pool_sig.mark(nc.gpsimd.tensor_tensor(dst(u)[:, CTX:], dst(u)[:, CTX:], tmp(u), ALU.add))
        Signal.end_stage()

    def attention(tq):
        units = [(h, q) for h in range(HEADS) for q in range(tq // P, TOK // P)]
        U = len(units)
        keys = lambda u: TOK if units[u][1] * P >= CTX else CTX
        PR = lambda u: MT[:, u % 2]
        PTR = lambda u: MT[:, 2 + u % 2]
        stat = carve(WORK, M1 + 4 * TOK, 3, TOK)
        with stage() as block:
            @block.tensor
            def _(pe):
                for u in range(U + 2):
                    if u < U:
                        h, q = units[u]
                        if u >= 2:
                            pe.wait_ge(*squares(u - 1))
                        product.mark(nc.tensor.matmul(BANK[:, u % 2, 0:keys(u)], QH[0:QK, h, q * P:(q + 1) * P], KHD[0:QK, h, 0:keys(u)], start=True, stop=True))
                    if 1 <= u <= U:
                        pe.wait_ge(*scaled(u))
                        if u >= 3:
                            pe.wait_ge(*turned_out(u - 2))
                        for k in range(keys(u - 1) // P):
                            last = nc.tensor.transpose(BANK[:, 2 + (u - 1) % 2, k * P:(k + 1) * P], PR(u - 1)[:, k * P:(k + 1) * P], ident[:])
                        rows_turned.mark(last)
                    if u >= 2:
                        h, q = units[u - 2]
                        rows = slice((h % 2) * VH, (h % 2 + 1) * VH)
                        pe.wait_ge(*turned_out(u - 1))
                        if u >= 4:
                            pe.wait_ge(*evacuated(u - 3))
                        n = keys(u - 2) // P
                        for k in range(n):
                            last = nc.tensor.matmul(BANK[rows, 4 + u % 2, 0:P], VT[:, k, h * VH:(h + 1) * VH], PTR(u - 2)[:, k * P:(k + 1) * P],
                                                    start=(k == 0), stop=(k == n - 1))
                        sums.mark(last)

            @block.vector
            def _(dve):
                c = 0
                for u in range(U + 2):
                    if u < U:
                        dve.wait_ge(*product(u + 1))
                        c += 1
                        dve_sig.mark(nc.vector.reduce_max(stat[:, 0, u:u + 1], BANK[:, u % 2, 0:keys(u)], AX.X))
                        dve.wait_ge(*dve_sig(c))
                        gate_ready.mark(nc.vector.tensor_scalar(stat[:, 1, u:u + 1], stat[:, 0, u:u + 1], -(QK ** -0.5), None, ALU.mult))
                    if u >= 1 and u <= U:
                        dve.wait_ge(*squares(u))
                        c += 1
                        dve_sig.mark(nc.vector.reciprocal(stat[:, 2, 2 * u - 1:2 * u], stat[:, 2, 2 * u - 2:2 * u - 1]))
                        dve.wait_ge(*dve_sig(c))
                        scaled.mark(nc.vector.tensor_scalar(PR(u - 1)[:, 0:keys(u - 1)], PR(u - 1)[:, 0:keys(u - 1)], stat[:, 2, 2 * u - 1:2 * u], None, ALU.mult))
                    if u >= 2:
                        h, q = units[u - 2]
                        rows = slice((h % 2) * VH, (h % 2 + 1) * VH)
                        dve.wait_ge(*sums(u - 1))
                        evacuated.mark(nc.vector.tensor_copy(O_M[rows, h // 2, q * P:(q + 1) * P], BANK[rows, 4 + u % 2, 0:P]))

            @block.scalar
            def _(act):
                for u in range(U + 1):
                    if u < U:
                        act.wait_ge(*gate_ready(u + 1))
                        if u >= 2:
                            act.wait_ge(*rows_turned(u - 1))
                        squares.mark(nc.scalar.activation(PR(u)[:, 0:keys(u)], BANK[:, u % 2, 0:keys(u)], ACT.Exp, bias=stat[:, 1, u:u + 1],
                                                          scale=QK ** -0.5, accum_out=stat[:, 2, 2 * u:2 * u + 1]))
                    if u >= 1:
                        act.wait_ge(*rows_turned(u))
                        if u >= 3:
                            act.wait_ge(*sums(u - 2))
                        turned_out.mark(nc.scalar.activation(PTR(u - 1)[:, 0:keys(u - 1)], BANK[:, 2 + (u - 1) % 2, 0:keys(u - 1)], ACT.Copy))
        Signal.end_stage()

    O_F = carve(WORK, M0, PAIRS, TOK)
    FN0 = M0 + PAIRS * TOK

    def fourier(l, t0):
        w = ins["w_in"][l]
        loads = Loads([k_tiles(w, C_FNO, C_FNO + 256), k_tiles(w, C_FNO + 256, C_FNO + 512)])
        ZF = carve(WORK, FN0, PAIRS, TOK)
        UF = carve(WORK, FN0 + PAIRS * TOK, PAIRS, 4, 2 * P)
        n = TOK - t0
        tiles = list(range(t0 // P, 4))
        with stage() as block:
            @block.sync
            def _(sp):
                loads.issue(sp)

            @block.tensor
            def _(pe):
                for m in range(PAIRS):
                    if m % 2 == 0:
                        wt = loads.arrived(pe, m // 2)
                    for k in range(DT):
                        last = nc.tensor.matmul(BANK[:, m, 0:n], wt[:, k, (m % 2) * P:(m % 2 + 1) * P], H[:, k, t0:],
                                                start=(k == 0), stop=(k == DT - 1))
                    product.mark(last)
                i = 0
                for m in range(PAIRS):
                    pe.wait_ge(*evacuated(m + 1))
                    for t in tiles:
                        if i >= 4:
                            pe.wait_ge(*turned_out(i - 3))
                        rows_turned.mark(nc.tensor.matmul(BANK[:, 4 + i % 4, 0:2 * P], ZF[:, m, t * P:(t + 1) * P], dft_feature[:], start=True, stop=True))
                        i += 1
                i = 0
                for m in range(PAIRS):
                    for s in range(t0 // CTX, 2):
                        pe.wait_ge(*turned_out(len(tiles) * m + 2 * (s - t0 // CTX) + 2))
                        if i >= 4:
                            pe.wait_ge(*scaled(i - 3))
                        for part in range(2):
                            for t in range(2):
                                last = nc.tensor.matmul(BANK[:, i % 4, 0:SEQ], UF[:, m, 2 * s + t, part * P:(part + 1) * P],
                                                        dft_token[:, t, part * SEQ:(part + 1) * SEQ],
                                                        start=(part == 0 and t == 0), stop=(part == 1 and t == 1))
                        sums.mark(last)
                        i += 1

            @block.scalar
            def _(act):
                for m in range(PAIRS):
                    act.wait_ge(*product(m + 1))
                    evacuated.mark(nc.scalar.activation(ZF[:, m, t0:], BANK[:, m, 0:n], ACT.Copy))
                i = 0
                for m in range(PAIRS):
                    for t in tiles:
                        act.wait_ge(*rows_turned(i + 1))
                        turned_out.mark(nc.scalar.activation(UF[:, m, t], BANK[:, 4 + i % 4, 0:2 * P], ACT.Copy))
                        i += 1

            @block.vector
            def _(dve):
                i = 0
                for m in range(PAIRS):
                    for s in range(t0 // CTX, 2):
                        dve.wait_ge(*sums(i + 1))
                        scaled.mark(nc.vector.tensor_copy(O_F[:, m, s * SEQ:(s + 1) * SEQ], BANK[:, i % 4, 0:SEQ]))
                        i += 1
        Signal.end_stage()

    MERGE = carve(WORK, FN0, DT, TOK)
    TMP = carve(WORK, FN0 + DT * TOK, 4, TOK)

    def merge(l, t0):
        n = TOK - t0
        w = ins["w_in"][l]
        sources = []
        for mm in range(DT // 2):
            for b, wo in enumerate(("w_rwkv_o", "w_mla_o", "w_fno")):
                c = C_GATE + b * D + mm * 2 * P
                sources += [k_tiles(w, c, c + 2 * P), k_tiles(ins[wo][l], mm * 2 * P, (mm + 1) * 2 * P)]
        loads = Loads(sources)
        units = [(mm, b, m) for mm in range(DT // 2) for b in range(3) for m in range(2)]
        branch = (O_R, O_M, O_F)
        sums_of = lambda u: sum(1 for x in units[:u + 1] if x[1] > 0)
        with stage() as block:
            @block.sync
            def _(sp):
                loads.issue(sp, lambda i: (product if i % 2 else pe_sig)(2 * (i // 2) + 2))

            @block.tensor
            def _(pe):
                for u, (mm, b, m) in enumerate(units):
                    if m == 0:
                        wg = loads.arrived(pe, (mm * 3 + b) * 2)
                        wo = loads.arrived(pe, (mm * 3 + b) * 2 + 1)
                    if u >= 2:
                        pe.wait_ge(*gate_ready(u - 1))
                    for k in range(DT):
                        last = nc.tensor.matmul(BANK[:, u % 2, 0:n], wg[:, k, m * P:(m + 1) * P], H[:, k, t0:], start=(k == 0), stop=(k == DT - 1))
                    pe_sig.mark(last)
                    if u >= 2:
                        pe.wait_ge(*scaled(u - 1))
                    for k in range(PAIRS):
                        last = nc.tensor.matmul(BANK[:, 2 + u % 2, 0:n], wo[:, k, m * P:(m + 1) * P], branch[b][:, k, t0:], start=(k == 0), stop=(k == PAIRS - 1))
                    product.mark(last)

            @block.scalar
            def _(act):
                for u in range(len(units)):
                    act.wait_ge(*pe_sig(u + 1))
                    if u >= 2:
                        act.wait_ge(*scaled(u - 1))
                    gate_ready.mark(nc.scalar.activation(TMP[:, u % 2, 0:n], BANK[:, u % 2, 0:n], ACT.Sigmoid))

            @block.vector
            def _(dve):
                for u, (mm, b, m) in enumerate(units):
                    out_m = MERGE[:, 2 * mm + m, t0:]
                    dve.wait_ge(*gate_ready(u + 1))
                    dve.wait_ge(*product(u + 1))
                    if b > 0 and sums_of(u - 2) > 0:
                        dve.wait_ge(*pool_sig(sums_of(u - 2)))
                    dst = out_m if b == 0 else TMP[:, 2 + u % 2, 0:n]
                    scaled.mark(nc.vector.tensor_tensor(dst, TMP[:, u % 2, 0:n], BANK[:, 2 + u % 2, 0:n], ALU.mult))

            @block.gpsimd
            def _(pool):
                for u, (mm, b, m) in enumerate(units):
                    out_m = MERGE[:, 2 * mm + m, t0:]
                    pool.wait_ge(*scaled(u + 1))
                    if b > 0:
                        if sums_of(u - 2) > 0:
                            pool.wait_ge(*pool_sig(sums_of(u - 2)))
                        pool_sig.mark(nc.gpsimd.tensor_tensor(out_m, out_m, TMP[:, 2 + u % 2, 0:n], ALU.add))
        Signal.end_stage()

    def add_to_stream(dve, m, bank, which, t0, mark):
        for s in range(t0 // CTX, 2):
            a = s * CTX
            last = nc.vector.scalar_tensor_tensor(X[:, m, a:a + CTX], BANK[:, bank, a - t0:a - t0 + CTX], mod[:, which, m, s:s + 1],
                                                  X[:, m, a:a + CTX], ALU.mult, ALU.add)
        mark(last)

    def project_out(l, t0):
        n = TOK - t0
        loads = Loads([k_tiles(ins["w_out"][l], c, c + 2 * P) for c in range(0, D, 2 * P)])
        with stage() as block:
            @block.sync
            def _(sp):
                loads.issue(sp)

            @block.tensor
            def _(pe):
                for m in range(DT):
                    if m % 2 == 0:
                        w = loads.arrived(pe, m // 2)
                    for k in range(DT):
                        last = nc.tensor.matmul(BANK[:, m, 0:n], w[:, k, (m % 2) * P:(m % 2 + 1) * P], MERGE[:, k, t0:], start=(k == 0), stop=(k == DT - 1))
                    product.mark(last)

            @block.vector
            def _(dve):
                for m in range(DT):
                    dve.wait_ge(*product(m + 1))
                    add_to_stream(dve, m, m, 2, t0, evacuated.mark)
        Signal.end_stage()

    HID = carve(WORK, 0, FT, TOK)
    FTMP = carve(WORK, FT * TOK, 2, TOK)

    def ffn_in(l, t0):
        n = TOK - t0
        w = ins["w_ffn_in"][l]
        sources = []
        for c in range(0, FFN, 2 * P):
            sources += [k_tiles(w, c, c + 2 * P), k_tiles(w, FFN + c, FFN + c + 2 * P)]
        loads = Loads(sources)
        with stage() as block:
            @block.sync
            def _(sp):
                loads.issue(sp, lambda i: (product if i % 2 else pe_sig)(i // 2 * 2 + 2))

            @block.tensor
            def _(pe):
                for u in range(FT):
                    if u % 2 == 0:
                        ws = [loads.arrived(pe, u), loads.arrived(pe, u + 1)]
                    for g, wt in enumerate(ws):
                        if u >= 2:
                            pe.wait_ge(*(gate_ready if g == 0 else scaled)(u - 1))
                        for k in range(DT):
                            last = nc.tensor.matmul(BANK[:, 2 * g + u % 2, 0:n], wt[:, k, (u % 2) * P:(u % 2 + 1) * P], H[:, k, t0:],
                                                    start=(k == 0), stop=(k == DT - 1))
                        (pe_sig if g == 0 else product).mark(last)

            @block.scalar
            def _(act):
                for u in range(FT):
                    act.wait_ge(*pe_sig(u + 1))
                    if u >= 2:
                        act.wait_ge(*scaled(u - 1))
                    gate_ready.mark(nc.scalar.activation(FTMP[:, u % 2, 0:n], BANK[:, u % 2, 0:n], ACT.Silu))

            @block.vector
            def _(dve):
                for u in range(FT):
                    dve.wait_ge(*gate_ready(u + 1))
                    dve.wait_ge(*product(u + 1))
                    scaled.mark(nc.vector.tensor_tensor(HID[:, u, t0:], FTMP[:, u % 2, 0:n], BANK[:, 2 + u % 2, 0:n], ALU.mult))
        Signal.end_stage()

    def ffn_out(l, t0):
        n = TOK - t0
        w = ins["w_ffn_out"][l].rearrange("(k p) n -> p k n", p=P)
        loads = Loads([w[:, k:k + 2, :] for k in range(0, FT, 2)])
        with stage() as block:
            @block.sync
            def _(sp):
                loads.issue(sp, lambda i: slot_used(i + 1))

            @block.tensor
            def _(pe):
                for i in range(FT // 2):
                    wt = loads.arrived(pe, i)
                    for m in range(DT):
                        for k in range(2):
                            last = nc.tensor.matmul(BANK[:, m, 0:n], wt[:, k, m * P:(m + 1) * P], HID[:, 2 * i + k, t0:],
                                                    start=(i == 0 and k == 0), stop=(i == FT // 2 - 1 and k == 1))
                        if i == FT // 2 - 1:
                            product.mark(last)
                    if i < FT // 2 - 1:
                        slot_used.mark(last)

            @block.vector
            def _(dve):
                for m in range(DT):
                    dve.wait_ge(*product(m + 1))
                    add_to_stream(dve, m, m, 5, t0, evacuated.mark)
        Signal.end_stage()

    for l in range(DEPTH):
        t0 = CTX if l == DEPTH - 1 else 0
        modulation(l)
        norm(scale_1, mod[:, 0], 0)
        project_rwkv(l)
        features()
        scan(0, l < DEPTH - 1, True)
        scan(1, True, False)
        rwkv_output(t0)
        norm(scale_1, mod[:, 0], 0)
        mla_project(l, t0)
        mla_heads(l, t0)
        attention(t0)
        fourier(l, t0)
        merge(l, t0)
        project_out(l, t0)
        norm(scale_2, mod[:, 3], t0)
        ffn_in(l, t0)
        ffn_out(l, t0)

    result = carve(WORK, 0, 2, D)
    with stage() as block:
        @block.tensor
        def _(pe):
            for b in range(4):
                for q in range(4):
                    t, k = b // 2, (b % 2) * 4 + q
                    last = nc.tensor.transpose(BANK[:, b, q * P:(q + 1) * P], X[:, k, CTX + t * P:CTX + (t + 1) * P], ident[:])
                rows_turned.mark(last)

        @block.vector
        def _(dve):
            for b in range(4):
                dve.wait_ge(*rows_turned(b + 1))
                turned_out.mark(nc.vector.tensor_copy(result[:, b // 2, (b % 2) * 512:(b % 2 + 1) * 512], BANK[:, b]))

        @block.sync
        def _(sp):
            sp.wait_ge(*turned_out(4))
            sp.dma_start(out[0].rearrange("(t p) d -> p t d", p=P), result).then_inc(out_stored, 16)
            sp.wait_ge(out_stored, 16)
    Signal.end_stage()


def kernel(**inputs):
    from concourse import bacc
    from concourse.bass_utils import run_bass_kernel_spmd

    nc = bacc.Bacc("TRN2", target_bir_lowering=False, num_devices=1)
    arrays, aps = {}, {}
    for name, a in {**inputs, **shape_constants()}.items():
        a = np.ascontiguousarray(a)
        arrays[f"{name}_dram"] = a
        aps[name] = nc.dram_tensor(f"{name}_dram", a.shape, mybir.dt.from_np(a.dtype), kind="ExternalInput").ap()
    out = nc.dram_tensor("out_dram", (1, SEQ, D), FP32, kind="ExternalOutput").ap()
    build(nc, aps, out)
    result = run_bass_kernel_spmd(nc, [arrays], core_ids=[0])
    return result.results[0]["out_dram"]
```

```python
from contextlib import ExitStack

import concourse.bass as bass
import numpy as np
from concourse import mybir

FP32 = mybir.dt.float32
FP32R = mybir.dt.float32r
ACT = mybir.ActivationFunctionType
ALU = mybir.AluOpType
AX = mybir.AxisListType

P = 128
D = 1024
DT = D // P
SEQ = 256
CTX = 256
TOK = CTX + SEQ
DEPTH = 2
GRID_W = 64

HEADS = 8
HD = 64
PAIRS = HEADS // 2
WIDTH = HEADS * HD
NDIR = 2
Z_R, Z_K, Z_V, Z_W, Z_A, Z_G = 0, 4, 8, 12, 13, 14
Z_TILES = 15
N_RWKV_IN = Z_TILES * P

QK_NOPE, QK_ROPE = 64, 32
QK = QK_NOPE + QK_ROPE
VH = 64
Q_LORA, KV_LORA = 384, 128
ROPE_AXIS = QK_ROPE // 2
N_MLA_IN = Q_LORA + KV_LORA + QK_ROPE
C_MLA = N_RWKV_IN
C_FNO = C_MLA + N_MLA_IN
C_GATE = C_FNO + WIDTH
N_IN = C_GATE + 3 * D

FFN = ((8 * D + 3 * 256 - 1) // (3 * 256)) * 256
FT = FFN // P

RMS_EPS = 1e-6
GN_EPS = 64e-5
KAPPA = float(np.exp(-0.5))

CHUNK = 64
SEG_CHUNKS = SEQ // CHUNK
LEVELS = 6

SLOTS = 3
SLOT = 2048
CHUNKS = 3
CHUNK_W = SLOT // 2

VEC_ROWS = [("g_norm1", 8), ("g_norm2", 8), ("mu_prev", 15), ("mu_next", 15), ("w0", 8), ("a0", 8),
            ("k_k", 4), ("k_a", 4), ("r_k", 4), ("gn_w", 4), ("gn_b", 4), ("g_cq", 3), ("g_ckv", 1)]
VEC_AT = {}
_n = 0
for _name, _k in VEC_ROWS:
    VEC_AT[_name] = (_n, _k)
    _n += _k
N_VEC = _n
N_BMOD = 6 * DT


def shape_constants():
    f = np.float32
    out = {}
    out["ident"] = np.eye(P, dtype=f)
    out["head_ones"] = np.kron(np.eye(2), np.ones((HD, HD))).astype(f)
    n = np.arange(HD)
    ang = 2 * np.pi * ((n[:, None] * n[None, :]) % HD) / HD
    out["dft_feature"] = np.concatenate([np.kron(np.eye(2), np.cos(ang)), np.kron(np.eye(2), np.sin(ang))],
                                        axis=1).astype(f)
    t = np.arange(SEQ)
    ang = 2 * np.pi * ((t[:, None] * t[None, :]) % SEQ) / SEQ
    norm = 1.0 / np.sqrt(SEQ * HD)
    out["dft_token"] = np.concatenate([np.cos(ang) * norm, -np.sin(ang) * norm], axis=1).astype(f)
    inv = 10000.0 ** (-np.arange(0, ROPE_AXIS, 2, dtype=np.float64) / ROPE_AXIS)
    cos, sin = np.ones((QK, SEQ)), np.zeros((QK, SEQ))
    rot = np.zeros((QK, QK))
    h = ROPE_AXIS // 2
    for axis, pos in enumerate((t // GRID_W, t % GRID_W)):
        a = pos[None, :] * inv[:, None]
        lo = QK_NOPE + axis * ROPE_AXIS
        for part in (0, h):
            cos[lo + part:lo + part + h] = np.cos(a)
            sin[lo + part:lo + part + h] = np.sin(a)
        for i in range(h):
            rot[lo + h + i, lo + i] = -1.0
            rot[lo + i, lo + h + i] = 1.0
    out["rope"] = np.concatenate([cos, sin, rot], axis=1).astype(f)
    r, c = np.arange(HD)[:, None], np.arange(HD)[None, :]
    stack = lambda m: np.concatenate([m, m], axis=0)
    masks = []
    for d in range(NDIR):
        earlier = (lambda a, b: a < b) if d == 0 else (lambda a, b: a > b)
        level = []
        for l in range(LEVELS):
            b = 1 << l
            same = (r // (2 * b) == c // (2 * b)) & (r // b != c // b)
            level.append(same & earlier(r, c))
        strict_t = earlier(r, c)
        incl_t = strict_t | (r == c)
        parts = [-(level[0].T.astype(f)), -(level[0].astype(f))] + [m.astype(f) for m in level[1:]]
        parts += [strict_t.astype(f), incl_t.astype(f)]
        masks.append(np.concatenate([stack(m) for m in parts], axis=1))
    out["masks"] = np.concatenate(masks, axis=1).astype(f)
    out["eye_heads"] = stack(np.eye(HD)).astype(f)
    return out


class Signal:

    trips = 1
    every = []

    def __init__(self, ctx, nc, name):
        self.sem = ctx.enter_context(nc.semaphore(name))
        self.base = 0
        self.made = 0
        Signal.every.append(self)

    def mark(self, ins):
        self.made += Signal.trips
        return ins.then_inc(self.sem, 1)

    def __call__(self, k):
        return self.sem, self.base + k

    @staticmethod
    def end_stage():
        for s in Signal.every:
            s.base += s.made
            s.made = 0


def build(nc, ins, out):
    Signal.every = []
    Signal.trips = 1
    with ExitStack() as ctx:
        ctx.enter_context(nc.allow_non_contiguous_dma(reason="two norm vectors as columns"))
        build_in(ctx, nc, ins, out)


def build_in(ctx, nc, ins, out):
    def sb(name, shape):
        return ctx.enter_context(nc.sbuf_tensor(name, shape, FP32))

    def sig(name):
        return Signal(ctx, nc, name)

    X = sb("X", [P, DT, TOK])
    ident = sb("ident", [P, P])
    ones = sb("ones", [P, P])
    head_ones = sb("head_ones", [P, P])
    eye_heads = sb("eye_heads", [P, HD])
    rope = sb("rope", [QK, 2 * SEQ + QK])
    pick = sb("pick", [QK, 4 * HEADS])
    masks = sb("masks", [P, NDIR, LEVELS + 3, HD])
    chunk_start = sb("chunk_start", [P, TOK])
    vec_rows = sb("vec_rows", [P, 2, P])
    vec = sb("vec", [P, N_VEC])
    bmod = sb("bmod", [P, N_BMOD])
    c_rows = sb("c_rows", [2 * DT, P])
    silu_c = sb("silu_c", [P, DT, 2])
    mod = sb("mod", [P, 6, DT, 2])
    scale_1 = sb("scale_1", [P, DT, 2])
    scale_2 = sb("scale_2", [P, DT, 2])
    mu_self = sb("mu_self", [P, Z_TILES])
    ka_rest = sb("ka_rest", [P, PAIRS])
    g_head = sb("g_head", [QK, 2])
    w2_sb = sb("w2_sb", [P, WIDTH])
    a2_sb = sb("a2_sb", [P, WIDTH])
    g2_sb = sb("g2_sb", [P, WIDTH])
    DEC = [sb(f"decay_{d}", [P, PAIRS]) for d in range(NDIR)]
    DEC_KEPT = [sb(f"decay_kept_{d}", [P, PAIRS]) for d in range(NDIR)]
    BANK = ctx.enter_context(nc.psum_tensor("BANK", [P, 8, 512], FP32))

    arena = (nc.sbuf_base + 63) // 64 * 64
    arena_n = (nc.sbuf_usable_end - arena) // 64 * 16

    def place(name, at, n, dtype=FP32):
        return nc.alloc_sbuf_tensor_at(name, [P, n], dtype, offset=arena + 4 * at)[:]

    def parts(name, at, tiles, n=TOK):
        return [place(f"{name}_{x}", at + i * tiles * n, tiles * n, FP32R).rearrange("p (k t) -> p k t", t=n)
                for i, x in enumerate(("high", "low"))]

    WORK0 = SLOTS * SLOT
    RING = place("RING", 0, SLOTS * SLOT).rearrange("p (s n) -> p s n", s=SLOTS)
    H0 = arena_n - 2 * DT * TOK
    W0 = H0 - 2 * CHUNKS * CHUNK_W
    WORK_N = arena_n - WORK0
    WORK = place("WORK", WORK0, WORK_N)
    HS = parts("H", H0, DT)
    WS2 = parts("W", W0, CHUNKS, CHUNK_W)

    def carve(mem, at, *shape):
        n = 1
        for s in shape:
            n *= s
        flat = mem[:, at:at + n]
        if len(shape) == 1:
            return flat
        names = "abcd"[:len(shape)]
        return flat.rearrange(f"p ({' '.join(names)}) -> p {' '.join(names)}",
                              **{k: s for k, s in zip(names[1:], shape[1:])})

    def v(name, i):
        at = VEC_AT[name][0] + i
        return vec[:, at:at + 1]

    slot_full = [ctx.enter_context(nc.semaphore(f"slot_full_{s}")) for s in range(SLOTS)]
    slot_used = sig("slot_used")
    ring = {"next": 0}

    class Loads:

        def __init__(self, sources):
            self.sources = sources
            self.first = ring["next"]
            self.sent = 0
            ring["next"] += len(sources)

        def start(self, sp, n):
            for i in range(self.sent, n):
                sp.dma_start(self.view(i), self.sources[i]).then_inc(slot_full[(self.first + i) % SLOTS], 16)
            self.sent = n

        def issue(self, sp, used=None, ahead=None):
            count = len(self.sources)
            self.start(sp, min(SLOTS, count))
            for i in range(SLOTS, count):
                sp.wait_ge(*used(i - SLOTS))
                self.start(sp, i + 1)
            if ahead:
                for i in range(min(SLOTS, len(ahead.sources))):
                    if count + i >= SLOTS:
                        sp.wait_ge(*used(count + i - SLOTS))
                    ahead.start(sp, i + 1)

        def view(self, i):
            src = self.sources[i]
            k, w = src.shape[1], src.shape[2]
            s = (self.first + i) % SLOTS
            return RING[:, s, 0:k * w].rearrange("p (k w) -> p k w", k=k)

        def arrived(self, pe, i):
            n = self.first + i
            pe.wait_ge(slot_full[n % SLOTS], 16 * (n // SLOTS + 1))
            return self.view(i)

    class Chunks:

        def __init__(self, sources, chunks, used):
            self.loads = Loads(sources)
            self.sources = sources
            self.chunks = chunks
            self.used = used

        def start(self, sp, n):
            self.loads.start(sp, n)

        def issue(self, sp, ahead=None):
            last = {load: c for c, (load, *_) in enumerate(self.chunks)}
            self.loads.issue(sp, lambda i: low_ready(last[i] + 1), ahead)

        def raw(self, c):
            load, k0, k, c0, w = self.chunks[c]
            return self.loads.view(load)[:, k0:k0 + k, c0:c0 + w]

        def part(self, x, c):
            _, _, k, _, w = self.chunks[c]
            return WS2[x][:, c % CHUNKS, 0:k * w].rearrange("p (k w) -> p k w", k=k)

        def high(self, act, c):
            if c >= len(self.chunks):
                return
            self.loads.arrived(act, self.chunks[c][0])
            if c >= CHUNKS:
                act.wait_ge(*self.used(c - CHUNKS))
            high_ready.mark(nc.scalar.activation(self.part(0, c), self.raw(c), ACT.Copy))

        def low(self, dve, c):
            if c >= len(self.chunks):
                return
            dve.wait_ge(*high_ready(c + 1))
            low_ready.mark(nc.vector.tensor_tensor(self.part(1, c), self.raw(c), self.part(0, c).bitcast(FP32), ALU.subtract))

        def arrived(self, pe, c):
            pe.wait_ge(*low_ready(c + 1))
            return self.part(0, c), self.part(1, c)

    def product3(out, w, x, start, stop):
        nc.tensor.matmul(out, w[0], x[0], start=start, stop=False)
        nc.tensor.matmul(out, w[0], x[1], start=False, stop=False)
        return nc.tensor.matmul(out, w[1], x[0], start=False, stop=stop)

    def k_tiles(dram, c0, c1):
        return dram[:, c0:c1].rearrange("(k p) n -> p k n", p=P)

    consts_in = ctx.enter_context(nc.semaphore("consts_in"))
    rows_in = ctx.enter_context(nc.semaphore("rows_in"))
    small_in = ctx.enter_context(nc.semaphore("small_in"))
    out_stored = ctx.enter_context(nc.semaphore("out_stored"))
    pe_sig, act_sig, dve_sig, pool_sig = sig("pe_step"), sig("act_step"), sig("dve_step"), sig("pool_step")
    rows_turned = sig("rows_turned")
    turned_out = sig("turned_out")
    squares = sig("squares")
    sums = sig("sums")
    inverse_rms = sig("inverse_rms")
    scaled = sig("scaled")
    h_ready = sig("h_ready")
    product = sig("product")
    evacuated = sig("evacuated")
    first_cut = sig("first_cut")
    gate_ready = sig("gate_ready")
    merged = sig("merged")
    high_ready = sig("weights_high")
    low_ready = sig("weights_low")
    h_saved = ctx.enter_context(nc.semaphore("h_saved"))
    h_back = ctx.enter_context(nc.semaphore("h_back"))
    dft_in = ctx.enter_context(nc.semaphore("dft_in"))
    H_DRAM = [nc.dram_tensor(f"h_{x}", [P, DT * TOK], FP32, kind="Internal").ap() for x in ("high", "low")]

    def stage():
        return nc.Block()

    waits_passed = {e: ctx.enter_context(nc.semaphore(f"waits_passed_{e}")) for e in ("pe", "dve", "pool")}

    def hold(eng, name="pe"):
        eng.sem_inc(waits_passed[name], 1)

    rows_loaded = {"n": 0}

    tokens_in = carve(WORK, 0, 4, D)
    with stage() as block:
        @block.sync
        def _(sp):
            sp.dma_start(tokens_in[:, 0:2], ins["ctx"][0].rearrange("(t p) d -> p t d", p=P)).then_inc(consts_in, 16)
            sp.dma_start(tokens_in[:, 2:4], ins["x"][0].rearrange("(t p) d -> p t d", p=P)).then_inc(consts_in, 16)
            sp.dma_start(ident[:], ins["ident"]).then_inc(consts_in, 16)
            sp.dma_start(head_ones[:], ins["head_ones"]).then_inc(consts_in, 16)
            sp.dma_start(eye_heads[:], ins["eye_heads"]).then_inc(consts_in, 16)
            sp.dma_start(rope[:], ins["rope"]).then_inc(consts_in, 16)
            sp.dma_start(masks[:].rearrange("p d m n -> p (d m n)"), ins["masks"]).then_inc(consts_in, 16)
            sp.dma_start(c_rows[0:DT, :], ins["c_ctx"].rearrange("(k p) -> k p", p=P)).then_inc(consts_in, 16)
            sp.dma_start(c_rows[DT:2 * DT, :], ins["c"][0].rearrange("(k p) -> k p", p=P)).then_inc(consts_in, 16)

        @block.gpsimd
        def _(pool):
            nc.gpsimd.memset(ones[:], 1.0)
            nc.gpsimd.memset(pick[:], 0.0)
            nc.gpsimd.memset(chunk_start[:], 1.0).then_inc(pool_sig.sem, 1)
            pool_sig.made += 1
            pool.wait_ge(*pool_sig(1))
            nc.gpsimd.memset(chunk_start[:].rearrange("p (c t) -> p c t", t=CHUNK)[:, :, 0:1], 0.0)
            nc.gpsimd.memset(pick[:, 2 * HEADS - 1:2 * HEADS], 1.0)

        @block.tensor
        def _(pe):
            pe.wait_ge(consts_in, 16 * 9)
            for k in range(DT):
                for t in range(4):
                    last = nc.tensor.transpose(BANK[:, k, t * P:(t + 1) * P], tokens_in[:, t, k * P:(k + 1) * P], ident[:])
                rows_turned.mark(last)
            pe.wait_ge(*turned_out(1))
            rows_turned.mark(nc.tensor.transpose(BANK[:, 0, 0:2 * DT], c_rows[:], ident[0:2 * DT, 0:2 * DT]))

        @block.vector
        def _(dve):
            for k in range(DT):
                dve.wait_ge(*rows_turned(k + 1))
                turned_out.mark(nc.vector.tensor_copy(X[:, k], BANK[:, k]))

        @block.scalar
        def _(act):
            act.wait_ge(*rows_turned(DT + 1))
            nc.scalar.activation(silu_c[:].rearrange("p k s -> p s k"),
                                 BANK[:, 0, 0:2 * DT].rearrange("p (s k) -> p s k", s=2), ACT.Silu)
    Signal.end_stage()

    GROUPS = N_BMOD // 4

    def modulation_weights(l):
        halves = [ins["w_mod"][l][a:a + D // 2] for a in (0, D // 2)]
        return Loads([k_tiles(half, c, c + 4 * P) for c in range(0, 6 * D, 4 * P) for half in halves])

    def modulation(l, loads, ahead):
        mod_rows = carve(WORK, 0, 4, 4 * P)
        n0 = rows_loaded["n"]
        rows_loaded["n"] += len(VEC_ROWS) + 1
        with stage() as block:
            @block.sync
            def _(sp):
                loads.issue(sp, lambda i: slot_used(i + 1), ahead)

            @block.gpsimd
            def _(pool):
                pool.dma_start(vec_rows[0:N_BMOD, 0, :], ins["b_mod"][l].rearrange("(k p) -> k p", p=P)).then_inc(rows_in, 16)
                for name, k in VEC_ROWS:
                    at = VEC_AT[name][0]
                    src = ins[name][l]
                    if len(src.shape) == 2:
                        src = src.rearrange("a b -> (a b)")
                    pool.dma_start(vec_rows[at:at + k, 1, :], src.rearrange("(k p) -> k p", p=P)).then_inc(rows_in, 16)
                pool.dma_start(w2_sb[:], ins["w2"][l].rearrange("d r c -> (d r) c")).then_inc(small_in, 16)
                pool.dma_start(a2_sb[:], ins["a2"][l].rearrange("d r c -> (d r) c")).then_inc(small_in, 16)
                pool.dma_start(g2_sb[:], ins["g2"][l]).then_inc(small_in, 16)
                pool.dma_start(g_head[:, 0:1], ins["g_qn"][l].rearrange("(a b) -> a b", b=1)).then_inc(small_in, 16)
                pool.dma_start(g_head[:, 1:2], ins["g_kn"][l].rearrange("(a b) -> a b", b=1)).then_inc(small_in, 16)
                pool.wait_ge(small_in, 16 * 5 * (l + 1))

            @block.tensor
            def _(pe):
                for g in range(GROUPS + 1):
                    if g < GROUPS:
                        if g >= 4:
                            pe.wait_ge(*evacuated(g - 3))
                        for half in range(2):
                            w = loads.arrived(pe, 2 * g + half)
                            for k in range(DT // 2):
                                last = nc.tensor.matmul(BANK[0:2, 4 + g % 4], silu_c[:, half * (DT // 2) + k], w[:, k],
                                                        start=(half + k == 0), stop=(half == 1 and k == DT // 2 - 1))
                            slot_used.mark(last)
                    if g >= 1:
                        pe.wait_ge(*evacuated(g))
                        for q in range(4):
                            m = 4 * (g - 1) + q
                            last = nc.tensor.transpose(BANK[:, 2, 2 * m:2 * m + 2], mod_rows[0:2, (g - 1) % 4, q * P:(q + 1) * P], ident[0:2, 0:2])
                        turned_out.mark(last)
                    if g == GROUPS // 2:
                        pe.wait_ge(rows_in, 16 * (n0 + len(VEC_ROWS) + 1))
                        rows_turned.mark(nc.tensor.transpose(BANK[:, 0, 0:N_BMOD], vec_rows[0:N_BMOD, 0, :], ident[0:N_BMOD, 0:N_BMOD]))
                        rows_turned.mark(nc.tensor.transpose(BANK[:, 1, 0:N_VEC], vec_rows[0:N_VEC, 1, :], ident[0:N_VEC, 0:N_VEC]))

            @block.scalar
            def _(act):
                for g in range(GROUPS):
                    act.wait_ge(*slot_used(2 * g + 2))
                    if g >= 4:
                        act.wait_ge(*turned_out(g - 3))
                    evacuated.mark(nc.scalar.activation(mod_rows[0:2, g % 4], BANK[0:2, 4 + g % 4], ACT.Copy))

            @block.vector
            def _(dve):
                dve.wait_ge(*rows_turned(1))
                dve_sig.mark(nc.vector.tensor_copy(bmod[:], BANK[:, 0, 0:N_BMOD]))
                dve.wait_ge(*rows_turned(2))
                dve_sig.mark(nc.vector.tensor_copy(vec[:], BANK[:, 1, 0:N_VEC]))
                dve.wait_ge(*dve_sig(2))
                mp, mn = VEC_AT["mu_prev"][0], VEC_AT["mu_next"][0]
                dve_sig.mark(nc.vector.tensor_tensor(mu_self[:], vec[:, mp:mp + Z_TILES], vec[:, mn:mn + Z_TILES], ALU.add))
                ka = VEC_AT["k_a"][0]
                dve_sig.mark(nc.vector.tensor_scalar(ka_rest[:], vec[:, ka:ka + PAIRS], -1.0, 1.0, ALU.mult, ALU.add))
                dve.wait_ge(*dve_sig(4))
                nc.vector.tensor_scalar(mu_self[:], mu_self[:], -1.0, 1.0, ALU.mult, ALU.add)
                dve.wait_ge(*turned_out(GROUPS))
                flat = mod[:].rearrange("p q k s -> p (q k) s")
                dve_sig.mark(nc.vector.tensor_tensor(flat, BANK[:, 2, 0:2 * N_BMOD].rearrange("p (m s) -> p m s", s=2),
                                                     bmod[:].unsqueeze(2).to_broadcast([P, N_BMOD, 2]), ALU.add))
                dve.wait_ge(*dve_sig(5))
                for which, dst, g in ((1, scale_1, "g_norm1"), (4, scale_2, "g_norm2")):
                    at = VEC_AT[g][0]
                    dve_sig.mark(nc.vector.tensor_scalar(dst[:], mod[:, which], 1.0, None, ALU.add))
                    dve.wait_ge(*dve_sig(6 if which == 1 else 7))
                    nc.vector.tensor_tensor(dst[:], dst[:], vec[:, at:at + DT].unsqueeze(2).to_broadcast([P, DT, 2]), ALU.mult)
        Signal.end_stage()

    def norm(scale, shift, t0, save=False):
        n = TOK - t0
        sq = carve(WORK, 0, DT, TOK)
        rms = carve(WORK, DT * TOK, TOK)
        segs = [s for s in range(2) if s * CTX >= t0]
        cells = [(k, s) for k in range(DT) for s in segs]
        with stage() as block:
            @block.scalar
            def _(act):
                for k in range(DT):
                    squares.mark(nc.scalar.activation(sq[:, k, t0:], X[:, k, t0:], ACT.Square))
                act.wait_ge(*dve_sig(2))
                inverse_rms.mark(nc.scalar.activation(rms[:, t0:], rms[:, t0:], ACT.Sqrt))
                for i, (k, s) in enumerate(cells):
                    a, b = s * CTX, (s + 1) * CTX
                    act.wait_ge(*scaled(i + 1))
                    gate_ready.mark(nc.scalar.activation(HS[0][:, k, a:b], sq[:, k, a:b], ACT.Identity, bias=shift[:, k, s:s + 1]))

            @block.tensor
            def _(pe):
                for k in range(DT):
                    pe.wait_ge(*squares(k + 1))
                    last = nc.tensor.matmul(BANK[:, 0, 0:n], ones[:], sq[:, k, t0:], start=(k == 0), stop=(k == DT - 1))
                sums.mark(last)

            @block.vector
            def _(dve):
                dve.wait_ge(*sums(1))
                dve_sig.mark(nc.vector.tensor_scalar(rms[:, t0:], BANK[:, 0, 0:n], 1.0 / D, RMS_EPS, ALU.mult, ALU.add))
                dve.wait_ge(*dve_sig(1))
                dve_sig.mark(nc.vector.reciprocal(rms[:, t0:], rms[:, t0:]))
                dve.wait_ge(*inverse_rms(1))
                LAG = 3
                for i in range(len(cells) + LAG):
                    if i < len(cells):
                        k, s = cells[i]
                        a, b = s * CTX, (s + 1) * CTX
                        scaled.mark(nc.vector.scalar_tensor_tensor(sq[:, k, a:b], X[:, k, a:b], scale[:, k, s:s + 1],
                                                                   rms[:, a:b], ALU.mult, ALU.mult))
                    if i >= LAG:
                        k, s = cells[i - LAG]
                        a, b = s * CTX, (s + 1) * CTX
                        dve.wait_ge(*gate_ready(i - LAG + 1))
                        h_ready.mark(nc.vector.scalar_tensor_tensor(HS[1][:, k, a:b], sq[:, k, a:b], shift[:, k, s:s + 1],
                                                                    HS[0][:, k, a:b].bitcast(FP32), ALU.add, ALU.subtract))

            @block.sync
            def _(sp):
                if save:
                    sp.wait_ge(*h_ready(len(cells)))
                    for x in range(2):
                        sp.dma_start(H_DRAM[x], HS[x].bitcast(FP32).rearrange("p k t -> p (k t)")).then_inc(h_saved, 16)
        Signal.end_stage()

    Z = carve(WORK, 0, Z_TILES, TOK)

    def rwkv_weights(l):
        return Chunks([k_tiles(ins["w_in"][l], c, min(c + 2 * P, N_RWKV_IN)) for c in range(0, N_RWKV_IN, 2 * P)],
                      [(m // 2, 0, DT, (m % 2) * P, P) for m in range(Z_TILES)], lambda c: product(c + 1))

    def project_rwkv(l, w):
        with stage() as block:
            @block.sync
            def _(sp):
                w.issue(sp)
                sp.wait_ge(h_saved, 32 * (l + 1))

            @block.tensor
            def _(pe):
                for m in range(Z_TILES):
                    wm = w.arrived(pe, m)
                    if m >= 4:
                        pe.wait_ge(*evacuated(m - 3))
                    for k in range(DT):
                        last = product3(BANK[:, m % 4], [x[:, k] for x in wm], [x[:, k] for x in HS], k == 0, k == DT - 1)
                    product.mark(last)

            @block.scalar
            def _(act):
                for c in range(CHUNKS):
                    w.high(act, c)
                for m in range(Z_TILES):
                    act.wait_ge(*product(m + 1))
                    first_cut.mark(nc.scalar.activation(Z[:, m], BANK[:, m % 4], ACT.Copy, scale=mu_self[:, m:m + 1]))
                    w.high(act, m + CHUNKS)

            @block.vector
            def _(dve):
                for c in range(CHUNKS):
                    w.low(dve, c)
                for m in range(Z_TILES):
                    z = Z[:, m].rearrange("p (s t) -> p s t", s=2)
                    raw = BANK[:, m % 4].rearrange("p (s t) -> p s t", s=2)
                    dve.wait_ge(*first_cut(m + 1))
                    dve_sig.mark(nc.vector.scalar_tensor_tensor(z[:, :, 1:], raw[:, :, :SEQ - 1], v("mu_prev", m), z[:, :, 1:],
                                                                ALU.mult, ALU.add))
                    dve.wait_ge(*dve_sig(m + 1))
                    evacuated.mark(nc.vector.scalar_tensor_tensor(z[:, :, :SEQ - 1], raw[:, :, 1:], v("mu_next", m),
                                                                  z[:, :, :SEQ - 1], ALU.mult, ALU.add))
                    w.low(dve, m + CHUNKS)
        Signal.end_stage()

    F0 = Z_TILES * TOK
    KK = carve(WORK, F0, PAIRS, TOK)
    KD = [carve(WORK, F0 + (1 + d) * WIDTH * 4, PAIRS, TOK) for d in range(NDIR)]
    BB = [carve(WORK, F0 + (3 + d) * WIDTH * 4, PAIRS, TOK) for d in range(NDIR)]
    INCL = [carve(WORK, F0 + (5 + d) * WIDTH * 4, PAIRS, TOK) for d in range(NDIR)]
    EXCL = [carve(WORK, F0 + (7 + d) * WIDTH * 4, PAIRS, TOK) for d in range(NDIR)]
    WORK_USED = F0 + 9 * WIDTH * 4
    Y = carve(WORK, Z_K * TOK, PAIRS, TOK)

    r_flat = RING.rearrange("p s n -> p (s n)")

    def features():
        sqk = carve(r_flat, 0, PAIRS, TOK)
        inv = carve(r_flat, PAIRS * TOK, PAIRS, TOK)
        with stage() as block:
            @block.scalar
            def _(act):
                act_sig.mark(nc.scalar.activation(Z[:, Z_W], Z[:, Z_W], ACT.Tanh))
                act_sig.mark(nc.scalar.activation(Z[:, Z_G], Z[:, Z_G], ACT.Sigmoid))
                n = 0
                for d in range(NDIR):
                    for j in range(PAIRS):
                        n += 1
                        act.wait_ge(*product(n))
                        gate_ready.mark(nc.scalar.activation(EXCL[d][:, j], BANK[:, n % 4], ACT.Sigmoid, bias=v("w0", d * PAIRS + j)))
                for d in range(NDIR):
                    for j in range(PAIRS):
                        n += 1
                        act.wait_ge(*product(n))
                        gate_ready.mark(nc.scalar.activation(BB[d][:, j], BANK[:, n % 4], ACT.Sigmoid, bias=v("a0", d * PAIRS + j)))
                for j in range(PAIRS):
                    act.wait_ge(*scaled(j + 1))
                    squares.mark(nc.scalar.activation(sqk[:, j], KK[:, j], ACT.Square))
                for j in range(PAIRS):
                    act.wait_ge(*sums(j + 1))
                    evacuated.mark(nc.scalar.activation(inv[:, j], BANK[:, 4 + j], ACT.Sqrt))

            @block.tensor
            def _(pe):
                n = 0
                for w, z in ((w2_sb, Z_W), (a2_sb, Z_A)):
                    for d in range(NDIR):
                        for j in range(PAIRS):
                            n += 1
                            if n == 1:
                                pe.wait_ge(*act_sig(1))
                            if n > 4:
                                pe.wait_ge(*gate_ready(n - 4))
                            product.mark(nc.tensor.matmul(BANK[:, n % 4], w[d * 64:(d + 1) * 64, j * P:(j + 1) * P],
                                                          Z[d * 64:(d + 1) * 64, z], start=True, stop=True))
                for j in range(PAIRS):
                    pe.wait_ge(*squares(j + 1))
                    sums.mark(nc.tensor.matmul(BANK[:, 4 + j], head_ones[:], sqk[:, j], start=True, stop=True))

            @block.vector
            def _(dve):
                c = 0
                for j in range(PAIRS):
                    scaled.mark(nc.vector.tensor_scalar(KK[:, j], Z[:, Z_K + j], v("k_k", j), None, ALU.mult))
                for d in range(NDIR):
                    for j in range(PAIRS):
                        dve.wait_ge(*gate_ready(d * PAIRS + j + 1))
                        c += 1
                        dve_sig.mark(nc.vector.tensor_tensor_scan(INCL[d][:, j], chunk_start[:], EXCL[d][:, j], 0.0, ALU.mult, ALU.add))
                    dve.wait_ge(*dve_sig(c))
                    nc.vector.tensor_tensor(EXCL[d], INCL[d], EXCL[d], ALU.subtract)
                for d in range(NDIR):
                    for j in range(PAIRS):
                        dve.wait_ge(*gate_ready((NDIR + d) * PAIRS + j + 1))
                        c += 1
                        dve_sig.mark(nc.vector.tensor_scalar(KD[d][:, j], BB[d][:, j], v("k_a", j), ka_rest[:, j:j + 1], ALU.mult, ALU.add))
                    dve.wait_ge(*dve_sig(c))
                    nc.vector.tensor_tensor(KD[d], KD[d], Z[:, Z_K:Z_K + PAIRS], ALU.mult)
                for j in range(PAIRS):
                    dve.wait_ge(*evacuated(j + 1))
                    c += 1
                    dve_sig.mark(nc.vector.tensor_scalar(inv[:, j], inv[:, j], 1e-12, None, ALU.max))
                dve.wait_ge(*dve_sig(c))
                c += 1
                dve_sig.mark(nc.vector.reciprocal(inv, inv))
                dve.wait_ge(*dve_sig(c))
                c += 1
                dve_sig.mark(nc.vector.tensor_tensor(KK, KK, inv, ALU.mult))
                dve.wait_ge(*dve_sig(c))
                for d in range(NDIR):
                    nc.vector.tensor_tensor(BB[d], BB[d], KK, ALU.mult)
                nc.vector.memset(Y, 0.0)
        Signal.end_stage()

    HALF = PAIRS * HD
    free = [(r_flat, 0, SLOTS * SLOT), (WORK, Z_W * TOK, Z_G * TOK), (WORK, WORK_USED, WORK_N)]

    def scratch(*shape):
        n = 1
        for s in shape:
            n *= s
        for i, (mem, at, end) in enumerate(free):
            if at + n <= end:
                free[i] = (mem, at + n, end)
                return carve(mem, at, *shape)
        raise ValueError(f"no room for {shape}: {[(a, e) for _, a, e in free]}")

    QR = [scratch(PAIRS, 2, HD) for _ in range(NDIR)]
    QR2 = [scratch(PAIRS, 2, HD) for _ in range(NDIR)]
    GA = [scratch(PAIRS, 2, HD) for _ in range(NDIR)]
    T2 = [scratch(2, PAIRS, HD) for _ in range(NDIR)]
    BK = [scratch(2, PAIRS, HD) for _ in range(NDIR)]
    BK_TOK = [scratch(2, PAIRS, HD) for _ in range(NDIR)]
    VF = [scratch(PAIRS, HD) for _ in range(NDIR)]
    V_TOK = [scratch(PAIRS, HD) for _ in range(NDIR)]
    EXPO = scratch(2, PAIRS, HD)
    EXPS = [scratch(3, PAIRS, HD) for _ in range(NDIR)]
    LTS = [scratch(PAIRS, HD) for _ in range(NDIR)]
    LM = [scratch(PAIRS, HD) for _ in range(NDIR)]
    ARB = [scratch(PAIRS, HD) for _ in range(NDIR)]
    X1 = [scratch(PAIRS, HD) for _ in range(NDIR)]
    WS = [scratch(PAIRS, HD) for _ in range(NDIR)]
    SA = [scratch(PAIRS, HD) for _ in range(NDIR)]
    ST = [scratch(PAIRS, HD) for _ in range(NDIR)]
    SD = [scratch(PAIRS, HD) for _ in range(NDIR)]

    s_expo = sig("exponents_ready")
    s_exp = sig("exps_ready")
    s_exp_used = [sig(f"exps_used_{i}") for i in range(2)]
    s_qr = [sig(f"qr_ready_{d}") for d in range(NDIR)]
    s_ops = [sig(f"operands_ready_{d}") for d in range(NDIR)]
    s_qr2 = [sig(f"qr_kept_{d}") for d in range(NDIR)]
    s_gram = [sig(f"gram_{d}") for d in range(NDIR)]
    s_lts = [sig(f"lt_kept_{d}") for d in range(NDIR)]
    s_gram_out = [sig(f"gram_out_{d}") for d in range(NDIR)]
    s_bk_tok = [sig(f"bk_token_major_{d}") for d in range(NDIR)]
    s_v = [sig(f"values_kept_{d}") for d in range(NDIR)]
    s_v_tok = [sig(f"v_token_major_{d}") for d in range(NDIR)]
    s_lm = [sig(f"level_mask_{d}") for d in range(NDIR)]
    s_x1 = [sig(f"x1_product_{d}") for d in range(NDIR)]
    s_x1_out = [sig(f"x1_out_{d}") for d in range(NDIR)]
    s_tx = [sig(f"merge_product_{d}") for d in range(NDIR)]
    s_t = [sig(f"inverse_merged_{d}") for d in range(NDIR)]
    s_w = [sig(f"w_product_{d}") for d in range(NDIR)]
    s_w_out = [sig(f"w_out_{d}") for d in range(NDIR)]
    s_sa = [sig(f"sa_product_{d}") for d in range(NDIR)]
    s_sa_out = [sig(f"sa_out_{d}") for d in range(NDIR)]
    s_y = [sig(f"y_product_{d}") for d in range(NDIR)]
    s_ds = [sig(f"state_product_{d}") for d in range(NDIR)]
    s_y_out = [sig(f"y_added_{d}") for d in range(NDIR)]
    s_sd = [sig(f"state_decayed_{d}") for d in range(NDIR)]
    s_st = [sig(f"state_new_{d}") for d in range(NDIR)]
    s_init = sig("state_cleared")
    s_first = [sig(f"first_level_{d}") for d in range(NDIR)]

    scan_signals = [s_expo, s_exp, s_init, *s_qr, *s_ops, *s_qr2, *s_gram, *s_lts, *s_gram_out, *s_bk_tok, *s_v, *s_v_tok, *s_lm, *s_x1, *s_x1_out,
                    *s_tx, *s_t, *s_w, *s_w_out, *s_sa, *s_sa_out, *s_y, *s_ds, *s_y_out, *s_sd, *s_st, *s_first]
    with stage() as block:
        @block.sync
        def _(sp):
            for s in scan_signals:
                sp.sem_inc(s.sem, 1)
                s.made += 1
    Signal.end_stage()

    NL = LEVELS - 1
    N = SEG_CHUNKS

    def lanes(mask):
        return mask.unsqueeze(1).to_broadcast([P, PAIRS, HD])

    STEPS = 2 * N

    def chunk_of(d, i):
        return CHUNK * i if d == 0 else (CHUNK * (N - 1) + (TOK - CHUNK) * i) % TOK

    def scan(context_y):
        y0 = 0 if context_y else N

        def tokens(eng, d, i):
            t = chunk_of(d, i)
            return t if isinstance(i, int) else eng.snap(t, min_val=0, max_val=TOK - CHUNK)

        def run(eng, step):
            for first, end, need_y in ((0, N, context_y), (N, STEPS - 1, True)):
                Signal.trips = end - first
                with eng.Fori(first, end) as i:
                    step(i, need_y, True)
                Signal.trips = 1
            step(STEPS - 1, True, False)

        def level_mask(d, l):
            return masks[:, d, 1 + l]

        def at_step(s, i, k=1, n=0):
            return s.sem, s.base + k * i + n

        first_half = lambda d: slice(HD // 2 * d, HD // 2 * (d + 1))
        later_half = lambda d: first_half(1 - d)

        def of_head(h, half):
            return slice(h * HD + half.start, h * HD + half.stop)

        B_L, B_LT, B_G, B_S = 0, 1, 2, 3
        pairs = lambda bank, a: BANK[:, bank, a:a + HALF].rearrange("p (j t) -> p j t", j=PAIRS)
        with stage() as block:
            @block.gpsimd
            def _(pool):
                def operands(i, t, d):
                    pool.wait_ge(*at_step(s_gram[d], i, 3))
                    pool.wait_ge(*at_step(s_bk_tok[d], i))
                    pool.wait_ge(*at_step(s_exp, i, 2, d + 1))
                    hold(pool, "pool")
                    s_ops[d].mark(nc.gpsimd.tensor_tensor(BK[d][:, 1], KD[d][:, :, bass.ds(t, CHUNK)], EXPS[d][:, 2], ALU.mult))

                def step(i, need_y, more):
                    t = [tokens(pool, d, i + 1) for d in range(NDIR)] if more else None
                    for d in range(NDIR):
                        pool.wait_ge(*at_step(s_st[d], i))
                        pool.wait_ge(*at_step(s_exp, i, 2, d + 1))
                        hold(pool, "pool")
                        nc.gpsimd.tensor_copy(DEC_KEPT[d][:], DEC[d][:])
                        s_sd[d].mark(nc.gpsimd.tensor_tensor(SD[d], ST[d], DEC[d][:].unsqueeze(2).to_broadcast([P, PAIRS, HD]), ALU.mult))
                    for l in range(1, LEVELS):
                        for d in range(NDIR):
                            if l == 1:
                                pool.wait_ge(*at_step(s_lts[d], i, 1, 1))
                            pool.wait_ge(*at_step(s_x1[d], i, NL, l - 1))
                            s_lm[d].mark(nc.gpsimd.tensor_tensor(LM[d], LTS[d], lanes(level_mask(d, l)), ALU.mult))
                        if more and l in (3, 5):
                            d = (l - 3) // 2
                            operands(i + 1, t[d], d)

                pool.wait_ge(*s_init(1))
                for d in range(NDIR):
                    operands(0, chunk_of(d, 0), d)
                run(pool, step)

            @block.scalar
            def _(act):
                def exps(i, t, d):
                    if d == 1:
                        act.wait_ge(*at_step(s_expo, i, 1, 1))
                    act.wait_ge(*at_step(s_ops[d], i))
                    act.wait_ge(*at_step(s_qr[d], i))
                    at = bass.ds(t, CHUNK)
                    e = EXPS[d]
                    excl = EXCL[0][:, :, at] if d == 0 else EXPO[:, 1]
                    incl = INCL[0][:, :, at] if d == 0 else EXPO[:, 0]
                    nc.scalar.activation(e[:, 0], excl, ACT.Exp, scale=-KAPPA)
                    nc.scalar.activation(e[:, 1], incl, ACT.Exp, scale=-KAPPA)
                    nc.scalar.activation(e[:, 2], incl, ACT.Exp, scale=KAPPA)
                    act.wait_ge(*at_step(s_sd[d], i))
                    s_exp.mark(nc.scalar.activation(DEC[d][:].unsqueeze(2), INCL[d][:, :, bass.ds(t + (CHUNK - 1), 1)],
                                                    ACT.Exp, scale=-KAPPA))

                def step(i, need_y, more):
                    here = [tokens(act, d, i) for d in range(NDIR)]
                    t = [tokens(act, d, i + 1) for d in range(NDIR)] if more else None
                    for d in range(NDIR):
                        act.wait_ge(*at_step(s_gram[d], i, 3, 1))
                        act.wait_ge(*at_step(s_lm[d], i, NL))
                        s_lts[d].mark(nc.scalar.activation(LTS[d], BANK[:, 4 * d + B_LT].rearrange("p (j q t) -> p j q t", j=PAIRS, q=2)[:, :, 0], ACT.Copy))
                    for d in range(NDIR):
                        act.wait_ge(*at_step(s_v_tok[d], i))
                        s_v[d].mark(nc.scalar.activation(VF[d], Z[:, Z_V:Z_V + PAIRS, bass.ds(here[d], CHUNK)], ACT.Copy))
                    for l in range(1, LEVELS):
                        for d in range(NDIR):
                            act.wait_ge(*at_step(s_x1[d], i, NL, l))
                            cols = slice(0, HD) if l < NL else first_half(d)
                            s_x1_out[d].mark(nc.scalar.activation(X1[d][:, :, cols], pairs(4 * d + B_L, 0)[:, :, cols], ACT.Copy))
                        if more and l in (2, 4):
                            exps(i + 1, t[l // 2 - 1], l // 2 - 1)
                    for d in range(NDIR):
                        act.wait_ge(*at_step(s_w[d], i, 1, 1))
                        s_w_out[d].mark(nc.scalar.activation(WS[d], pairs(4 * d + B_L, 0), ACT.Copy))
                    for d in range(NDIR):
                        act.wait_ge(*at_step(s_sa[d], i, 1, 1))
                        s_sa_out[d].mark(nc.scalar.activation(SA[d], pairs(4 * d + B_LT, 0), ACT.Copy, scale=-1.0))

                for d in range(NDIR):
                    exps(0, chunk_of(d, 0), d)
                run(act, step)

            @block.vector
            def _(dve):
                def exponents(i, t):
                    at = bass.ds(t, CHUNK)
                    whole = INCL[1][:, :, bass.ds(t + (CHUNK - 1), 1)].to_broadcast([P, PAIRS, CHUNK])
                    dve.wait_ge(*at_step(s_exp, i, 2))
                    hold(dve, "dve")
                    nc.vector.tensor_tensor(EXPO[:, 0], whole, EXCL[1][:, :, at], ALU.subtract)
                    s_expo.mark(nc.vector.tensor_tensor(EXPO[:, 1], whole, INCL[1][:, :, at], ALU.subtract))

                def turn(dst, src):
                    B = HD // 2
                    for h in range(2):
                        for f in range(2):
                            for k in range(2):
                                last = nc.vector.transpose(dst[h * HD + k * B:h * HD + (k + 1) * B, :, f * B:(f + 1) * B],
                                                           src(k * B, B)[h * HD + f * B:h * HD + (f + 1) * B])
                    return last

                def turn_bk(i, d):
                    dve.wait_ge(*at_step(s_ops[d], i, 1, 1))
                    dve.wait_ge(*at_step(s_qr[d], i, 1, 1))
                    dve.wait_ge(*at_step(s_ds[d], i))
                    both = BK[d].rearrange("p q j t -> p (q j) t")
                    s_bk_tok[d].mark(turn(BK_TOK[d].rearrange("p q j t -> p (q j) t"), lambda a, n: both[:, :, a:a + n]))

                def turn_v(i, d):
                    dve.wait_ge(*at_step(s_v[d], i, 1, 1))
                    dve.wait_ge(*at_step(s_ds[d], i))
                    s_v_tok[d].mark(turn(V_TOK[d], lambda a, n: VF[d][:, :, a:a + n]))

                def operands(i, t, d):
                    at = bass.ds(t, CHUNK)
                    e = EXPS[d]
                    dve.wait_ge(*at_step(s_exp, i, 2, d + 1))
                    dve.wait_ge(*at_step(s_gram[d], i, 3))
                    dve.wait_ge(*at_step(s_bk_tok[d], i))
                    hold(dve, "dve")
                    nc.vector.tensor_tensor(BK[d][:, 0], BB[d][:, :, at], e[:, 2], ALU.mult)
                    nc.vector.tensor_tensor(QR[d][:, :, 0], KK[:, :, at], e[:, 0], ALU.mult)
                    s_qr[d].mark(nc.vector.tensor_tensor(QR[d][:, :, 1], Z[:, Z_R:Z_R + PAIRS, at], e[:, 1], ALU.mult))

                def keep(i, d):
                    dve.wait_ge(*at_step(s_ds[d], i))
                    dve.wait_ge(*at_step(s_qr[d], i, 1, 1))
                    s_qr2[d].mark(nc.vector.tensor_copy(QR2[d], QR[d]))

                def step(i, need_y, more):
                    here = [tokens(dve, d, i) for d in range(NDIR)] if need_y else None
                    t = [tokens(dve, d, i + 1) for d in range(NDIR)] if more else None
                    for d in range(NDIR):
                        lt = BANK[:, 4 * d + B_LT].rearrange("p (j q t) -> p j q t", j=PAIRS, q=2)
                        dve.wait_ge(*at_step(s_lts[d], i, 1, 1))
                        nc.vector.tensor_tensor(ARB[d], lt[:, :, 1], lanes(masks[:, d, LEVELS + 2]), ALU.mult)
                        dve.wait_ge(*at_step(s_gram[d], i, 3, 2))
                        nc.vector.tensor_tensor(T2[d][:, 0], pairs(4 * d + B_L, 0), lanes(masks[:, d, 0]), ALU.mult)
                        s_first[d].mark(nc.vector.tensor_tensor(T2[d][:, 1], LTS[d], lanes(masks[:, d, 1]), ALU.mult))
                        dve.wait_ge(*at_step(s_first[d], i, 1, 1))
                        s_t[d].mark(nc.vector.tensor_tensor(T2[d].rearrange("p q j t -> p (q j) t"), T2[d].rearrange("p q j t -> p (q j) t"),
                                                            eye_heads[:].unsqueeze(1).to_broadcast([P, 2 * PAIRS, HD]), ALU.add))
                        dve.wait_ge(*at_step(s_gram[d], i, 3, 3))
                        s_gram_out[d].mark(nc.vector.tensor_tensor(
                            GA[d].rearrange("p j q t -> p j (q t)"),
                            BANK[:, 4 * d + B_G].rearrange("p (j n) -> p j n", j=PAIRS),
                            masks[:, d, LEVELS + 1:LEVELS + 3].rearrange("p q t -> p (q t)").unsqueeze(1).to_broadcast([P, PAIRS, 2 * HD]),
                            ALU.mult))
                    for l in range(1, LEVELS):
                        for d in range(NDIR):
                            dve.wait_ge(*at_step(s_tx[d], i, NL, l))
                            dve.wait_ge(*at_step(s_t[d], i, LEVELS, l))
                            if l < LEVELS - 1:
                                s_t[d].mark(nc.vector.tensor_tensor(T2[d].rearrange("p q j t -> p (q j t)"), T2[d].rearrange("p q j t -> p (q j t)"),
                                                                    BANK[:, 4 * d + B_LT], ALU.subtract))
                            else:
                                for h in range(2):
                                    rows, cols = of_head(h, first_half(d)), later_half(d)
                                    last = nc.vector.tensor_tensor(T2[d][rows, 1, :, cols], T2[d][rows, 1, :, cols],
                                                                   pairs(4 * d + B_LT, HALF)[rows, :, cols], ALU.subtract)
                                s_t[d].mark(last)
                        if l in (1, 2):
                            turn_bk(i, l - 1)
                        if l in (3, 4):
                            turn_v(i, l - 3)
                        if more and l == 3:
                            operands(i + 1, t[0], 0)
                            exponents(i + 1, t[1])
                        if more and l == 5:
                            operands(i + 1, t[1], 1)
                    if need_y:
                        for d in range(NDIR):
                            at = bass.ds(here[d], CHUNK)
                            dve.wait_ge(*at_step(s_y[d], i - y0, 1, 1))
                            dve.wait_ge(*at_step(s_y_out[1 - d], i - y0, 1, d))
                            hold(dve, "dve")
                            s_y_out[d].mark(nc.vector.tensor_tensor(Y[:, :, at], Y[:, :, at], pairs(4 * d + B_G, 0), ALU.add))
                    for d in range(NDIR):
                        dve.wait_ge(*at_step(s_sd[d], i, 1, 1))
                        dve.wait_ge(*at_step(s_ds[d], i, 1, 1))
                        for j in range(PAIRS):
                            last = nc.vector.scalar_tensor_tensor(ST[d][:, j], BANK[:, 4 * d + B_S, j * HD:(j + 1) * HD], DEC_KEPT[d][:, j:j + 1],
                                                                  SD[d][:, j], ALU.mult, ALU.add)
                        s_st[d].mark(last)
                        if more:
                            keep(i + 1, d)

                nc.vector.memset(ST[0], 0.0)
                s_init.mark(nc.vector.memset(ST[1], 0.0))
                exponents(0, chunk_of(1, 0))
                for d in range(NDIR):
                    operands(0, chunk_of(d, 0), d)
                    keep(0, d)
                run(dve, step)

            @block.tensor
            def _(pe):
                def each(bank, at, width, *terms):
                    for j in range(PAIRS):
                        for h in range(2):
                            rows = slice(h * HD, (h + 1) * HD)
                            for n, (lhs, rhs) in enumerate(terms):
                                last = nc.tensor.matmul(BANK[rows, bank, at + j * width:at + (j + 1) * width],
                                                        lhs(j)[rows], rhs(j)[rows], start=(n == 0), stop=(n == len(terms) - 1))
                    return last

                def halves(bank, at, out_rows, out_cols, lhs, rhs, k_rows):
                    for j in range(PAIRS):
                        for h in range(2):
                            k = of_head(h, k_rows)
                            last = nc.tensor.matmul(BANK[of_head(h, out_rows), bank, at + j * HD + out_cols.start:at + j * HD + out_cols.stop],
                                                    lhs[k, j, out_rows], rhs[k, j, out_cols], start=True, stop=True)
                    return last

                def step(i, need_y, more):
                    for d in range(NDIR):
                        bank = 4 * d
                        q = lambda j: QR[d][:, j, 0]
                        qr = lambda j: QR[d][:, j].rearrange("p q t -> p (q t)")
                        pe.wait_ge(*at_step(s_qr[d], i, 1, 1))
                        pe.wait_ge(*at_step(s_sa_out[d], i))
                        hold(pe)
                        s_gram[d].mark(each(bank + B_LT, 0, 2 * HD, (lambda j: BK[d][:, 0, j], qr)))
                        s_gram[d].mark(each(bank + B_L, 0, HD, (q, lambda j: BK[d][:, 0, j])))
                        pe.wait_ge(*at_step(s_ops[d], i, 1, 1))
                        if need_y:
                            pe.wait_ge(*at_step(s_y_out[d], i - y0))
                        hold(pe)
                        s_gram[d].mark(each(bank + B_G, 0, 2 * HD, (lambda j: BK[d][:, 1, j], qr)))
                    for l in range(1, LEVELS):
                        for d in range(NDIR):
                            pe.wait_ge(*at_step(s_t[d], i, LEVELS, l))
                            pe.wait_ge(*at_step(s_lm[d], i, NL, l))
                            hold(pe)
                            if l < NL:
                                s_x1[d].mark(each(4 * d + B_L, 0, HD, (lambda j: LM[d][:, j], lambda j: T2[d][:, 0, j])))
                            else:
                                s_x1[d].mark(halves(4 * d + B_L, 0, later_half(d), first_half(d), LM[d], T2[d][:, 0], first_half(d)))
                        for d in range(NDIR):
                            pe.wait_ge(*at_step(s_x1_out[d], i, NL, l))
                            hold(pe)
                            if l < NL:
                                each(4 * d + B_LT, 0, HD, (lambda j: T2[d][:, 1, j], lambda j: X1[d][:, j]))
                                s_tx[d].mark(each(4 * d + B_LT, HALF, HD, (lambda j: X1[d][:, j], lambda j: T2[d][:, 1, j])))
                            else:
                                s_tx[d].mark(halves(4 * d + B_LT, HALF, first_half(d), later_half(d), X1[d], T2[d][:, 1], later_half(d)))
                    for d in range(NDIR):
                        pe.wait_ge(*at_step(s_gram_out[d], i, 1, 1))
                        pe.wait_ge(*at_step(s_qr2[d], i, 1, 1))
                        pe.wait_ge(*at_step(s_v_tok[d], i, 1, 1))
                        pe.wait_ge(*at_step(s_st[d], i))
                        hold(pe)
                        s_w[d].mark(each(4 * d + B_L, 0, HD, (lambda j: QR2[d][:, j, 0], lambda j: ST[d][:, j]),
                                         (lambda j: GA[d][:, j, 0], lambda j: V_TOK[d][:, j])))
                    for d in range(NDIR):
                        pe.wait_ge(*at_step(s_w_out[d], i, 1, 1))
                        pe.wait_ge(*at_step(s_t[d], i, LEVELS, LEVELS))
                        hold(pe)
                        s_sa[d].mark(each(4 * d + B_LT, 0, HD, (lambda j: T2[d][:, 1, j], lambda j: WS[d][:, j])))
                    for d in range(NDIR):
                        pe.wait_ge(*at_step(s_sa_out[d], i, 1, 1))
                        pe.wait_ge(*at_step(s_bk_tok[d], i, 1, 1))
                        hold(pe)
                        if need_y:
                            s_y[d].mark(each(4 * d + B_G, 0, HD, (lambda j: ST[d][:, j], lambda j: QR2[d][:, j, 1]),
                                             (lambda j: SA[d][:, j], lambda j: ARB[d][:, j]),
                                             (lambda j: V_TOK[d][:, j], lambda j: GA[d][:, j, 1])))
                        s_ds[d].mark(each(4 * d + B_S, 0, HD, (lambda j: BK_TOK[d][:, 0, j], lambda j: SA[d][:, j]),
                                          (lambda j: BK_TOK[d][:, 1, j], lambda j: V_TOK[d][:, j])))

                pe.wait_ge(*s_init(1))
                run(pe, step)
        Signal.end_stage()

    TILES = PAIRS * TOK
    OR0 = WORK0 + F0 + 3 * TILES + TOK * 2
    O_R = parts("o_rwkv", OR0, PAIRS)

    def rwkv_output(l, t0, ahead):
        n = TOK - t0
        A1 = carve(WORK, F0 + 6 * WIDTH * 4, PAIRS, TOK)
        A2 = carve(WORK, F0 + 7 * WIDTH * 4, PAIRS, TOK)
        A3 = carve(WORK, F0 + 8 * WIDTH * 4, PAIRS, TOK)
        A4 = carve(WORK, WORK_USED, PAIRS, TOK)
        with stage() as block:
            @block.sync
            def _(sp):
                ahead.start(sp, SLOTS)
                for x in range(2):
                    sp.dma_start(HS[x].bitcast(FP32).rearrange("p k t -> p (k t)"), H_DRAM[x]).then_inc(h_back, 16)
                sp.wait_ge(h_back, 32 * (l + 1))

            @block.tensor
            def _(pe):
                for j in range(PAIRS):
                    sums.mark(nc.tensor.matmul(BANK[:, j, 0:n], head_ones[:], Y[:, j, t0:], start=True, stop=True))
                for j in range(PAIRS):
                    pe.wait_ge(*scaled(j + 1))
                    product.mark(nc.tensor.matmul(BANK[:, 4 + j, 0:n], head_ones[:], A1[:, j, t0:], start=True, stop=True))
                for j in range(PAIRS):
                    pe.wait_ge(*squares(j + 1))
                    pe.wait_ge(*dve_sig(3 * j + 3))
                    sums.mark(nc.tensor.matmul(BANK[:, j, 0:n], head_ones[:], A2[:, j, t0:], start=True, stop=True))
                for j in range(PAIRS):
                    pe.wait_ge(*evacuated(j + 1))
                    product.mark(nc.tensor.matmul(BANK[:, 4 + j, 0:n], g2_sb[:, j * P:(j + 1) * P], Z[:, Z_G, t0:], start=True, stop=True))

            @block.scalar
            def _(act):
                for j in range(PAIRS):
                    act.wait_ge(*dve_sig(3 * j + 3))
                    squares.mark(nc.scalar.activation(A2[:, j, t0:], Y[:, j, t0:], ACT.Square))
                for j in range(PAIRS):
                    act.wait_ge(*merged(j + 1))
                    inverse_rms.mark(nc.scalar.activation(A2[:, j, t0:], A2[:, j, t0:], ACT.Sqrt))
                for j in range(PAIRS):
                    act.wait_ge(*gate_ready(j + 1))
                    high_ready.mark(nc.scalar.activation(O_R[0][:, j, t0:], A4[:, j, t0:], ACT.Copy))

            @block.vector
            def _(dve):
                c = 0
                for j in range(PAIRS):
                    dve_sig.mark(nc.vector.tensor_tensor(A1[:, j, t0:], KD[0][:, j, t0:], KD[1][:, j, t0:], ALU.add))
                    dve.wait_ge(*dve_sig(3 * j + 1))
                    dve_sig.mark(nc.vector.tensor_scalar(A1[:, j, t0:], A1[:, j, t0:], v("r_k", j), None, ALU.mult))
                    dve.wait_ge(*dve_sig(3 * j + 2))
                    scaled.mark(nc.vector.tensor_tensor(A1[:, j, t0:], A1[:, j, t0:], Z[:, Z_R + j, t0:], ALU.mult))
                    dve.wait_ge(*sums(j + 1))
                    dve_sig.mark(nc.vector.scalar_tensor_tensor(Y[:, j, t0:], BANK[:, j, 0:n], -1.0 / HD, Y[:, j, t0:], ALU.mult, ALU.add))
                c = 3 * PAIRS
                for j in range(PAIRS):
                    dve.wait_ge(*product(j + 1))
                    evacuated.mark(nc.vector.tensor_tensor(A3[:, j, t0:], BANK[:, 4 + j, 0:n], Z[:, Z_V + j, t0:], ALU.mult))
                for j in range(PAIRS):
                    dve.wait_ge(*sums(PAIRS + j + 1))
                    c += 1
                    dve_sig.mark(nc.vector.tensor_scalar(A2[:, j, t0:], BANK[:, j, 0:n], 1.0 / HD, GN_EPS, ALU.mult, ALU.add))
                    dve.wait_ge(*dve_sig(c))
                    merged.mark(nc.vector.reciprocal(A2[:, j, t0:], A2[:, j, t0:]))
                for j in range(PAIRS):
                    dve.wait_ge(*inverse_rms(j + 1))
                    c += 1
                    dve_sig.mark(nc.vector.scalar_tensor_tensor(Y[:, j, t0:], Y[:, j, t0:], v("gn_w", j), A2[:, j, t0:], ALU.mult, ALU.mult))
                    dve.wait_ge(*dve_sig(c))
                    c += 1
                    dve_sig.mark(nc.vector.scalar_tensor_tensor(Y[:, j, t0:], Y[:, j, t0:], v("gn_b", j), A3[:, j, t0:], ALU.add, ALU.add))
                    dve.wait_ge(*dve_sig(c))
                    dve.wait_ge(*product(PAIRS + j + 1))
                    gate_ready.mark(nc.vector.tensor_tensor(A4[:, j, t0:], Y[:, j, t0:], BANK[:, 4 + j, 0:n], ALU.mult))
                for j in range(PAIRS):
                    dve.wait_ge(*high_ready(j + 1))
                    nc.vector.tensor_tensor(O_R[1][:, j, t0:], A4[:, j, t0:], O_R[0][:, j, t0:].bitcast(FP32), ALU.subtract)
        Signal.end_stage()

    ZM = carve(WORK, 0, 5, TOK)
    QH = carve(WORK, 5 * TOK, HEADS, TOK)
    KHD = carve(WORK, (5 + HEADS) * TOK, HEADS, TOK)
    VT = carve(WORK, (5 + 2 * HEADS) * TOK, 4, WIDTH)
    OM1 = (9 + 2 * HEADS) * TOK
    O_M = [place("o_mla_high", WORK0, TILES, FP32R).rearrange("p (k t) -> p k t", t=TOK),
           place("o_mla_low", WORK0 + OM1, TILES, FP32R).rearrange("p (k t) -> p k t", t=TOK)]
    assert WORK0 + OM1 + TILES <= OR0, (OM1, OR0)
    M1 = OR0 - WORK0 + 2 * TILES
    MT = carve(WORK, M1, 4, TOK)
    assert WORK0 + M1 + 5 * TOK <= W0, (M1, W0)

    def mla_weights(l):
        wi = ins["w_in"][l]
        sources = [k_tiles(wi, C_MLA, C_MLA + 256), k_tiles(wi, C_MLA + 256, C_MLA + 512), k_tiles(wi, C_MLA + 512, C_FNO)]
        return Chunks(sources, [(m // 2, 0, DT, (m % 2) * P, P if m < 4 else QK_ROPE) for m in range(5)], lambda c: product(c + 1))

    def head_weights(l):
        wq = ins["w_uq"][l].rearrange("(k p) n -> p k n", p=P)
        return Loads([ins["w_ukv"][l].rearrange("(k p) n -> p k n", p=P), wq[:, :, 0:4 * QK], wq[:, :, 4 * QK:8 * QK]])

    def mla_project(l, w, ahead):
        groups = ((0, 3, Q_LORA, "g_cq"), (3, 4, KV_LORA, "g_ckv"))
        sq = carve(WORK, 5 * TOK, 6, TOK)
        with stage() as block:
            @block.sync
            def _(sp):
                w.issue(sp, ahead)

            @block.tensor
            def _(pe):
                for m in range(5):
                    wm = w.arrived(pe, m)
                    rows = P if m < 4 else QK_ROPE
                    for k in range(DT):
                        last = product3(BANK[0:rows, m], [x[:, k] for x in wm], [x[:, k] for x in HS], k == 0, k == DT - 1)
                    product.mark(last)
                for g, (m0, m1, _, _) in enumerate(groups):
                    for m in range(m0, m1):
                        pe.wait_ge(*squares(m + 1))
                        last = nc.tensor.matmul(BANK[:, 5 + g], ones[:], sq[:, m], start=(m == m0), stop=(m == m1 - 1))
                    sums.mark(last)

            @block.scalar
            def _(act):
                for c in range(CHUNKS):
                    w.high(act, c)
                for m in range(5):
                    rows = P if m < 4 else QK_ROPE
                    act.wait_ge(*product(m + 1))
                    w.high(act, m + CHUNKS)
                    evacuated.mark(nc.scalar.activation(ZM[0:rows, m], BANK[0:rows, m], ACT.Copy))
                    if m < 4:
                        squares.mark(nc.scalar.activation(sq[:, m], BANK[:, m], ACT.Square))
                for g in range(2):
                    act.wait_ge(*merged(g + 1))
                    inverse_rms.mark(nc.scalar.activation(sq[:, 4 + g], sq[:, 4 + g], ACT.Sqrt))

            @block.vector
            def _(dve):
                for c in range(5):
                    w.low(dve, c)
                for g, (m0, m1, width, gname) in enumerate(groups):
                    dve.wait_ge(*sums(g + 1))
                    dve_sig.mark(nc.vector.tensor_scalar(sq[:, 4 + g], BANK[:, 5 + g], 1.0 / width, RMS_EPS, ALU.mult, ALU.add))
                    dve.wait_ge(*dve_sig(g + 1))
                    merged.mark(nc.vector.reciprocal(sq[:, 4 + g], sq[:, 4 + g]))
                for g, (m0, m1, width, gname) in enumerate(groups):
                    dve.wait_ge(*inverse_rms(g + 1))
                    for m in range(m0, m1):
                        dve.wait_ge(*evacuated(m + 1))
                        nc.vector.scalar_tensor_tensor(ZM[:, m], ZM[:, m], v(gname, m - m0), sq[:, 4 + g], ALU.mult, ALU.mult)
        Signal.end_stage()

    def mla_heads(l, tq, loads):
        units = [("k", h) for h in range(HEADS)] + [("q", h) for h in range(HEADS)]
        U = len(units)
        cos, sin = rope[:, 0:SEQ], rope[:, SEQ:2 * SEQ]
        rotate = rope[:, 2 * SEQ:]
        dst = lambda u: (QH if units[u][0] == "q" else KHD)[0:QK, units[u][1]]
        sq = lambda u: MT[0:QK, u % 2]
        roots = MT[0:U, 2]
        spread = WORK[0:U, M1 + 4 * TOK:M1 + 4 * TOK + U * QK].rearrange("p (u n) -> p u n", n=QK)
        assert WORK0 + M1 + 4 * TOK + U * QK <= W0
        tmp = lambda u: MT[0:QK, 3 + u % 2, 0:SEQ] if u % 2 == 0 else MT[0:QK, 3, SEQ:]
        with stage() as block:
            @block.gpsimd
            def _(pool):
                h_ready.mark(nc.gpsimd.memset(spread, 0.0))
                pool.wait_ge(*h_ready(1))
                h_ready.mark(nc.gpsimd.affine_select(out=spread, in_=spread, compare_op=ALU.not_equal, fill=1.0, base=0,
                                                     pattern=[[-1, 2 * HEADS], [0, QK]], channel_multiplier=1))
                for u in range(U):
                    pool.wait_ge(*gate_ready(u + 1))
                    pool_sig.mark(nc.gpsimd.tensor_tensor(dst(u)[:, CTX:], dst(u)[:, CTX:], cos, ALU.mult))
                    pool.wait_ge(*pool_sig(2 * u + 1))
                    pool_sig.mark(nc.gpsimd.tensor_tensor(dst(u)[:, CTX:], dst(u)[:, CTX:], tmp(u), ALU.add))

            @block.tensor
            def _(pe):
                for u in range(U + 1):
                    if u < U:
                        kind, h = units[u]
                        if u >= 2:
                            pe.wait_ge(*evacuated(u - 1))
                        if kind == "q":
                            w = loads.arrived(pe, 1 + h // 4)
                            for k in range(3):
                                last = nc.tensor.matmul(BANK[0:QK, u % 2, tq:], w[:, k, (h % 4) * QK:(h % 4 + 1) * QK], ZM[:, k, tq:],
                                                        start=(k == 0), stop=(k == 2))
                        else:
                            w = loads.arrived(pe, 0)
                            last = nc.tensor.matmul(BANK[0:QK_NOPE, u % 2], w[:, 0, h * P:h * P + QK_NOPE], ZM[:, 3], start=True, stop=True)
                        product.mark(last)
                    if u >= 1:
                        pe.wait_ge(*squares(u))
                        t = tq if units[u - 1][0] == "q" else 0
                        sums.mark(nc.tensor.matmul(BANK[0:U, 2, t:], pick[:, U - u:2 * U - u], sq(u - 1)[:, t:],
                                                   start=(u == 1), stop=(u == U)))
                w = loads.arrived(pe, 0)
                wv = w[:, 0].rearrange("p (h n) -> p h n", h=HEADS)[:, :, QK_NOPE:]
                for t in range(4):
                    rows_turned.mark(nc.tensor.matmul(BANK[:, 4 + t].rearrange("p (h n) -> p h n", h=HEADS), ZM[:, 3, t * P:(t + 1) * P], wv,
                                                      start=True, stop=True))
                pe.wait_ge(*inverse_rms(1))
                pe.wait_ge(*h_ready(2))
                for u in range(U + 2):
                    if u < U:
                        t = tq if units[u][0] == "q" else 0
                        if u >= 4:
                            pe.wait_ge(*scaled(u - 3))
                        merged.mark(nc.tensor.matmul(BANK[0:QK, u % 4, t:], spread[:, u], roots[:, t:], start=True, stop=True))
                    if u >= 2:
                        pe.wait_ge(*scaled(u - 1))
                        if u < 6:
                            pe.wait_ge(*slot_used(4))
                        else:
                            pe.wait_ge(*gate_ready(u - 5))
                        turned_out.mark(nc.tensor.matmul(BANK[0:QK, 4 + u % 4, 0:SEQ], rotate, dst(u - 2)[:, CTX:], start=True, stop=True))

            @block.scalar
            def _(act):
                for u in range(U):
                    kind, h = units[u]
                    t = tq if kind == "q" else 0
                    rows = QK if kind == "q" else QK_NOPE
                    act.wait_ge(*product(u + 1))
                    if kind == "k":
                        act.wait_ge(*first_cut(h + 1))
                    evacuated.mark(nc.scalar.activation(dst(u)[0:rows, t:], BANK[0:rows, u % 2, t:], ACT.Copy))
                    act.wait_ge(*evacuated(u + 1))
                    if u >= 2:
                        act.wait_ge(*sums(u - 1))
                    squares.mark(nc.scalar.activation(sq(u)[:, t:], dst(u)[:, t:], ACT.Square))
                act.wait_ge(*dve_sig(2))
                inverse_rms.mark(nc.scalar.activation(roots, roots, ACT.Sqrt))
                for t in range(4):
                    act.wait_ge(*rows_turned(t + 1))
                    slot_used.mark(nc.scalar.activation(VT[:, t], BANK[:, 4 + t], ACT.Copy))

            @block.vector
            def _(dve):
                for h in range(HEADS):
                    first_cut.mark(nc.vector.tensor_copy(KHD[QK_NOPE:QK, h], ZM[0:QK_ROPE, 4]))
                dve.wait_ge(*sums(U))
                dve_sig.mark(nc.vector.tensor_scalar(roots, BANK[0:U, 2], 1.0 / QK, RMS_EPS, ALU.mult, ALU.add))
                dve.wait_ge(*dve_sig(1))
                dve_sig.mark(nc.vector.reciprocal(roots, roots))
                for u in range(U + 2):
                    if u < U:
                        t = tq if units[u][0] == "q" else 0
                        g = 0 if units[u][0] == "q" else 1
                        dve.wait_ge(*merged(u + 1))
                        scaled.mark(nc.vector.scalar_tensor_tensor(dst(u)[:, t:], dst(u)[:, t:], g_head[:, g:g + 1], BANK[0:QK, u % 4, t:],
                                                                   ALU.mult, ALU.mult))
                    if u >= 2:
                        dve.wait_ge(*turned_out(u - 1))
                        if u >= 4:
                            dve.wait_ge(*pool_sig(2 * (u - 4) + 2))
                        gate_ready.mark(nc.vector.tensor_tensor(tmp(u), BANK[0:QK, 4 + u % 4, 0:SEQ], sin, ALU.mult))
        Signal.end_stage()

    def attention(tq, ahead):
        units = [(h, q) for h in range(HEADS) for q in range(tq // P, TOK // P)]
        U = len(units)
        keys = lambda u: TOK if units[u][1] * P >= CTX else CTX
        PR = lambda u: MT[:, u % 2]
        PTR = lambda u: MT[:, 2 + u % 2]
        stat = carve(WORK, M1 + 4 * TOK, 3, 2 * len(units) + 1)
        with stage() as block:
            @block.sync
            def _(sp):
                ahead.start(sp, len(ahead.sources))

            @block.tensor
            def _(pe):
                for u in range(U + 2):
                    if u < U:
                        h, q = units[u]
                        if u >= 2:
                            pe.wait_ge(*squares(u - 1))
                        product.mark(nc.tensor.matmul(BANK[:, u % 2, 0:keys(u)], QH[0:QK, h, q * P:(q + 1) * P], KHD[0:QK, h, 0:keys(u)], start=True, stop=True))
                    if 1 <= u <= U:
                        pe.wait_ge(*scaled(u))
                        if u >= 3:
                            pe.wait_ge(*turned_out(u - 2))
                        for k in range(keys(u - 1) // P):
                            last = nc.tensor.transpose(BANK[:, 2 + (u - 1) % 2, k * P:(k + 1) * P], PR(u - 1)[:, k * P:(k + 1) * P], ident[:])
                        rows_turned.mark(last)
                    if u >= 2:
                        h, q = units[u - 2]
                        rows = slice((h % 2) * VH, (h % 2 + 1) * VH)
                        pe.wait_ge(*turned_out(u - 1))
                        if u >= 4:
                            pe.wait_ge(*evacuated(u - 3))
                        n = keys(u - 2) // P
                        for k in range(n):
                            last = nc.tensor.matmul(BANK[rows, 4 + u % 2, 0:P], VT[:, k, h * VH:(h + 1) * VH], PTR(u - 2)[:, k * P:(k + 1) * P],
                                                    start=(k == 0), stop=(k == n - 1))
                        sums.mark(last)

            @block.vector
            def _(dve):
                c = 0
                for u in range(U + 2):
                    if u < U:
                        dve.wait_ge(*product(u + 1))
                        c += 1
                        dve_sig.mark(nc.vector.reduce_max(stat[:, 0, u:u + 1], BANK[:, u % 2, 0:keys(u)], AX.X))
                        dve.wait_ge(*dve_sig(c))
                        gate_ready.mark(nc.vector.tensor_scalar(stat[:, 1, u:u + 1], stat[:, 0, u:u + 1], -(QK ** -0.5), None, ALU.mult))
                    if u >= 1 and u <= U:
                        dve.wait_ge(*squares(u))
                        c += 1
                        dve_sig.mark(nc.vector.reciprocal(stat[:, 2, 2 * u - 1:2 * u], stat[:, 2, 2 * u - 2:2 * u - 1]))
                        dve.wait_ge(*dve_sig(c))
                        scaled.mark(nc.vector.tensor_scalar(PR(u - 1)[:, 0:keys(u - 1)], PR(u - 1)[:, 0:keys(u - 1)], stat[:, 2, 2 * u - 1:2 * u], None, ALU.mult))
                    if u >= 2:
                        h, q = units[u - 2]
                        rows = slice((h % 2) * VH, (h % 2 + 1) * VH)
                        dve.wait_ge(*sums(u - 1))
                        o = [x[rows, h // 2, q * P:(q + 1) * P] for x in O_M]
                        high_ready.mark(nc.vector.tensor_copy(o[0], BANK[rows, 4 + u % 2, 0:P]))
                        dve.wait_ge(*high_ready(u - 1))
                        evacuated.mark(nc.vector.tensor_tensor(o[1], BANK[rows, 4 + u % 2, 0:P], o[0].bitcast(FP32), ALU.subtract))

            @block.scalar
            def _(act):
                for u in range(U + 1):
                    if u < U:
                        act.wait_ge(*gate_ready(u + 1))
                        if u >= 2:
                            act.wait_ge(*rows_turned(u - 1))
                        squares.mark(nc.scalar.activation(PR(u)[:, 0:keys(u)], BANK[:, u % 2, 0:keys(u)], ACT.Exp, bias=stat[:, 1, u:u + 1],
                                                          scale=QK ** -0.5, accum_out=stat[:, 2, 2 * u:2 * u + 1]))
                    if u >= 1:
                        act.wait_ge(*rows_turned(u))
                        if u >= 3:
                            act.wait_ge(*sums(u - 2))
                        turned_out.mark(nc.scalar.activation(PTR(u - 1)[:, 0:keys(u - 1)], BANK[:, 2 + (u - 1) % 2, 0:keys(u - 1)], ACT.Copy))
        Signal.end_stage()

    ZF = carve(WORK, TILES, PAIRS, TOK)
    UF = carve(WORK, 2 * TILES, PAIRS, 4, 2 * P)
    OF0 = 4 * TILES
    O_F = parts("o_fourier", WORK0 + OF0, PAIRS)
    assert OF0 + 2 * TILES <= OM1
    dft_feature = carve(WORK, M1, 2 * P)
    dft_token = carve(WORK, M1 + 2 * P, 2, 2 * SEQ)

    def fourier_weights(l):
        wi = ins["w_in"][l]
        return Chunks([k_tiles(wi, C_FNO, C_FNO + 256), k_tiles(wi, C_FNO + 256, C_FNO + 512)],
                      [(m // 2, 0, DT, (m % 2) * P, P) for m in range(PAIRS)], lambda c: product(c + 1))

    def fourier(l, t0, w, ahead):
        n = TOK - t0
        tiles = list(range(t0 // P, 4))
        with stage() as block:
            @block.sync
            def _(sp):
                sp.dma_start(dft_feature, ins["dft_feature"]).then_inc(dft_in, 16)
                sp.dma_start(dft_token, ins["dft_token"].rearrange("(t p) n -> p t n", p=P)).then_inc(dft_in, 16)
                w.issue(sp, ahead)

            @block.tensor
            def _(pe):
                for m in range(PAIRS):
                    wm = w.arrived(pe, m)
                    for k in range(DT):
                        last = product3(BANK[:, m, 0:n], [x[:, k] for x in wm], [x[:, k, t0:] for x in HS], k == 0, k == DT - 1)
                    product.mark(last)
                pe.wait_ge(dft_in, 32 * (l + 1))
                i = 0
                for m in range(PAIRS):
                    pe.wait_ge(*evacuated(m + 1))
                    for t in tiles:
                        if i >= 4:
                            pe.wait_ge(*turned_out(i - 3))
                        rows_turned.mark(nc.tensor.matmul(BANK[:, 4 + i % 4, 0:2 * P], ZF[:, m, t * P:(t + 1) * P], dft_feature, start=True, stop=True))
                        i += 1
                i = 0
                for m in range(PAIRS):
                    for s in range(t0 // CTX, 2):
                        pe.wait_ge(*turned_out(len(tiles) * m + 2 * (s - t0 // CTX) + 2))
                        if i >= 4:
                            pe.wait_ge(*scaled(i - 3))
                        for part in range(2):
                            for t in range(2):
                                last = nc.tensor.matmul(BANK[:, i % 4, 0:SEQ], UF[:, m, 2 * s + t, part * P:(part + 1) * P],
                                                        dft_token[:, t, part * SEQ:(part + 1) * SEQ],
                                                        start=(part == 0 and t == 0), stop=(part == 1 and t == 1))
                        sums.mark(last)
                        i += 1

            @block.scalar
            def _(act):
                for c in range(PAIRS):
                    w.high(act, c)
                for m in range(PAIRS):
                    act.wait_ge(*product(m + 1))
                    evacuated.mark(nc.scalar.activation(ZF[:, m, t0:], BANK[:, m, 0:n], ACT.Copy))
                i = 0
                for m in range(PAIRS):
                    for t in tiles:
                        act.wait_ge(*rows_turned(i + 1))
                        turned_out.mark(nc.scalar.activation(UF[:, m, t], BANK[:, 4 + i % 4, 0:2 * P], ACT.Copy))
                        i += 1

            @block.vector
            def _(dve):
                for c in range(PAIRS):
                    w.low(dve, c)
                i = 0
                for m in range(PAIRS):
                    for s in range(t0 // CTX, 2):
                        dve.wait_ge(*sums(i + 1))
                        o = [x[:, m, s * SEQ:(s + 1) * SEQ] for x in O_F]
                        dve_sig.mark(nc.vector.tensor_copy(o[0], BANK[:, i % 4, 0:SEQ]))
                        dve.wait_ge(*dve_sig(i + 1))
                        scaled.mark(nc.vector.tensor_tensor(o[1], BANK[:, i % 4, 0:SEQ], o[0].bitcast(FP32), ALU.subtract))
                        i += 1
        Signal.end_stage()

    MERGE = [place("merge_high", WORK0 + TILES, DT * TOK, FP32R).rearrange("p (k t) -> p k t", t=TOK),
             place("merge_low", WORK0 + M1, DT * TOK, FP32R).rearrange("p (k t) -> p k t", t=TOK)]
    TMP = place("merge_tiles", WORK0 + 3 * TILES, 4 * TOK).rearrange("p (k t) -> p k t", t=TOK)
    assert WORK0 + M1 + DT * TOK <= W0, (WORK0 + M1 + DT * TOK, W0)

    steps = [(mm, b) for mm in range(DT // 2) for b in range(3)]

    def merge_weights(l):
        wi = ins["w_in"][l]
        sources, chunks = [], []
        for i, (mm, b) in enumerate(steps):
            c = C_GATE + b * D + mm * 2 * P
            wo = ins[("w_rwkv_o", "w_mla_o", "w_fno")[b]][l]
            sources += [k_tiles(wi, c, c + 2 * P), k_tiles(wo, mm * 2 * P, (mm + 1) * 2 * P)]
            chunks += [(2 * i, 0, DT, 0, P), (2 * i, 0, DT, P, P), (2 * i + 1, 0, PAIRS, 0, 2 * P)]
        return Chunks(sources, chunks, lambda c: pe_sig(c // 3 * 2 + c % 3 + 1) if c % 3 < 2 else product(c // 3 * 2 + 2))

    def merge(l, t0, w, ahead):
        n = TOK - t0
        branch = (O_R, O_M, O_F)
        gate = lambda u: TMP[:, u % 2, 0:n]
        total = lambda m: TMP[:, 2 + m, 0:n]
        adds = lambda i: sum(2 for x in steps[:i] if x[1] > 0)
        with stage() as block:
            @block.sync
            def _(sp):
                w.issue(sp, ahead)

            @block.tensor
            def _(pe):
                for i, (mm, b) in enumerate(steps):
                    for m in range(2):
                        u = 2 * i + m
                        wg = w.arrived(pe, 3 * i + m)
                        if i > 0:
                            pe.wait_ge(*gate_ready(u - 1))
                        for k in range(DT):
                            last = product3(BANK[:, m, 0:n], [x[:, k] for x in wg], [x[:, k, t0:] for x in HS], k == 0, k == DT - 1)
                        pe_sig.mark(last)
                    wo = w.arrived(pe, 3 * i + 2)
                    for m in range(2):
                        u = 2 * i + m
                        if i > 0:
                            pe.wait_ge(*scaled(u - 1))
                        for k in range(PAIRS):
                            last = product3(BANK[:, 2 + m, 0:n], [x[:, k, m * P:(m + 1) * P] for x in wo], [x[:, k, t0:] for x in branch[b]],
                                            k == 0, k == PAIRS - 1)
                        product.mark(last)

            @block.scalar
            def _(act):
                for c in range(CHUNKS):
                    w.high(act, c)
                for i, (mm, b) in enumerate(steps):
                    for m in range(2):
                        u = 2 * i + m
                        act.wait_ge(*pe_sig(u + 1))
                        w.high(act, 3 * (i + 1) + m)
                        if u >= 2:
                            act.wait_ge(*scaled(u - 1))
                            if adds(i) and steps[i - 1][1] > 0:
                                act.wait_ge(*pool_sig(adds(i - 1) + m + 1))
                        gate_ready.mark(nc.scalar.activation(gate(u), BANK[:, m, 0:n], ACT.Sigmoid))
                    if b == 2:
                        for m in range(2):
                            act.wait_ge(*pool_sig(adds(i) + m + 1))
                            merged.mark(nc.scalar.activation(MERGE[0][:, 2 * mm + m, t0:], total(m), ACT.Copy))
                    w.high(act, 3 * (i + 1) + 2)

            @block.vector
            def _(dve):
                for c in range(CHUNKS):
                    w.low(dve, c)
                for i, (mm, b) in enumerate(steps):
                    for m in range(2):
                        w.low(dve, 3 * (i + 1) + m)
                    for m in range(2):
                        u = 2 * i + m
                        dve.wait_ge(*gate_ready(u + 1))
                        dve.wait_ge(*product(u + 1))
                        if b == 0:
                            if mm > 0:
                                dve.wait_ge(*h_ready(2 * (mm - 1) + m + 1))
                            scaled.mark(nc.vector.tensor_tensor(total(m), gate(u), BANK[:, 2 + m, 0:n], ALU.mult))
                        else:
                            scaled.mark(nc.vector.tensor_tensor(gate(u), gate(u), BANK[:, 2 + m, 0:n], ALU.mult))
                    if b == 2:
                        for m in range(2):
                            dve.wait_ge(*merged(2 * mm + m + 1))
                            h_ready.mark(nc.vector.tensor_tensor(MERGE[1][:, 2 * mm + m, t0:], total(m),
                                                                 MERGE[0][:, 2 * mm + m, t0:].bitcast(FP32), ALU.subtract))
                    w.low(dve, 3 * (i + 1) + 2)

            @block.gpsimd
            def _(pool):
                for i, (mm, b) in enumerate(steps):
                    for m in range(2):
                        u = 2 * i + m
                        if b > 0:
                            pool.wait_ge(*scaled(u + 1))
                            if b > 1:
                                pool.wait_ge(*pool_sig(adds(i) - 2 + m + 1))
                            pool_sig.mark(nc.gpsimd.tensor_tensor(total(m), total(m), gate(u), ALU.add))
        Signal.end_stage()

    def add_to_stream(dve, m, bank, which, t0, mark):
        for s in range(t0 // CTX, 2):
            a = s * CTX
            last = nc.vector.scalar_tensor_tensor(X[:, m, a:a + CTX], BANK[:, bank, a - t0:a - t0 + CTX], mod[:, which, m, s:s + 1],
                                                  X[:, m, a:a + CTX], ALU.mult, ALU.add)
        mark(last)

    def out_weights(l):
        return Chunks([k_tiles(ins["w_out"][l], c, c + 2 * P) for c in range(0, D, 2 * P)],
                      [(m // 2, 0, DT, (m % 2) * P, P) for m in range(DT)], lambda c: product(c + 1))

    def project_out(l, t0, w, ahead):
        n = TOK - t0
        with stage() as block:
            @block.sync
            def _(sp):
                w.issue(sp, ahead)

            @block.tensor
            def _(pe):
                for m in range(DT):
                    wm = w.arrived(pe, m)
                    for k in range(DT):
                        last = product3(BANK[:, m, 0:n], [x[:, k] for x in wm], [x[:, k, t0:] for x in MERGE], k == 0, k == DT - 1)
                    product.mark(last)

            @block.scalar
            def _(act):
                for c in range(DT):
                    w.high(act, c)

            @block.vector
            def _(dve):
                for c in range(CHUNKS):
                    w.low(dve, c)
                for m in range(DT):
                    dve.wait_ge(*product(m + 1))
                    add_to_stream(dve, m, m, 2, t0, evacuated.mark)
                    w.low(dve, m + CHUNKS)
        Signal.end_stage()

    HID = parts("hidden", WORK0, FT)
    FTMP = place("ffn_tiles", WORK0 + 2 * FT * TOK, 2 * TOK).rearrange("p (k t) -> p k t", t=TOK)
    assert WORK0 + 2 * FT * TOK + 2 * TOK <= W0, (W0,)

    def ffn_in_weights(l):
        wi = ins["w_ffn_in"][l]
        sources = []
        for c in range(0, FFN, 2 * P):
            sources += [k_tiles(wi, c, c + 2 * P), k_tiles(wi, FFN + c, FFN + c + 2 * P)]
        return Chunks(sources, [(u // 2 * 2 + g, 0, DT, (u % 2) * P, P) for u in range(FT) for g in range(2)],
                      lambda c: (product if c % 2 else pe_sig)(c // 2 + 1))

    def ffn_in(l, t0, w, ahead):
        n = TOK - t0
        tile = lambda u: FTMP[:, u % 2, 0:n]
        with stage() as block:
            @block.sync
            def _(sp):
                w.issue(sp, ahead)

            @block.tensor
            def _(pe):
                for u in range(FT):
                    for g in range(2):
                        wm = w.arrived(pe, 2 * u + g)
                        if u >= 2:
                            pe.wait_ge(*(gate_ready if g == 0 else scaled)(u - 1))
                        for k in range(DT):
                            last = product3(BANK[:, 2 * g + u % 2, 0:n], [x[:, k] for x in wm], [x[:, k, t0:] for x in HS], k == 0, k == DT - 1)
                        (pe_sig if g == 0 else product).mark(last)

            @block.scalar
            def _(act):
                for c in range(CHUNKS):
                    w.high(act, c)
                for u in range(FT):
                    act.wait_ge(*pe_sig(u + 1))
                    w.high(act, 2 * u + CHUNKS)
                    if u >= 2:
                        act.wait_ge(*evacuated(u - 1))
                    gate_ready.mark(nc.scalar.activation(tile(u), BANK[:, u % 2, 0:n], ACT.Silu))
                    w.high(act, 2 * u + 1 + CHUNKS)
                    act.wait_ge(*scaled(u + 1))
                    merged.mark(nc.scalar.activation(HID[0][:, u, t0:], tile(u), ACT.Copy))

            @block.vector
            def _(dve):
                for c in range(CHUNKS):
                    w.low(dve, c)
                for u in range(FT):
                    w.low(dve, 2 * u + CHUNKS)
                    dve.wait_ge(*gate_ready(u + 1))
                    dve.wait_ge(*product(u + 1))
                    scaled.mark(nc.vector.tensor_tensor(tile(u), tile(u), BANK[:, 2 + u % 2, 0:n], ALU.mult))
                    w.low(dve, 2 * u + 1 + CHUNKS)
                    dve.wait_ge(*merged(u + 1))
                    evacuated.mark(nc.vector.tensor_tensor(HID[1][:, u, t0:], tile(u), HID[0][:, u, t0:].bitcast(FP32), ALU.subtract))
        Signal.end_stage()

    def ffn_out_weights(l):
        wo = ins["w_ffn_out"][l].rearrange("(k p) n -> p k n", p=P)
        return Chunks([wo[:, k:k + 2, :] for k in range(0, FT, 2)], [(k // 2, k % 2, 1, 0, D) for k in range(FT)],
                      lambda c: slot_used(c + 1))

    def ffn_out(l, t0, w, ahead):
        n = TOK - t0
        with stage() as block:
            @block.sync
            def _(sp):
                w.issue(sp, ahead)

            @block.tensor
            def _(pe):
                for k in range(FT):
                    wk = w.arrived(pe, k)
                    for m in range(DT):
                        last = product3(BANK[:, m, 0:n], [x[:, 0, m * P:(m + 1) * P] for x in wk], [x[:, k, t0:] for x in HID],
                                        k == 0, k == FT - 1)
                        if k == FT - 1:
                            product.mark(last)
                    if k < FT - 1:
                        slot_used.mark(last)

            @block.scalar
            def _(act):
                for c in range(FT):
                    w.high(act, c)

            @block.vector
            def _(dve):
                for c in range(FT):
                    w.low(dve, c)
                for m in range(DT):
                    dve.wait_ge(*product(m + 1))
                    add_to_stream(dve, m, m, 5, t0, evacuated.mark)
        Signal.end_stage()

    w_modulation = modulation_weights(0)
    for l in range(DEPTH):
        t0 = CTX if l == DEPTH - 1 else 0
        w_rwkv = rwkv_weights(l)
        modulation(l, w_modulation, w_rwkv)
        norm(scale_1, mod[:, 0], 0, save=True)
        project_rwkv(l, w_rwkv)
        features()
        scan(l < DEPTH - 1)
        w_mla, w_heads, w_fourier = mla_weights(l), head_weights(l), fourier_weights(l)
        rwkv_output(l, t0, w_mla)
        mla_project(l, w_mla, w_heads)
        mla_heads(l, t0, w_heads)
        attention(t0, w_fourier)
        w_merge, w_out = merge_weights(l), out_weights(l)
        fourier(l, t0, w_fourier, w_merge)
        merge(l, t0, w_merge, w_out)
        w_ffn_in, w_ffn_out = ffn_in_weights(l), ffn_out_weights(l)
        project_out(l, t0, w_out, w_ffn_in)
        norm(scale_2, mod[:, 3], t0)
        ffn_in(l, t0, w_ffn_in, w_ffn_out)
        w_modulation = modulation_weights(l + 1) if l + 1 < DEPTH else None
        ffn_out(l, t0, w_ffn_out, w_modulation)

    result = carve(WORK, 0, 2, D)
    with stage() as block:
        @block.tensor
        def _(pe):
            for b in range(4):
                for q in range(4):
                    t, k = b // 2, (b % 2) * 4 + q
                    last = nc.tensor.transpose(BANK[:, b, q * P:(q + 1) * P], X[:, k, CTX + t * P:CTX + (t + 1) * P], ident[:])
                rows_turned.mark(last)

        @block.vector
        def _(dve):
            for b in range(4):
                dve.wait_ge(*rows_turned(b + 1))
                turned_out.mark(nc.vector.tensor_copy(result[:, b // 2, (b % 2) * 512:(b % 2 + 1) * 512], BANK[:, b]))

        @block.sync
        def _(sp):
            sp.wait_ge(*turned_out(4))
            sp.dma_start(out[0].rearrange("(t p) d -> p t d", p=P), result).then_inc(out_stored, 16)
            sp.wait_ge(out_stored, 16)
    Signal.end_stage()


def kernel(**inputs):
    from concourse import bacc
    from concourse.bass_utils import run_bass_kernel_spmd

    nc = bacc.Bacc("TRN2", target_bir_lowering=False, num_devices=1)
    arrays, aps = {}, {}
    for name, a in {**inputs, **shape_constants()}.items():
        a = np.ascontiguousarray(a)
        arrays[f"{name}_dram"] = a
        aps[name] = nc.dram_tensor(f"{name}_dram", a.shape, mybir.dt.from_np(a.dtype), kind="ExternalInput").ap()
    out = nc.dram_tensor("out_dram", (1, SEQ, D), FP32, kind="ExternalOutput").ap()
    build(nc, aps, out)
    result = run_bass_kernel_spmd(nc, [arrays], core_ids=[0])
    return result.results[0]["out_dram"]
```

```python
from contextlib import ExitStack

import concourse.bass as bass
import numpy as np
from concourse import mybir

FP32 = mybir.dt.float32
FP32R = mybir.dt.float32r
ACT = mybir.ActivationFunctionType
ALU = mybir.AluOpType
AX = mybir.AxisListType

P = 128
D = 1024
DT = D // P
SEQ = 256
CTX = 256
TOK = CTX + SEQ
DEPTH = 2
GRID_W = 64

HEADS = 8
HD = 64
PAIRS = HEADS // 2
WIDTH = HEADS * HD
NDIR = 2
Z_R, Z_K, Z_V, Z_W, Z_A, Z_G = 0, 4, 8, 12, 13, 14
Z_TILES = 15
N_RWKV_IN = Z_TILES * P

QK_NOPE, QK_ROPE = 64, 32
QK = QK_NOPE + QK_ROPE
VH = 64
Q_LORA, KV_LORA = 384, 128
ROPE_AXIS = QK_ROPE // 2
N_MLA_IN = Q_LORA + KV_LORA + QK_ROPE
C_MLA = N_RWKV_IN
C_FNO = C_MLA + N_MLA_IN
C_GATE = C_FNO + WIDTH
N_IN = C_GATE + 3 * D

FFN = ((8 * D + 3 * 256 - 1) // (3 * 256)) * 256
FT = FFN // P

RMS_EPS = 1e-6
GN_EPS = 64e-5
KAPPA = float(np.exp(-0.5))

CHUNK = 64
SEG_CHUNKS = SEQ // CHUNK
LEVELS = 6

SLOTS = 3
SLOT = 2048
CHUNKS = 3
CHUNK_W = SLOT // 2

VEC_ROWS = [("g_norm1", 8), ("g_norm2", 8), ("mu_prev", 15), ("mu_next", 15), ("w0", 8), ("a0", 8),
            ("k_k", 4), ("k_a", 4), ("r_k", 4), ("gn_w", 4), ("gn_b", 4), ("g_cq", 3), ("g_ckv", 1)]
VEC_AT = {}
_n = 0
for _name, _k in VEC_ROWS:
    VEC_AT[_name] = (_n, _k)
    _n += _k
N_VEC = _n
N_BMOD = 6 * DT


def shape_constants():
    f = np.float32
    out = {}
    out["ident"] = np.eye(P, dtype=f)
    out["head_ones"] = np.kron(np.eye(2), np.ones((HD, HD))).astype(f)
    n = np.arange(HD)
    ang = 2 * np.pi * ((n[:, None] * n[None, :]) % HD) / HD
    pick = np.zeros((PAIRS, 2, HD, HEADS))
    for g in range(HEADS):
        pick[g // 2, g % 2, :, g] = 1.0
    pick = pick.reshape(PAIRS, P, HEADS)
    out["pick_heads"] = pick.transpose(1, 0, 2).reshape(P, PAIRS * HEADS).astype(f)
    out["spread_heads"] = pick.transpose(2, 0, 1).reshape(HEADS, PAIRS * P).astype(f)
    out["dft_feature"] = np.concatenate([np.kron(np.eye(2), np.cos(ang)), np.kron(np.eye(2), np.sin(ang))],
                                        axis=1).astype(f)
    t = np.arange(SEQ)
    ang = 2 * np.pi * ((t[:, None] * t[None, :]) % SEQ) / SEQ
    norm = 1.0 / np.sqrt(SEQ * HD)
    out["dft_token"] = np.concatenate([np.cos(ang) * norm, -np.sin(ang) * norm], axis=1).astype(f)
    inv = 10000.0 ** (-np.arange(0, ROPE_AXIS, 2, dtype=np.float64) / ROPE_AXIS)
    cos, sin = np.ones((QK, SEQ)), np.zeros((QK, SEQ))
    rot = np.zeros((QK, QK))
    h = ROPE_AXIS // 2
    for axis, pos in enumerate((t // GRID_W, t % GRID_W)):
        a = pos[None, :] * inv[:, None]
        lo = QK_NOPE + axis * ROPE_AXIS
        for part in (0, h):
            cos[lo + part:lo + part + h] = np.cos(a)
            sin[lo + part:lo + part + h] = np.sin(a)
        for i in range(h):
            rot[lo + h + i, lo + i] = -1.0
            rot[lo + i, lo + h + i] = 1.0
    out["rope"] = np.concatenate([cos, sin, rot], axis=1).astype(f)
    r, c = np.arange(HD)[:, None], np.arange(HD)[None, :]
    stack = lambda m: np.concatenate([m, m], axis=0)
    masks = []
    for d in range(NDIR):
        earlier = (lambda a, b: a < b) if d == 0 else (lambda a, b: a > b)
        level = []
        for l in range(LEVELS):
            b = 1 << l
            same = (r // (2 * b) == c // (2 * b)) & (r // b != c // b)
            level.append(same & earlier(r, c))
        strict_t = earlier(r, c)
        incl_t = strict_t | (r == c)
        parts = [-(level[0].T.astype(f)), -(level[0].astype(f))] + [m.astype(f) for m in level[1:]]
        parts += [strict_t.astype(f), incl_t.astype(f)]
        masks.append(np.concatenate([stack(m) for m in parts], axis=1))
    out["masks"] = np.concatenate(masks, axis=1).astype(f)
    out["eye_heads"] = stack(np.eye(HD)).astype(f)
    return out


class Signal:

    trips = 1
    every = []

    def __init__(self, ctx, nc, name):
        self.sem = ctx.enter_context(nc.semaphore(name))
        self.base = 0
        self.made = 0
        Signal.every.append(self)

    def mark(self, ins):
        self.made += Signal.trips
        return ins.then_inc(self.sem, 1)

    def count(self, eng):
        self.made += 1
        eng.sem_inc(self.sem, 1)

    def __call__(self, k):
        return self.sem, self.base + k

    @staticmethod
    def end_stage():
        for s in Signal.every:
            s.base += s.made
            s.made = 0


def build(nc, ins, out):
    Signal.every = []
    Signal.trips = 1
    with ExitStack() as ctx:
        ctx.enter_context(nc.allow_non_contiguous_dma(reason="two norm vectors as columns"))
        build_in(ctx, nc, ins, out)


def build_in(ctx, nc, ins, out):
    def sb(name, shape):
        return ctx.enter_context(nc.sbuf_tensor(name, shape, FP32))

    def sig(name):
        return Signal(ctx, nc, name)

    X = sb("X", [P, DT, TOK])
    ident = sb("ident", [P, P])
    ones = sb("ones", [P, P])
    head_ones = sb("head_ones", [P, P])
    eye_heads = sb("eye_heads", [P, HD])
    pick_heads = sb("pick_heads", [P, PAIRS, HEADS])
    spread_heads = sb("spread_heads", [HEADS, PAIRS, P])
    rope = sb("rope", [QK, 2 * SEQ + QK])
    pick = sb("pick", [QK, 4 * HEADS])
    masks = sb("masks", [P, NDIR, LEVELS + 3, HD])
    vec_rows = sb("vec_rows", [P, 2, P])
    vec = sb("vec", [P, N_VEC])
    bmod = sb("bmod", [P, N_BMOD])
    silu_c = sb("silu_c", [P, DT, 2])
    SILU_C = [ctx.enter_context(nc.sbuf_tensor(f"silu_c_{x}", [P, DT, 2], FP32R))[:] for x in ("high", "low")]
    mod = sb("mod", [P, 6, DT, 2])
    scale_1 = sb("scale_1", [P, DT, 2])
    scale_2 = sb("scale_2", [P, DT, 2])
    mu_self = sb("mu_self", [P, Z_TILES])
    ka_rest = sb("ka_rest", [P, PAIRS])
    g_head = sb("g_head", [QK, 2])
    w2_sb = sb("w2_sb", [P, WIDTH])
    a2_sb = sb("a2_sb", [P, WIDTH])
    g2_sb = sb("g2_sb", [P, WIDTH])
    DEC = [sb(f"decay_{d}", [HD, HEADS]) for d in range(NDIR)]
    DEC_KEPT = [sb(f"decay_kept_{d}", [HD, HEADS]) for d in range(NDIR)]
    BANK = ctx.enter_context(nc.psum_tensor("BANK", [P, 8, 512], FP32))

    arena = (nc.sbuf_base + 63) // 64 * 64
    arena_n = (nc.sbuf_usable_end - arena) // 64 * 16

    def place(name, at, n, dtype=FP32):
        return nc.alloc_sbuf_tensor_at(name, [P, n], dtype, offset=arena + 4 * at)[:]

    def parts(name, at, tiles, n=TOK):
        return [place(f"{name}_{x}", at + i * tiles * n, tiles * n, FP32R).rearrange("p (k t) -> p k t", t=n)
                for i, x in enumerate(("high", "low"))]

    WORK0 = SLOTS * SLOT
    RING = place("RING", 0, SLOTS * SLOT).rearrange("p (s n) -> p s n", s=SLOTS)
    H0 = arena_n - 2 * DT * TOK
    W0 = H0 - 2 * CHUNKS * CHUNK_W
    WORK_N = arena_n - WORK0
    WORK = place("WORK", WORK0, WORK_N)
    HS = parts("H", H0, DT)
    WS2 = parts("W", W0, CHUNKS, CHUNK_W)

    def carve(mem, at, *shape):
        n = 1
        for s in shape:
            n *= s
        flat = mem[:, at:at + n]
        if len(shape) == 1:
            return flat
        names = "abcd"[:len(shape)]
        return flat.rearrange(f"p ({' '.join(names)}) -> p {' '.join(names)}",
                              **{k: s for k, s in zip(names[1:], shape[1:])})

    def v(name, i):
        at = VEC_AT[name][0] + i
        return vec[:, at:at + 1]

    slot_full = [ctx.enter_context(nc.semaphore(f"slot_full_{s}")) for s in range(SLOTS)]
    slot_used = sig("slot_used")
    ring = {"next": 0}

    class Loads:

        def __init__(self, sources):
            self.sources = sources
            self.first = ring["next"]
            self.sent = 0
            ring["next"] += len(sources)

        def start(self, sp, n):
            for i in range(self.sent, n):
                sp.dma_start(self.view(i), self.sources[i]).then_inc(slot_full[(self.first + i) % SLOTS], 16)
            self.sent = n

        def issue(self, sp, used=None, ahead=None):
            count = len(self.sources)
            self.start(sp, min(SLOTS, count))
            for i in range(SLOTS, count):
                if used(i - SLOTS):
                    sp.wait_ge(*used(i - SLOTS))
                self.start(sp, i + 1)
            if ahead:
                for i in range(min(SLOTS, len(ahead.sources))):
                    if count + i >= SLOTS and used(count + i - SLOTS):
                        sp.wait_ge(*used(count + i - SLOTS))
                    ahead.start(sp, i + 1)

        def view(self, i):
            src = self.sources[i]
            k, w = src.shape[1], src.shape[2]
            s = (self.first + i) % SLOTS
            return RING[:, s, 0:k * w].rearrange("p (k w) -> p k w", k=k)

        def arrived(self, pe, i):
            n = self.first + i
            pe.wait_ge(slot_full[n % SLOTS], 16 * (n // SLOTS + 1))
            return self.view(i)

    class Chunks:

        def __init__(self, sources, chunks, used):
            self.loads = Loads(sources)
            self.sources = sources
            self.chunks = chunks
            self.used = used
            self.early = 0

        def start(self, sp, n):
            self.loads.start(sp, n)

        def issue(self, sp, ahead=None):
            last = {load: c for c, (load, *_) in enumerate(self.chunks)}
            self.loads.issue(sp, lambda i: low_ready(last[i] + 1 - self.early) if last[i] >= self.early else None, ahead)

        def raw(self, c):
            load, k0, k, c0, w = self.chunks[c]
            return self.loads.view(load)[:, k0:k0 + k, c0:c0 + w]

        def part(self, x, c):
            _, _, k, _, w = self.chunks[c]
            return WS2[x][:, c % CHUNKS, 0:k * w].rearrange("p (k w) -> p k w", k=k)

        def make_high(self, act, c):
            self.loads.arrived(act, self.chunks[c][0])
            high_ready.mark(nc.scalar.activation(self.part(0, c), self.raw(c), ACT.Copy))

        def make_low(self, c):
            low_ready.mark(nc.vector.tensor_tensor(self.part(1, c), self.raw(c), self.part(0, c).bitcast(FP32), ALU.subtract))

        def high(self, act, c):
            if self.early <= c < len(self.chunks):
                if c >= CHUNKS:
                    act.wait_ge(*self.used(c - CHUNKS))
                self.make_high(act, c)

        def low(self, dve, c):
            if self.early <= c < len(self.chunks):
                dve.wait_ge(*high_ready(c + 1 - self.early))
                self.make_low(c)

        def arrived(self, pe, c):
            if c >= self.early:
                pe.wait_ge(*low_ready(c + 1 - self.early))
            return self.part(0, c), self.part(1, c)

        def high_ahead(self, act, before=None):
            for c in range(CHUNKS):
                if before:
                    n = len(before.chunks)
                    act.wait_ge(*before.used(max(q for q in range(n) if q % CHUNKS == c)))
                self.make_high(act, c)

        def low_ahead(self, dve, before=None):
            done = len(before.chunks) - before.early if before else 0
            for c in range(CHUNKS):
                dve.wait_ge(*high_ready(done + c + 1))
                self.make_low(c)
            return CHUNKS

    def product3(out, w, x, start, stop):
        nc.tensor.matmul(out, w[0], x[0], start=start, stop=False)
        nc.tensor.matmul(out, w[0], x[1], start=False, stop=False)
        return nc.tensor.matmul(out, w[1], x[0], start=False, stop=stop)

    def k_tiles(dram, c0, c1):
        return dram[:, c0:c1].rearrange("(k p) n -> p k n", p=P)

    consts_in = ctx.enter_context(nc.semaphore("consts_in"))
    rows_in = ctx.enter_context(nc.semaphore("rows_in"))
    small_in = ctx.enter_context(nc.semaphore("small_in"))
    out_stored = ctx.enter_context(nc.semaphore("out_stored"))
    pe_sig, act_sig, dve_sig, pool_sig = sig("pe_step"), sig("act_step"), sig("dve_step"), sig("pool_step")
    rows_turned = sig("rows_turned")
    turned_out = sig("turned_out")
    squares = sig("squares")
    sums = sig("sums")
    inverse_rms = sig("inverse_rms")
    scaled = sig("scaled")
    h_ready = sig("h_ready")
    product = sig("product")
    evacuated = sig("evacuated")
    first_cut = sig("first_cut")
    gate_ready = sig("gate_ready")
    merged = sig("merged")
    high_ready = sig("weights_high")
    low_ready = sig("weights_low")
    h_saved = ctx.enter_context(nc.semaphore("h_saved"))
    h_back = ctx.enter_context(nc.semaphore("h_back"))
    dft_in = ctx.enter_context(nc.semaphore("dft_in"))
    H_DRAM = [nc.dram_tensor(f"h_{x}", [P, DT * TOK], FP32, kind="Internal").ap() for x in ("high", "low")]

    def stage():
        return nc.Block()

    waits_passed = {e: ctx.enter_context(nc.semaphore(f"waits_passed_{e}")) for e in ("pe", "dve", "pool")}

    def hold(eng, name="pe"):
        eng.sem_inc(waits_passed[name], 1)

    rows_loaded = {"n": 0}

    GROUPS = N_BMOD // 4

    def modulation_weights(l):
        halves = [ins["w_mod"][l][a:a + D // 2] for a in (0, D // 2)]
        return Chunks([k_tiles(half, c, c + 4 * P) for c in range(0, 6 * D, 4 * P) for half in halves],
                      [(i // 2, i % 2 * 2, 2, 0, 4 * P) for i in range(4 * GROUPS)], lambda c: slot_used(c + 1))

    w_modulation = modulation_weights(0)
    tokens_in = carve(WORK, 0, 4, D)
    c_rows = carve(WORK, 4 * D, P)[0:2 * DT]
    with stage() as block:
        @block.sync
        def _(sp):
            sp.dma_start(tokens_in[:, 0:2], ins["ctx"][0].rearrange("(t p) d -> p t d", p=P)).then_inc(consts_in, 16)
            sp.dma_start(tokens_in[:, 2:4], ins["x"][0].rearrange("(t p) d -> p t d", p=P)).then_inc(consts_in, 16)
            sp.dma_start(ident[:], ins["ident"]).then_inc(consts_in, 16)
            sp.dma_start(head_ones[:], ins["head_ones"]).then_inc(consts_in, 16)
            sp.dma_start(eye_heads[:], ins["eye_heads"]).then_inc(consts_in, 16)
            sp.dma_start(rope[:], ins["rope"]).then_inc(consts_in, 16)
            sp.dma_start(pick_heads[:].rearrange("p j g -> p (j g)"), ins["pick_heads"]).then_inc(consts_in, 16)
            sp.dma_start(spread_heads[:].rearrange("g j p -> g (j p)"), ins["spread_heads"]).then_inc(consts_in, 16)
            sp.dma_start(masks[:].rearrange("p d m n -> p (d m n)"), ins["masks"]).then_inc(consts_in, 16)
            sp.dma_start(c_rows[0:DT, :], ins["c_ctx"].rearrange("(k p) -> k p", p=P)).then_inc(consts_in, 16)
            sp.dma_start(c_rows[DT:2 * DT, :], ins["c"][0].rearrange("(k p) -> k p", p=P)).then_inc(consts_in, 16)
            w_modulation.start(sp, SLOTS)

        @block.gpsimd
        def _(pool):
            nc.gpsimd.memset(ones[:], 1.0)
            pool_sig.mark(nc.gpsimd.memset(pick[:], 0.0))
            pool.wait_ge(*pool_sig(1))
            nc.gpsimd.memset(pick[:, 2 * HEADS - 1:2 * HEADS], 1.0)

        @block.tensor
        def _(pe):
            pe.wait_ge(consts_in, 16 * 11)
            for k in range(DT):
                for t in range(4):
                    last = nc.tensor.transpose(BANK[:, k, t * P:(t + 1) * P], tokens_in[:, t, k * P:(k + 1) * P], ident[:])
                rows_turned.mark(last)
            pe.wait_ge(*turned_out(1))
            rows_turned.mark(nc.tensor.transpose(BANK[:, 0, 0:2 * DT], c_rows, ident[0:2 * DT, 0:2 * DT]))

        @block.vector
        def _(dve):
            for k in range(DT):
                dve.wait_ge(*rows_turned(k + 1))
                turned_out.mark(nc.vector.tensor_copy(X[:, k], BANK[:, k]))
            dve.wait_ge(*act_sig(2))
            nc.vector.tensor_tensor(SILU_C[1], silu_c[:], SILU_C[0].bitcast(FP32), ALU.subtract)

        @block.scalar
        def _(act):
            act.wait_ge(*rows_turned(DT + 1))
            act_sig.mark(nc.scalar.activation(silu_c[:].rearrange("p k s -> p s k"),
                                              BANK[:, 0, 0:2 * DT].rearrange("p (s k) -> p s k", s=2), ACT.Silu))
            act.wait_ge(*act_sig(1))
            act_sig.mark(nc.scalar.activation(SILU_C[0], silu_c[:], ACT.Copy))
    Signal.end_stage()

    def modulation(l, w, ahead):
        mod_rows = carve(WORK, 0, 4, 4 * P)
        n0 = rows_loaded["n"]
        rows_loaded["n"] += len(VEC_ROWS) + 1
        with stage() as block:
            @block.sync
            def _(sp):
                w.issue(sp, ahead)

            @block.gpsimd
            def _(pool):
                pool.dma_start(vec_rows[0:N_BMOD, 0, :], ins["b_mod"][l].rearrange("(k p) -> k p", p=P)).then_inc(rows_in, 16)
                for name, k in VEC_ROWS:
                    at = VEC_AT[name][0]
                    src = ins[name][l]
                    if len(src.shape) == 2:
                        src = src.rearrange("a b -> (a b)")
                    pool.dma_start(vec_rows[at:at + k, 1, :], src.rearrange("(k p) -> k p", p=P)).then_inc(rows_in, 16)
                pool.dma_start(w2_sb[:], ins["w2"][l].rearrange("d r c -> (d r) c")).then_inc(small_in, 16)
                pool.dma_start(a2_sb[:], ins["a2"][l].rearrange("d r c -> (d r) c")).then_inc(small_in, 16)
                pool.dma_start(g2_sb[:], ins["g2"][l]).then_inc(small_in, 16)
                pool.dma_start(g_head[:, 0:1], ins["g_qn"][l].rearrange("(a b) -> a b", b=1)).then_inc(small_in, 16)
                pool.dma_start(g_head[:, 1:2], ins["g_kn"][l].rearrange("(a b) -> a b", b=1)).then_inc(small_in, 16)
                pool.wait_ge(small_in, 16 * 5 * (l + 1))

            @block.tensor
            def _(pe):
                for g in range(GROUPS + 1):
                    if g < GROUPS:
                        if g >= 4:
                            pe.wait_ge(*evacuated(g - 3))
                        for c in range(4):
                            wc = w.arrived(pe, 4 * g + c)
                            for k in range(2):
                                last = product3(BANK[0:2, 4 + g % 4], [x[:, 2 * c + k] for x in SILU_C], [x[:, k] for x in wc],
                                                c + k == 0, c == 3 and k == 1)
                            slot_used.mark(last)
                    if g >= 1:
                        pe.wait_ge(*evacuated(g))
                        for q in range(4):
                            m = 4 * (g - 1) + q
                            last = nc.tensor.transpose(BANK[:, 2, 2 * m:2 * m + 2], mod_rows[0:2, (g - 1) % 4, q * P:(q + 1) * P], ident[0:2, 0:2])
                        turned_out.mark(last)
                    if g == GROUPS // 2:
                        pe.wait_ge(rows_in, 16 * (n0 + len(VEC_ROWS) + 1))
                        rows_turned.mark(nc.tensor.transpose(BANK[:, 0, 0:N_BMOD], vec_rows[0:N_BMOD, 0, :], ident[0:N_BMOD, 0:N_BMOD]))
                        rows_turned.mark(nc.tensor.transpose(BANK[:, 1, 0:N_VEC], vec_rows[0:N_VEC, 1, :], ident[0:N_VEC, 0:N_VEC]))

            @block.scalar
            def _(act):
                for c in range(CHUNKS):
                    w.high(act, c)
                for g in range(GROUPS):
                    for c in range(4):
                        w.high(act, 4 * g + c + CHUNKS)
                    act.wait_ge(*slot_used(4 * g + 4))
                    if g >= 4:
                        act.wait_ge(*turned_out(g - 3))
                    evacuated.mark(nc.scalar.activation(mod_rows[0:2, g % 4], BANK[0:2, 4 + g % 4], ACT.Copy))

            @block.vector
            def _(dve):
                for c in range(4 * GROUPS):
                    w.low(dve, c)
                dve.wait_ge(*rows_turned(1))
                dve_sig.mark(nc.vector.tensor_copy(bmod[:], BANK[:, 0, 0:N_BMOD]))
                dve.wait_ge(*rows_turned(2))
                dve_sig.mark(nc.vector.tensor_copy(vec[:], BANK[:, 1, 0:N_VEC]))
                dve.wait_ge(*dve_sig(2))
                mp, mn = VEC_AT["mu_prev"][0], VEC_AT["mu_next"][0]
                dve_sig.mark(nc.vector.tensor_tensor(mu_self[:], vec[:, mp:mp + Z_TILES], vec[:, mn:mn + Z_TILES], ALU.add))
                ka = VEC_AT["k_a"][0]
                dve_sig.mark(nc.vector.tensor_scalar(ka_rest[:], vec[:, ka:ka + PAIRS], -1.0, 1.0, ALU.mult, ALU.add))
                dve.wait_ge(*dve_sig(4))
                nc.vector.tensor_scalar(mu_self[:], mu_self[:], -1.0, 1.0, ALU.mult, ALU.add)
                dve.wait_ge(*turned_out(GROUPS))
                flat = mod[:].rearrange("p q k s -> p (q k) s")
                dve_sig.mark(nc.vector.tensor_tensor(flat, BANK[:, 2, 0:2 * N_BMOD].rearrange("p (m s) -> p m s", s=2),
                                                     bmod[:].unsqueeze(2).to_broadcast([P, N_BMOD, 2]), ALU.add))
                dve.wait_ge(*dve_sig(5))
                for which, dst, g in ((1, scale_1, "g_norm1"), (4, scale_2, "g_norm2")):
                    at = VEC_AT[g][0]
                    dve_sig.mark(nc.vector.tensor_scalar(dst[:], mod[:, which], 1.0, None, ALU.add))
                    dve.wait_ge(*dve_sig(6 if which == 1 else 7))
                    nc.vector.tensor_tensor(dst[:], dst[:], vec[:, at:at + DT].unsqueeze(2).to_broadcast([P, DT, 2]), ALU.mult)
        Signal.end_stage()

    def norm(scale, shift, t0, ahead, save=False):
        n = TOK - t0
        sq = carve(WORK, 0, DT, TOK)
        rms = carve(WORK, DT * TOK, TOK)
        segs = [s for s in range(2) if s * CTX >= t0]
        cells = [(k, s) for k in range(DT) for s in segs]
        with stage() as block:
            @block.scalar
            def _(act):
                for k in range(DT):
                    squares.mark(nc.scalar.activation(sq[:, k, t0:], X[:, k, t0:], ACT.Square))
                ahead.high_ahead(act)
                act.wait_ge(*dve_sig(2))
                inverse_rms.mark(nc.scalar.activation(rms[:, t0:], rms[:, t0:], ACT.Sqrt))
                for i, (k, s) in enumerate(cells):
                    a, b = s * CTX, (s + 1) * CTX
                    act.wait_ge(*scaled(i + 1))
                    gate_ready.mark(nc.scalar.activation(HS[0][:, k, a:b], sq[:, k, a:b], ACT.Identity, bias=shift[:, k, s:s + 1]))


            @block.tensor
            def _(pe):
                for k in range(DT):
                    pe.wait_ge(*squares(k + 1))
                    last = nc.tensor.matmul(BANK[:, 0, 0:n], ones[:], sq[:, k, t0:], start=(k == 0), stop=(k == DT - 1))
                sums.mark(last)
                w0 = ahead.part(0, 0), ahead.part(1, 0)
                pe.wait_ge(*low_ready(1))
                for k in range(DT):
                    i = len(segs) * (k + 1)
                    pe.wait_ge(*gate_ready(i))
                    pe.wait_ge(*h_ready(i - i // 3))
                    if i // 3:
                        pe.wait_ge(*evacuated(i // 3))
                    product3(BANK[:, 0, 0:n], [x[:, k] for x in w0], [x[:, k, t0:] for x in HS], k == 0, k == DT - 1)

            @block.vector
            def _(dve):
                ahead.low_ahead(dve)
                dve.wait_ge(*sums(1))
                dve_sig.mark(nc.vector.tensor_scalar(rms[:, t0:], BANK[:, 0, 0:n], 1.0 / D, RMS_EPS, ALU.mult, ALU.add))
                dve.wait_ge(*dve_sig(1))
                dve_sig.mark(nc.vector.reciprocal(rms[:, t0:], rms[:, t0:]))
                dve.wait_ge(*inverse_rms(1))
                LAG = 3
                lows = [i for i in range(len(cells)) if i % 3 != 2]
                for i in range(len(cells) + LAG):
                    if i < len(cells):
                        k, s = cells[i]
                        a, b = s * CTX, (s + 1) * CTX
                        scaled.mark(nc.vector.scalar_tensor_tensor(sq[:, k, a:b], X[:, k, a:b], scale[:, k, s:s + 1],
                                                                   rms[:, a:b], ALU.mult, ALU.mult))
                    if i >= LAG and i - LAG in lows:
                        k, s = cells[i - LAG]
                        a, b = s * CTX, (s + 1) * CTX
                        dve.wait_ge(*gate_ready(i - LAG + 1))
                        h_ready.mark(nc.vector.scalar_tensor_tensor(HS[1][:, k, a:b], sq[:, k, a:b], shift[:, k, s:s + 1],
                                                                    HS[0][:, k, a:b].bitcast(FP32), ALU.add, ALU.subtract))

            @block.gpsimd
            def _(pool):
                for i, (k, s) in enumerate(cells):
                    if i % 3 == 2:
                        a, b = s * CTX, (s + 1) * CTX
                        pool.wait_ge(*gate_ready(i + 1))
                        pool_sig.mark(nc.gpsimd.tensor_scalar(sq[:, k, a:b], sq[:, k, a:b], shift[:, k, s:s + 1], None, ALU.add))
                        pool.wait_ge(*pool_sig(i // 3 + 1))
                        evacuated.mark(nc.gpsimd.tensor_tensor(HS[1][:, k, a:b], sq[:, k, a:b], HS[0][:, k, a:b].bitcast(FP32), ALU.subtract))

            @block.sync
            def _(sp):
                if save:
                    sp.wait_ge(*h_ready(len(cells) - len(cells) // 3))
                    sp.wait_ge(*evacuated(len(cells) // 3))
                    for x in range(2):
                        sp.dma_start(H_DRAM[x], HS[x].bitcast(FP32).rearrange("p k t -> p (k t)")).then_inc(h_saved, 16)
        ahead.early = CHUNKS
        Signal.end_stage()

    Z = carve(WORK, 0, Z_TILES, TOK)

    def rwkv_weights(l):
        return Chunks([k_tiles(ins["w_in"][l], c, min(c + 2 * P, N_RWKV_IN)) for c in range(0, N_RWKV_IN, 2 * P)],
                      [(m // 2, 0, DT, (m % 2) * P, P) for m in range(Z_TILES)], lambda c: product(c + 1))

    def project_rwkv(l, w):
        with stage() as block:
            @block.sync
            def _(sp):
                w.issue(sp)
                sp.wait_ge(h_saved, 32 * (l + 1))

            @block.tensor
            def _(pe):
                product.count(pe)
                for m in range(1, Z_TILES):
                    wm = w.arrived(pe, m)
                    if m >= 4:
                        pe.wait_ge(*evacuated(m - 3))
                    for k in range(DT):
                        last = product3(BANK[:, m % 4], [x[:, k] for x in wm], [x[:, k] for x in HS], k == 0, k == DT - 1)
                    product.mark(last)

            @block.scalar
            def _(act):
                for c in range(CHUNKS):
                    w.high(act, c)
                for m in range(Z_TILES):
                    act.wait_ge(*product(m + 1))
                    first_cut.mark(nc.scalar.activation(Z[:, m], BANK[:, m % 4], ACT.Copy, scale=mu_self[:, m:m + 1]))
                    w.high(act, m + CHUNKS)

            @block.vector
            def _(dve):
                for c in range(CHUNKS):
                    w.low(dve, c)
                for m in range(Z_TILES):
                    z = Z[:, m].rearrange("p (s t) -> p s t", s=2)
                    raw = BANK[:, m % 4].rearrange("p (s t) -> p s t", s=2)
                    dve.wait_ge(*first_cut(m + 1))
                    dve_sig.mark(nc.vector.scalar_tensor_tensor(z[:, :, 1:], raw[:, :, :SEQ - 1], v("mu_prev", m), z[:, :, 1:],
                                                                ALU.mult, ALU.add))
                    dve.wait_ge(*dve_sig(m + 1))
                    evacuated.mark(nc.vector.scalar_tensor_tensor(z[:, :, :SEQ - 1], raw[:, :, 1:], v("mu_next", m),
                                                                  z[:, :, :SEQ - 1], ALU.mult, ALU.add))
                    w.low(dve, m + CHUNKS)
        Signal.end_stage()

    F0 = Z_TILES * TOK
    KK = carve(WORK, F0, PAIRS, TOK)
    KD = [carve(WORK, F0 + (1 + d) * WIDTH * 4, PAIRS, TOK) for d in range(NDIR)]
    BB = [carve(WORK, F0 + (3 + d) * WIDTH * 4, PAIRS, TOK) for d in range(NDIR)]
    INCL = [carve(WORK, F0 + (5 + d) * WIDTH * 4, PAIRS, TOK) for d in range(NDIR)]
    EXCL = [carve(WORK, F0 + (7 + d) * WIDTH * 4, PAIRS, TOK) for d in range(NDIR)]
    WORK_USED = F0 + 9 * WIDTH * 4
    Y = carve(WORK, Z_K * TOK, PAIRS, TOK)

    r_flat = RING.rearrange("p s n -> p (s n)")

    def features():
        sqk = carve(r_flat, 0, PAIRS, TOK)
        head_rows = carve(r_flat, PAIRS * TOK, TOK)[0:HEADS]
        chunk_start = carve(r_flat, (PAIRS + 1) * TOK, TOK)
        gate_w = carve(r_flat, (PAIRS + 2) * TOK, 2, NDIR, WIDTH)
        of_dir = lambda d: slice(d * HD, (d + 1) * HD)
        with stage() as block:
            @block.gpsimd
            def _(pool):
                for x in range(2):
                    high_ready.mark(nc.gpsimd.memset(gate_w[:, x], 0.0))
                pool_sig.mark(nc.gpsimd.memset(chunk_start, 1.0))
                pool.wait_ge(*pool_sig(1))
                pool_sig.mark(nc.gpsimd.memset(chunk_start.rearrange("p (c t) -> p c t", t=CHUNK)[:, :, 0:1], 0.0))
                for j in range(PAIRS):
                    for d in range(NDIR):
                        pool.wait_ge(*h_ready(NDIR * j + d + 1))
                        nc.gpsimd.tensor_tensor(KD[d][:, j], KD[d][:, j], Z[:, Z_K + j], ALU.mult)

            @block.scalar
            def _(act):
                act_sig.mark(nc.scalar.activation(Z[:, Z_W], Z[:, Z_W], ACT.Tanh))
                for j in range(PAIRS):
                    act.wait_ge(*scaled(j + 1))
                    squares.mark(nc.scalar.activation(sqk[:, j], KK[:, j], ACT.Square))
                act.wait_ge(*sums(1))
                first_cut.mark(nc.scalar.activation(head_rows, BANK[0:HEADS, 4], ACT.Sqrt))
                n = 0
                for out, bias in ((EXCL, "w0"), (BB, "a0")):
                    for j in range(PAIRS):
                        for d in range(NDIR):
                            n += 1
                            act.wait_ge(*product(n))
                            gate_ready.mark(nc.scalar.activation(out[d][:, j], BANK[:, n % 4], ACT.Sigmoid, bias=v(bias, d * PAIRS + j)))
                act_sig.mark(nc.scalar.activation(Z[:, Z_G], Z[:, Z_G], ACT.Sigmoid))

            @block.tensor
            def _(pe):
                for j in range(PAIRS):
                    pe.wait_ge(*squares(j + 1))
                    last = nc.tensor.matmul(BANK[0:HEADS, 4], pick_heads[:, j], sqk[:, j], start=(j == 0), stop=(j == PAIRS - 1))
                sums.mark(last)
                n = 0
                for x, z in enumerate((Z_W, Z_A)):
                    pe.wait_ge(*low_ready(x + 1))
                    for j in range(PAIRS):
                        for d in range(NDIR):
                            n += 1
                            if n == 1:
                                pe.wait_ge(*act_sig(1))
                            if n > 4:
                                pe.wait_ge(*gate_ready(n - 4))
                            product.mark(nc.tensor.matmul(BANK[:, n % 4], gate_w[:, x, d, j * P:(j + 1) * P], Z[:, z], start=True, stop=True))
                    if x == 0:
                        pe.wait_ge(*inverse_rms(1))
                        for j in range(PAIRS):
                            merged.mark(nc.tensor.matmul(BANK[:, 4 + j], spread_heads[:, j], head_rows, start=True, stop=True))

            @block.vector
            def _(dve):
                for j in range(PAIRS):
                    scaled.mark(nc.vector.tensor_scalar(KK[:, j], Z[:, Z_K + j], v("k_k", j), None, ALU.mult))
                for x, w in enumerate((w2_sb, a2_sb)):
                    dve.wait_ge(*high_ready(x + 1))
                    for d in range(NDIR):
                        last = nc.vector.tensor_copy(gate_w[of_dir(d), x, d], w[of_dir(d)])
                    low_ready.mark(last)
                dve.wait_ge(*first_cut(1))
                dve_sig.mark(nc.vector.tensor_scalar(head_rows, head_rows, 1e-12, None, ALU.max))
                dve.wait_ge(*dve_sig(1))
                inverse_rms.mark(nc.vector.reciprocal(head_rows, head_rows))
                dve.wait_ge(*pool_sig(2))
                c = 1
                for d in range(NDIR):
                    for j in range(PAIRS):
                        dve.wait_ge(*gate_ready(NDIR * j + d + 1))
                        c += 1
                        dve_sig.mark(nc.vector.tensor_tensor_scan(INCL[d][:, j], chunk_start, EXCL[d][:, j], 0.0, ALU.mult, ALU.add))
                    dve.wait_ge(*dve_sig(c))
                    nc.vector.tensor_tensor(EXCL[d], INCL[d], EXCL[d], ALU.subtract)
                for j in range(PAIRS):
                    dve.wait_ge(*merged(j + 1))
                    c += 1
                    dve_sig.mark(nc.vector.tensor_tensor(KK[:, j], KK[:, j], BANK[:, 4 + j], ALU.mult))
                dve.wait_ge(*dve_sig(c))
                for j in range(PAIRS):
                    for d in range(NDIR):
                        dve.wait_ge(*gate_ready(NDIR * PAIRS + NDIR * j + d + 1))
                        h_ready.mark(nc.vector.tensor_scalar(KD[d][:, j], BB[d][:, j], v("k_a", j), ka_rest[:, j:j + 1], ALU.mult, ALU.add))
                        dve.wait_ge(*h_ready(NDIR * j + d + 1))
                        nc.vector.tensor_tensor(BB[d][:, j], BB[d][:, j], KK[:, j], ALU.mult)
        Signal.end_stage()

    HALF = PAIRS * HD
    free = [(r_flat, 0, SLOTS * SLOT), (WORK, Z_W * TOK, Z_G * TOK), (WORK, WORK_USED, WORK_N)]

    def scratch(*shape):
        n = 1
        for s in shape:
            n *= s
        for i, (mem, at, end) in enumerate(free):
            if at + n <= end:
                free[i] = (mem, at + n, end)
                return carve(mem, at, *shape)
        raise ValueError(f"no room for {shape}: {[(a, e) for _, a, e in free]}")

    QR = [scratch(PAIRS, 2, HD) for _ in range(NDIR)]
    BK = [scratch(2, PAIRS, HD) for _ in range(NDIR)]
    VF = [scratch(PAIRS, HD) for _ in range(NDIR)]
    T2 = [scratch(2, PAIRS, HD) for _ in range(NDIR)]
    QRG = [scratch(HEADS, 2, HD) for _ in range(NDIR)]
    STATE_V = [scratch(HEADS, HD) for _ in range(NDIR)]
    SA_V = [scratch(HEADS, HD) for _ in range(NDIR)]
    BK_TOK = [scratch(HEADS, HD) for _ in range(NDIR)]
    ARB = [scratch(HEADS, HD) for _ in range(NDIR)]
    SD = [scratch(HEADS, HD) for _ in range(NDIR)]
    EXPO = scratch(2, PAIRS, HD)
    EXPS = [scratch(3, PAIRS, HD) for _ in range(NDIR)]
    LTS = [scratch(PAIRS, HD) for _ in range(NDIR)]
    LM = [scratch(PAIRS, HD) for _ in range(NDIR)]
    X1 = [scratch(PAIRS, HD) for _ in range(NDIR)]
    WS = [scratch(PAIRS, HD) for _ in range(NDIR)]
    UP, DOWN = slice(0, HD), slice(HD, P)

    s_expo = sig("exponents_ready")
    s_exp = sig("exps_ready")
    s_exp_used = [sig(f"exps_used_{i}") for i in range(2)]
    s_qr = [sig(f"qr_ready_{d}") for d in range(NDIR)]
    s_ops = [sig(f"operands_ready_{d}") for d in range(NDIR)]
    s_qr2 = [sig(f"qr_kept_{d}") for d in range(NDIR)]
    s_gram = [sig(f"gram_{d}") for d in range(NDIR)]
    s_lts = [sig(f"lt_kept_{d}") for d in range(NDIR)]
    s_gram_out = [sig(f"gram_out_{d}") for d in range(NDIR)]
    s_bk_tok = [sig(f"bk_token_major_{d}") for d in range(NDIR)]
    s_v = [sig(f"values_kept_{d}") for d in range(NDIR)]
    s_v_tok = [sig(f"v_token_major_{d}") for d in range(NDIR)]
    s_lm = [sig(f"level_mask_{d}") for d in range(NDIR)]
    s_x1 = [sig(f"x1_product_{d}") for d in range(NDIR)]
    s_x1_out = [sig(f"x1_out_{d}") for d in range(NDIR)]
    s_tx = [sig(f"merge_product_{d}") for d in range(NDIR)]
    s_t = [sig(f"inverse_merged_{d}") for d in range(NDIR)]
    s_w = [sig(f"w_product_{d}") for d in range(NDIR)]
    s_w_out = [sig(f"w_out_{d}") for d in range(NDIR)]
    s_sa_v = [sig(f"values_doubled_{d}") for d in range(NDIR)]
    s_sa = [sig(f"sa_product_{d}") for d in range(NDIR)]
    s_sa_out = [sig(f"sa_out_{d}") for d in range(NDIR)]
    s_y = [sig(f"y_product_{d}") for d in range(NDIR)]
    s_add = [sig(f"state_product_decayed_{d}") for d in range(NDIR)]
    s_ds = [sig(f"state_product_{d}") for d in range(NDIR)]
    s_y_out = [sig(f"y_added_{d}") for d in range(NDIR)]
    s_sd = [sig(f"state_decayed_{d}") for d in range(NDIR)]
    s_st = [sig(f"state_new_{d}") for d in range(NDIR)]
    s_init = sig("state_cleared")
    y_clear = sig("y_cleared")
    s_first = [sig(f"first_level_{d}") for d in range(NDIR)]

    scan_signals = [s_expo, s_exp, s_init, *s_qr, *s_ops, *s_qr2, *s_gram, *s_lts, *s_gram_out, *s_bk_tok, *s_add, *s_v, *s_v_tok, *s_sa_v, *s_lm, *s_x1, *s_x1_out,
                    *s_tx, *s_t, *s_w, *s_w_out, *s_sa, *s_sa_out, *s_y, *s_ds, *s_y_out, *s_sd, *s_st, *s_first]
    with stage() as block:
        @block.sync
        def _(sp):
            for s in scan_signals:
                sp.sem_inc(s.sem, 1)
                s.made += 1
    Signal.end_stage()

    NL = LEVELS - 1
    N = SEG_CHUNKS

    def lanes(mask):
        return mask.unsqueeze(1).to_broadcast([P, PAIRS, HD])

    STEPS = 2 * N

    def chunk_of(d, i):
        return CHUNK * i if d == 0 else (CHUNK * (N - 1) + (TOK - CHUNK) * i) % TOK

    def scan(context_y):
        y0 = 0 if context_y else N

        def tokens(eng, d, i):
            t = chunk_of(d, i)
            return t if isinstance(i, int) else eng.snap(t, min_val=0, max_val=TOK - CHUNK)

        def run(eng, step):
            for first, end, need_y in ((0, N, context_y), (N, STEPS - 1, True)):
                Signal.trips = end - first
                with eng.Fori(first, end) as i:
                    step(i, need_y, True)
                Signal.trips = 1
            step(STEPS - 1, True, False)

        def level_mask(d, l):
            return masks[:, d, 1 + l]

        def at_step(s, i, k=1, n=0):
            return s.sem, s.base + k * i + n

        first_half = lambda d: slice(HD // 2 * d, HD // 2 * (d + 1))
        later_half = lambda d: first_half(1 - d)

        def of_head(h, half):
            return slice(h * HD + half.start, h * HD + half.stop)

        B_L, B_LT, B_G, B_S = 0, 1, 2, 3
        by_head = lambda tile, h: (tile.rearrange("p (j h) t -> p j h t", h=2)[:, :, h] if len(tile.shape) == 3 else
                                   tile.rearrange("p (j h) q t -> p j h q t", h=2)[:, :, h])
        pairs = lambda bank, a: BANK[:, bank, a:a + HALF].rearrange("p (j t) -> p j t", j=PAIRS)
        with stage() as block:
            @block.gpsimd
            def _(pool):
                def operands(i, t, d):
                    pool.wait_ge(*at_step(s_gram[d], i, 3))
                    pool.wait_ge(*at_step(s_bk_tok[d], i))
                    pool.wait_ge(*at_step(s_exp, i, 2, d + 1))
                    hold(pool, "pool")
                    s_ops[d].mark(nc.gpsimd.tensor_tensor(BK[d][:, 1], KD[d][:, :, bass.ds(t, CHUNK)], EXPS[d][:, 2], ALU.mult))

                def step(i, need_y, more):
                    t = [tokens(pool, d, i + 1) for d in range(NDIR)] if more else None
                    for d in range(NDIR):
                        pool.wait_ge(*at_step(s_st[d], i))
                        pool.wait_ge(*at_step(s_exp, i, 2, d + 1))
                        hold(pool, "pool")
                        nc.gpsimd.tensor_copy(DEC_KEPT[d][:], DEC[d][:])
                        s_sd[d].mark(nc.gpsimd.tensor_tensor(SD[d][UP], STATE_V[d][UP], DEC[d][:].unsqueeze(2).to_broadcast([HD, HEADS, HD]), ALU.mult))
                    for l in range(1, LEVELS):
                        for d in range(NDIR):
                            if l == 1:
                                pool.wait_ge(*at_step(s_lts[d], i, 1, 1))
                            pool.wait_ge(*at_step(s_x1[d], i, NL, l - 1))
                            s_lm[d].mark(nc.gpsimd.tensor_tensor(LM[d], LTS[d], lanes(level_mask(d, l)), ALU.mult))
                        if more and l in (3, 5):
                            d = (l - 3) // 2
                            operands(i + 1, t[d], d)

                pool.wait_ge(*s_init(1))
                for d in range(NDIR):
                    operands(0, chunk_of(d, 0), d)
                y_clear.mark(nc.gpsimd.memset(Y, 0.0))
                run(pool, step)

            @block.scalar
            def _(act):
                def exps(i, t, d):
                    if d == 1:
                        act.wait_ge(*at_step(s_expo, i, 1, 1))
                    act.wait_ge(*at_step(s_ops[d], i))
                    act.wait_ge(*at_step(s_qr[d], i))
                    at = bass.ds(t, CHUNK)
                    e = EXPS[d]
                    excl = EXCL[0][:, :, at] if d == 0 else EXPO[:, 1]
                    incl = INCL[0][:, :, at] if d == 0 else EXPO[:, 0]
                    nc.scalar.activation(e[:, 0], excl, ACT.Exp, scale=-KAPPA)
                    nc.scalar.activation(e[:, 1], incl, ACT.Exp, scale=-KAPPA)
                    nc.scalar.activation(e[:, 2], incl, ACT.Exp, scale=KAPPA)
                    act.wait_ge(*at_step(s_sd[d], i))
                    for h, rows in enumerate((UP, DOWN)):
                        last = nc.scalar.activation(DEC[d][:].rearrange("p (j h) -> p j h", h=2)[:, :, h:h + 1],
                                                    INCL[d][rows, :, bass.ds(t + (CHUNK - 1), 1)], ACT.Exp, scale=-KAPPA)
                    s_exp.mark(last)

                def step(i, need_y, more):
                    here = [tokens(act, d, i) for d in range(NDIR)]
                    t = [tokens(act, d, i + 1) for d in range(NDIR)] if more else None
                    for d in range(NDIR):
                        act.wait_ge(*at_step(s_gram[d], i, 3, 1))
                        act.wait_ge(*at_step(s_lm[d], i, NL))
                        s_lts[d].mark(nc.scalar.activation(LTS[d], BANK[:, 4 * d + B_LT].rearrange("p (j q t) -> p j q t", j=PAIRS, q=2)[:, :, 0], ACT.Copy))
                    for d in range(NDIR):
                        act.wait_ge(*at_step(s_v_tok[d], i))
                        s_v[d].mark(nc.scalar.activation(VF[d], Z[:, Z_V:Z_V + PAIRS, bass.ds(here[d], CHUNK)], ACT.Copy))
                    for l in range(1, LEVELS):
                        for d in range(NDIR):
                            act.wait_ge(*at_step(s_x1[d], i, NL, l))
                            cols = slice(0, HD) if l < NL else first_half(d)
                            s_x1_out[d].mark(nc.scalar.activation(X1[d][:, :, cols], pairs(4 * d + B_L, 0)[:, :, cols], ACT.Copy))
                        if more and l in (2, 4):
                            exps(i + 1, t[l // 2 - 1], l // 2 - 1)
                        if l >= 4:
                            d = l - 4
                            act.wait_ge(*at_step(s_v_tok[d], i, 1, 1))
                            act.wait_ge(*at_step(s_ds[d], i))
                            s_sa_v[d].mark(nc.scalar.activation(SA_V[d][DOWN], STATE_V[d][DOWN], ACT.Copy))
                    for d in range(NDIR):
                        act.wait_ge(*at_step(s_w[d], i, 1, 1))
                        s_w_out[d].mark(nc.scalar.activation(WS[d], pairs(4 * d + B_L, 0), ACT.Copy))
                    for d in range(NDIR):
                        act.wait_ge(*at_step(s_sa[d], i, 1, 1))
                        for h, rows in enumerate((UP, DOWN)):
                            last = nc.scalar.activation(by_head(SA_V[d][UP], h), pairs(4 * d + B_LT, 0)[rows], ACT.Copy, scale=-1.0)
                        s_sa_out[d].mark(last)

                for d in range(NDIR):
                    exps(0, chunk_of(d, 0), d)
                run(act, step)

            @block.vector
            def _(dve):
                def exponents(i, t):
                    at = bass.ds(t, CHUNK)
                    whole = INCL[1][:, :, bass.ds(t + (CHUNK - 1), 1)].to_broadcast([P, PAIRS, CHUNK])
                    dve.wait_ge(*at_step(s_exp, i, 2))
                    hold(dve, "dve")
                    nc.vector.tensor_tensor(EXPO[:, 0], whole, EXCL[1][:, :, at], ALU.subtract)
                    s_expo.mark(nc.vector.tensor_tensor(EXPO[:, 1], whole, INCL[1][:, :, at], ALU.subtract))

                def turn(dst, src):
                    B = HD // 2
                    for h in range(2):
                        for f in range(0, HD, B):
                            for t in range(0, HD, B):
                                last = nc.vector.transpose(by_head(dst, h)[t:t + B, :, f:f + B],
                                                           src[h * HD + f:h * HD + f + B, :, t:t + B])
                    return last

                def turn_bk(i, d):
                    dve.wait_ge(*at_step(s_ops[d], i, 1, 1))
                    dve.wait_ge(*at_step(s_qr[d], i, 1, 1))
                    dve.wait_ge(*at_step(s_ds[d], i))
                    turn(BK_TOK[d][UP], BK[d][:, 0])
                    s_bk_tok[d].mark(turn(BK_TOK[d][DOWN], BK[d][:, 1]))

                def turn_v(i, d):
                    dve.wait_ge(*at_step(s_v[d], i, 1, 1))
                    dve.wait_ge(*at_step(s_ds[d], i))
                    dve.wait_ge(*at_step(s_sa_v[d], i))
                    s_v_tok[d].mark(turn(STATE_V[d][DOWN], VF[d]))

                def operands(i, t, d):
                    at = bass.ds(t, CHUNK)
                    e = EXPS[d]
                    dve.wait_ge(*at_step(s_exp, i, 2, d + 1))
                    dve.wait_ge(*at_step(s_gram[d], i, 3))
                    dve.wait_ge(*at_step(s_bk_tok[d], i))
                    hold(dve, "dve")
                    nc.vector.tensor_tensor(BK[d][:, 0], BB[d][:, :, at], e[:, 2], ALU.mult)
                    nc.vector.tensor_tensor(QR[d][:, :, 0], KK[:, :, at], e[:, 0], ALU.mult)
                    s_qr[d].mark(nc.vector.tensor_tensor(QR[d][:, :, 1], Z[:, Z_R:Z_R + PAIRS, at], e[:, 1], ALU.mult))

                def keep(i, d):
                    dve.wait_ge(*at_step(s_ds[d], i))
                    dve.wait_ge(*at_step(s_qr[d], i, 1, 1))
                    for h, rows in enumerate((UP, DOWN)):
                        last = nc.vector.tensor_copy(by_head(QRG[d][UP], h), QR[d][rows])
                    s_qr2[d].mark(last)

                def step(i, need_y, more):
                    here = [tokens(dve, d, i) for d in range(NDIR)] if need_y else None
                    t = [tokens(dve, d, i + 1) for d in range(NDIR)] if more else None
                    for d in range(NDIR):
                        lt = BANK[:, 4 * d + B_LT].rearrange("p (j q t) -> p j q t", j=PAIRS, q=2)
                        dve.wait_ge(*at_step(s_lts[d], i, 1, 1))
                        for h, rows in enumerate((UP, DOWN)):
                            nc.vector.tensor_tensor(by_head(ARB[d][UP], h), lt[rows, :, 1],
                                                    masks[rows, d, LEVELS + 2].unsqueeze(1).to_broadcast([HD, PAIRS, HD]), ALU.mult)
                        dve.wait_ge(*at_step(s_gram[d], i, 3, 2))
                        nc.vector.tensor_tensor(T2[d][:, 0], pairs(4 * d + B_L, 0), lanes(masks[:, d, 0]), ALU.mult)
                        s_first[d].mark(nc.vector.tensor_tensor(T2[d][:, 1], LTS[d], lanes(masks[:, d, 1]), ALU.mult))
                        dve.wait_ge(*at_step(s_first[d], i, 1, 1))
                        s_t[d].mark(nc.vector.tensor_tensor(T2[d].rearrange("p q j t -> p (q j) t"), T2[d].rearrange("p q j t -> p (q j) t"),
                                                            eye_heads[:].unsqueeze(1).to_broadcast([P, 2 * PAIRS, HD]), ALU.add))
                    for d in range(NDIR):
                        dve.wait_ge(*at_step(s_gram[d], i, 3, 3))
                        for h, rows in enumerate((UP, DOWN)):
                            last = nc.vector.tensor_tensor(
                                by_head(QRG[d][DOWN], h).rearrange("p j q t -> p j (q t)"),
                                BANK[rows, 4 * d + B_G].rearrange("p (j n) -> p j n", j=PAIRS),
                                masks[rows, d, LEVELS + 1:LEVELS + 3].rearrange("p q t -> p (q t)").unsqueeze(1).to_broadcast([HD, PAIRS, 2 * HD]),
                                ALU.mult)
                        s_gram_out[d].mark(last)
                    for l in range(1, LEVELS):
                        for d in range(NDIR):
                            dve.wait_ge(*at_step(s_tx[d], i, NL, l))
                            dve.wait_ge(*at_step(s_t[d], i, LEVELS, l))
                            if l < LEVELS - 1:
                                s_t[d].mark(nc.vector.tensor_tensor(T2[d].rearrange("p q j t -> p (q j t)"), T2[d].rearrange("p q j t -> p (q j t)"),
                                                                    BANK[:, 4 * d + B_LT], ALU.subtract))
                            else:
                                for h in range(2):
                                    rows, cols = of_head(h, first_half(d)), later_half(d)
                                    last = nc.vector.tensor_tensor(T2[d][rows, 1, :, cols], T2[d][rows, 1, :, cols],
                                                                   pairs(4 * d + B_LT, HALF)[rows, :, cols], ALU.subtract)
                                s_t[d].mark(last)
                        if l in (1, 2):
                            turn_bk(i, l - 1)
                        if l in (3, 4):
                            turn_v(i, l - 3)
                        if more and l == 3:
                            operands(i + 1, t[0], 0)
                            exponents(i + 1, t[1])
                        if more and l == 5:
                            operands(i + 1, t[1], 1)
                    if need_y:
                        dve.wait_ge(*y_clear(1))
                        for d in range(NDIR):
                            at = bass.ds(here[d], CHUNK)
                            dve.wait_ge(*at_step(s_y[d], i - y0, 1, 1))
                            dve.wait_ge(*at_step(s_y_out[1 - d], i - y0, 1, d))
                            hold(dve, "dve")
                            s_y_out[d].mark(nc.vector.tensor_tensor(Y[:, :, at], Y[:, :, at], pairs(4 * d + B_G, 0), ALU.add))
                    for d in range(NDIR):
                        dve.wait_ge(*at_step(s_sd[d], i, 1, 1))
                        dve.wait_ge(*at_step(s_ds[d], i, 1, 1))
                        s_add[d].mark(nc.vector.tensor_tensor(STATE_V[d][UP], BANK[UP, 4 * d + B_S].rearrange("p (g t) -> p g t", g=HEADS),
                                                              DEC_KEPT[d][:].unsqueeze(2).to_broadcast([HD, HEADS, HD]), ALU.mult))
                        dve.wait_ge(*at_step(s_add[d], i, 1, 1))
                        s_st[d].mark(nc.vector.tensor_tensor(STATE_V[d][UP], STATE_V[d][UP], SD[d][UP], ALU.add))
                        if more:
                            keep(i + 1, d)

                nc.vector.memset(STATE_V[0][UP], 0.0)
                s_init.mark(nc.vector.memset(STATE_V[1][UP], 0.0))
                exponents(0, chunk_of(1, 0))
                for d in range(NDIR):
                    operands(0, chunk_of(d, 0), d)
                    keep(0, d)
                run(dve, step)

            @block.tensor
            def _(pe):
                def each(bank, at, width, lhs, rhs):
                    for j in range(PAIRS):
                        for rows in (UP, DOWN):
                            last = nc.tensor.matmul(BANK[rows, bank, at + j * width:at + (j + 1) * width],
                                                    lhs(j)[rows], rhs(j)[rows], start=True, stop=True)
                    return last

                def heads():
                    return [(2 * j + h, j, rows) for j in range(PAIRS) for h, rows in enumerate((UP, DOWN))]

                def halves(bank, at, out_rows, out_cols, lhs, rhs, k_rows):
                    for j in range(PAIRS):
                        for h in range(2):
                            k = of_head(h, k_rows)
                            last = nc.tensor.matmul(BANK[of_head(h, out_rows), bank, at + j * HD + out_cols.start:at + j * HD + out_cols.stop],
                                                    lhs[k, j, out_rows], rhs[k, j, out_cols], start=True, stop=True)
                    return last

                def step(i, need_y, more):
                    for d in range(NDIR):
                        bank = 4 * d
                        q = lambda j: QR[d][:, j, 0]
                        qr = lambda j: QR[d][:, j].rearrange("p q t -> p (q t)")
                        pe.wait_ge(*at_step(s_qr[d], i, 1, 1))
                        pe.wait_ge(*at_step(s_sa_out[d], i))
                        hold(pe)
                        s_gram[d].mark(each(bank + B_LT, 0, 2 * HD, lambda j: BK[d][:, 0, j], qr))
                        s_gram[d].mark(each(bank + B_L, 0, HD, q, lambda j: BK[d][:, 0, j]))
                        pe.wait_ge(*at_step(s_ops[d], i, 1, 1))
                        if need_y:
                            pe.wait_ge(*at_step(s_y_out[d], i - y0))
                        hold(pe)
                        s_gram[d].mark(each(bank + B_G, 0, 2 * HD, lambda j: BK[d][:, 1, j], qr))
                    for l in range(1, LEVELS):
                        for d in range(NDIR):
                            pe.wait_ge(*at_step(s_t[d], i, LEVELS, l))
                            pe.wait_ge(*at_step(s_lm[d], i, NL, l))
                            hold(pe)
                            if l < NL:
                                s_x1[d].mark(each(4 * d + B_L, 0, HD, lambda j: LM[d][:, j], lambda j: T2[d][:, 0, j]))
                            else:
                                s_x1[d].mark(halves(4 * d + B_L, 0, later_half(d), first_half(d), LM[d], T2[d][:, 0], first_half(d)))
                        for d in range(NDIR):
                            pe.wait_ge(*at_step(s_x1_out[d], i, NL, l))
                            hold(pe)
                            if l < NL:
                                each(4 * d + B_LT, 0, HD, lambda j: T2[d][:, 1, j], lambda j: X1[d][:, j])
                                s_tx[d].mark(each(4 * d + B_LT, HALF, HD, lambda j: X1[d][:, j], lambda j: T2[d][:, 1, j]))
                            else:
                                s_tx[d].mark(halves(4 * d + B_LT, HALF, first_half(d), later_half(d), X1[d], T2[d][:, 1], later_half(d)))
                    for d in range(NDIR):
                        pe.wait_ge(*at_step(s_gram_out[d], i, 1, 1))
                        pe.wait_ge(*at_step(s_qr2[d], i, 1, 1))
                        pe.wait_ge(*at_step(s_v_tok[d], i, 1, 1))
                        pe.wait_ge(*at_step(s_st[d], i))
                        hold(pe)
                        for g, j, rows in heads():
                            last = nc.tensor.matmul(BANK[rows, 4 * d + B_L, j * HD:(j + 1) * HD], QRG[d][:, g, 0], STATE_V[d][:, g],
                                                    start=True, stop=True)
                        s_w[d].mark(last)
                    for d in range(NDIR):
                        pe.wait_ge(*at_step(s_w_out[d], i, 1, 1))
                        pe.wait_ge(*at_step(s_t[d], i, LEVELS, LEVELS))
                        hold(pe)
                        s_sa[d].mark(each(4 * d + B_LT, 0, HD, lambda j: T2[d][:, 1, j], lambda j: WS[d][:, j]))
                    for d in range(NDIR):
                        pe.wait_ge(*at_step(s_sa_out[d], i, 1, 1))
                        pe.wait_ge(*at_step(s_bk_tok[d], i, 1, 1))
                        hold(pe)
                        if need_y:
                            for g, j, rows in heads():
                                y = BANK[rows, 4 * d + B_G, j * HD:(j + 1) * HD]
                                nc.tensor.matmul(y, STATE_V[d][:, g], QRG[d][:, g, 1], start=True, stop=False)
                                last = nc.tensor.matmul(y, SA_V[d][UP, g], ARB[d][UP, g], start=False, stop=True)
                            s_y[d].mark(last)
                        pe.wait_ge(*at_step(s_sa_v[d], i, 1, 1))
                        hold(pe)
                        for g, j, rows in heads():
                            last = nc.tensor.matmul(BANK[UP, 4 * d + B_S, g * HD:(g + 1) * HD], BK_TOK[d][:, g], SA_V[d][:, g],
                                                    start=True, stop=True)
                        s_ds[d].mark(last)

                pe.wait_ge(*s_init(1))
                run(pe, step)
        Signal.end_stage()

    TILES = PAIRS * TOK
    OR0 = WORK0 + F0 + 3 * TILES + TOK * 2
    O_R = parts("o_rwkv", OR0, PAIRS)

    def rwkv_output(l, t0, ahead):
        n = TOK - t0
        A1 = carve(WORK, F0 + 6 * WIDTH * 4, PAIRS, TOK)
        A2 = carve(WORK, F0 + 7 * WIDTH * 4, PAIRS, TOK)
        head_rows = carve(WORK, F0 + 5 * WIDTH * 4 + 2 * TOK, TOK)[0:HEADS]
        A3 = carve(WORK, F0 + 8 * WIDTH * 4, PAIRS, TOK)
        A4 = carve(WORK, WORK_USED, PAIRS, TOK)
        with stage() as block:
            @block.sync
            def _(sp):
                ahead.start(sp, SLOTS)
                for x in range(2):
                    sp.dma_start(HS[x].bitcast(FP32).rearrange("p k t -> p (k t)"), H_DRAM[x]).then_inc(h_back, 16)
                sp.wait_ge(h_back, 32 * (l + 1))

            @block.tensor
            def _(pe):
                for j in range(PAIRS):
                    sums.mark(nc.tensor.matmul(BANK[:, j, 0:n], head_ones[:], Y[:, j, t0:], start=True, stop=True))
                for j in range(PAIRS):
                    pe.wait_ge(*scaled(j + 1))
                    product.mark(nc.tensor.matmul(BANK[:, 4 + j, 0:n], head_ones[:], A1[:, j, t0:], start=True, stop=True))
                for j in range(PAIRS):
                    pe.wait_ge(*squares(j + 1))
                    if j == 0:
                        pe.wait_ge(*dve_sig(3))
                    last = nc.tensor.matmul(BANK[0:HEADS, 0, 0:n], pick_heads[:, j], A2[:, j, t0:], start=(j == 0), stop=(j == PAIRS - 1))
                sums.mark(last)
                for j in range(PAIRS):
                    pe.wait_ge(*evacuated(j + 1))
                    product.mark(nc.tensor.matmul(BANK[:, 4 + j, 0:n], g2_sb[:, j * P:(j + 1) * P], Z[:, Z_G, t0:], start=True, stop=True))
                pe.wait_ge(*inverse_rms(1))
                for j in range(PAIRS):
                    h_ready.mark(nc.tensor.matmul(BANK[:, j, 0:n], spread_heads[:, j], head_rows[:, 0:n], start=True, stop=True))

            @block.scalar
            def _(act):
                for j in range(PAIRS):
                    act.wait_ge(*dve_sig(3 * j + 3))
                    squares.mark(nc.scalar.activation(A2[:, j, t0:], Y[:, j, t0:], ACT.Square))
                act.wait_ge(*merged(1))
                inverse_rms.mark(nc.scalar.activation(head_rows[:, 0:n], head_rows[:, 0:n], ACT.Sqrt))
                for j in range(PAIRS):
                    act.wait_ge(*gate_ready(j + 1))
                    high_ready.mark(nc.scalar.activation(O_R[0][:, j, t0:], A4[:, j, t0:], ACT.Copy))

            @block.vector
            def _(dve):
                c = 0
                for j in range(PAIRS):
                    dve_sig.mark(nc.vector.tensor_tensor(A1[:, j, t0:], KD[0][:, j, t0:], KD[1][:, j, t0:], ALU.add))
                    dve.wait_ge(*dve_sig(3 * j + 1))
                    dve_sig.mark(nc.vector.tensor_scalar(A1[:, j, t0:], A1[:, j, t0:], v("r_k", j), None, ALU.mult))
                    dve.wait_ge(*dve_sig(3 * j + 2))
                    scaled.mark(nc.vector.tensor_tensor(A1[:, j, t0:], A1[:, j, t0:], Z[:, Z_R + j, t0:], ALU.mult))
                    dve.wait_ge(*sums(j + 1))
                    dve_sig.mark(nc.vector.scalar_tensor_tensor(Y[:, j, t0:], BANK[:, j, 0:n], -1.0 / HD, Y[:, j, t0:], ALU.mult, ALU.add))
                c = 3 * PAIRS
                for j in range(PAIRS):
                    dve.wait_ge(*product(j + 1))
                    evacuated.mark(nc.vector.tensor_tensor(A3[:, j, t0:], BANK[:, 4 + j, 0:n], Z[:, Z_V + j, t0:], ALU.mult))
                dve.wait_ge(*sums(PAIRS + 1))
                c += 1
                dve_sig.mark(nc.vector.tensor_scalar(head_rows[:, 0:n], BANK[0:HEADS, 0, 0:n], 1.0 / HD, GN_EPS, ALU.mult, ALU.add))
                dve.wait_ge(*dve_sig(c))
                merged.mark(nc.vector.reciprocal(head_rows[:, 0:n], head_rows[:, 0:n]))
                for j in range(PAIRS):
                    dve.wait_ge(*h_ready(j + 1))
                    c += 1
                    dve_sig.mark(nc.vector.scalar_tensor_tensor(Y[:, j, t0:], Y[:, j, t0:], v("gn_w", j), BANK[:, j, 0:n], ALU.mult, ALU.mult))
                    dve.wait_ge(*dve_sig(c))
                    c += 1
                    dve_sig.mark(nc.vector.scalar_tensor_tensor(Y[:, j, t0:], Y[:, j, t0:], v("gn_b", j), A3[:, j, t0:], ALU.add, ALU.add))
                    dve.wait_ge(*dve_sig(c))
                    dve.wait_ge(*product(PAIRS + j + 1))
                    gate_ready.mark(nc.vector.tensor_tensor(A4[:, j, t0:], Y[:, j, t0:], BANK[:, 4 + j, 0:n], ALU.mult))
                for j in range(PAIRS):
                    dve.wait_ge(*high_ready(j + 1))
                    nc.vector.tensor_tensor(O_R[1][:, j, t0:], A4[:, j, t0:], O_R[0][:, j, t0:].bitcast(FP32), ALU.subtract)
        Signal.end_stage()

    ZM = carve(WORK, 0, 5, TOK)
    QH = carve(WORK, 5 * TOK, HEADS, TOK)
    KHD = carve(WORK, (5 + HEADS) * TOK, HEADS, TOK)
    VT = carve(WORK, (5 + 2 * HEADS) * TOK, 4, WIDTH)
    OM1 = (9 + 2 * HEADS) * TOK
    O_M = [place("o_mla_high", WORK0, TILES, FP32R).rearrange("p (k t) -> p k t", t=TOK),
           place("o_mla_low", WORK0 + OM1, TILES, FP32R).rearrange("p (k t) -> p k t", t=TOK)]
    assert WORK0 + OM1 + TILES <= OR0, (OM1, OR0)
    M1 = OR0 - WORK0 + 2 * TILES
    MT = carve(WORK, M1, 4, TOK)
    assert WORK0 + M1 + 5 * TOK <= W0, (M1, W0)

    MLA_ORDER = (3, 2, 0, 1, 4)

    def mla_weights(l):
        wi = ins["w_in"][l]
        sources = [k_tiles(wi, C_MLA + 256, C_MLA + 512), k_tiles(wi, C_MLA, C_MLA + 256), k_tiles(wi, C_MLA + 512, C_FNO)]
        return Chunks(sources, [(0, 0, DT, P, P), (0, 0, DT, 0, P), (1, 0, DT, 0, P), (1, 0, DT, P, P), (2, 0, DT, 0, QK_ROPE)],
                      lambda c: product(c + 1))

    def head_weights(l):
        wq = ins["w_uq"][l].rearrange("(k p) n -> p k n", p=P)
        return Loads([ins["w_ukv"][l].rearrange("(k p) n -> p k n", p=P), wq[:, :, 0:4 * QK], wq[:, :, 4 * QK:8 * QK]])

    def mla_project(l, w, ahead):
        groups = (((3,), KV_LORA, "g_ckv"), ((2, 0, 1), Q_LORA, "g_cq"))
        sq = carve(WORK, 5 * TOK, 6, TOK)
        with stage() as block:
            @block.sync
            def _(sp):
                w.issue(sp, ahead)

            @block.tensor
            def _(pe):
                def sum_group(g, first):
                    tiles = groups[g][0]
                    for i, m in enumerate(tiles):
                        pe.wait_ge(*squares(first + i + 1))
                        last = nc.tensor.matmul(BANK[:, 5 + g], ones[:], sq[:, m], start=(i == 0), stop=(i == len(tiles) - 1))
                    sums.mark(last)

                for c, m in enumerate(MLA_ORDER):
                    wm = w.arrived(pe, c)
                    rows = P if m < 4 else QK_ROPE
                    for k in range(DT):
                        last = product3(BANK[0:rows, m], [x[:, k] for x in wm], [x[:, k] for x in HS], k == 0, k == DT - 1)
                    product.mark(last)
                    if c == 1:
                        sum_group(0, 0)
                    if c == 3:
                        sum_group(1, 1)

            @block.scalar
            def _(act):
                def root(g):
                    act.wait_ge(*merged(g + 1))
                    inverse_rms.mark(nc.scalar.activation(sq[:, 4 + g], sq[:, 4 + g], ACT.Sqrt))

                for c in range(CHUNKS):
                    w.high(act, c)
                for c, m in enumerate(MLA_ORDER):
                    rows = P if m < 4 else QK_ROPE
                    act.wait_ge(*product(c + 1))
                    if m < 4:
                        squares.mark(nc.scalar.activation(sq[:, m], BANK[:, m], ACT.Square))
                    evacuated.mark(nc.scalar.activation(ZM[0:rows, m], BANK[0:rows, m], ACT.Copy))
                    w.high(act, c + CHUNKS)
                    if c == 2:
                        root(0)
                root(1)

            @block.vector
            def _(dve):
                def scale(g):
                    tiles, _, gname = groups[g]
                    dve.wait_ge(*inverse_rms(g + 1))
                    for m in tiles:
                        dve.wait_ge(*evacuated(MLA_ORDER.index(m) + 1))
                        nc.vector.scalar_tensor_tensor(ZM[:, m], ZM[:, m], v(gname, m % 3), sq[:, 4 + g], ALU.mult, ALU.mult)

                for c in range(4):
                    w.low(dve, c)
                for g, (_, width, _) in enumerate(groups):
                    dve.wait_ge(*sums(g + 1))
                    dve_sig.mark(nc.vector.tensor_scalar(sq[:, 4 + g], BANK[:, 5 + g], 1.0 / width, RMS_EPS, ALU.mult, ALU.add))
                    dve.wait_ge(*dve_sig(g + 1))
                    merged.mark(nc.vector.reciprocal(sq[:, 4 + g], sq[:, 4 + g]))
                    if g == 0:
                        w.low(dve, 4)
                    scale(g)
        Signal.end_stage()

    def mla_heads(l, tq, loads):
        units = [("k", h) for h in range(HEADS)] + [("q", h) for h in range(HEADS)]
        U = len(units)
        cos, sin = rope[:, 0:SEQ], rope[:, SEQ:2 * SEQ]
        rotate = rope[:, 2 * SEQ:]
        dst = lambda u: (QH if units[u][0] == "q" else KHD)[0:QK, units[u][1]]
        sq = lambda u: MT[0:QK, u % 2]
        roots = MT[0:U, 2]
        spread = WORK[0:U, M1 + 4 * TOK:M1 + 4 * TOK + U * QK].rearrange("p (u n) -> p u n", n=QK)
        assert WORK0 + M1 + 4 * TOK + U * QK <= W0
        tmp = lambda u: MT[0:QK, 3 + u % 2, 0:SEQ] if u % 2 == 0 else MT[0:QK, 3, SEQ:]
        with stage() as block:
            @block.gpsimd
            def _(pool):
                h_ready.mark(nc.gpsimd.memset(spread, 0.0))
                pool.wait_ge(*h_ready(1))
                h_ready.mark(nc.gpsimd.affine_select(out=spread, in_=spread, compare_op=ALU.not_equal, fill=1.0, base=0,
                                                     pattern=[[-1, 2 * HEADS], [0, QK]], channel_multiplier=1))
                for u in range(U):
                    pool.wait_ge(*gate_ready(u + 1))
                    pool_sig.mark(nc.gpsimd.tensor_tensor(dst(u)[:, CTX:], dst(u)[:, CTX:], cos, ALU.mult))
                    pool.wait_ge(*pool_sig(2 * u + 1))
                    pool_sig.mark(nc.gpsimd.tensor_tensor(dst(u)[:, CTX:], dst(u)[:, CTX:], tmp(u), ALU.add))

            @block.tensor
            def _(pe):
                for u in range(U + 1):
                    if u < U:
                        kind, h = units[u]
                        if u >= 2:
                            pe.wait_ge(*evacuated(u - 1))
                        if kind == "q":
                            w = loads.arrived(pe, 1 + h // 4)
                            for k in range(3):
                                last = nc.tensor.matmul(BANK[0:QK, u % 2, tq:], w[:, k, (h % 4) * QK:(h % 4 + 1) * QK], ZM[:, k, tq:],
                                                        start=(k == 0), stop=(k == 2))
                        else:
                            w = loads.arrived(pe, 0)
                            last = nc.tensor.matmul(BANK[0:QK_NOPE, u % 2], w[:, 0, h * P:h * P + QK_NOPE], ZM[:, 3], start=True, stop=True)
                        product.mark(last)
                    if u >= 1:
                        pe.wait_ge(*squares(u))
                        t = tq if units[u - 1][0] == "q" else 0
                        sums.mark(nc.tensor.matmul(BANK[0:U, 2, t:], pick[:, U - u:2 * U - u], sq(u - 1)[:, t:],
                                                   start=(u == 1), stop=(u == U)))
                w = loads.arrived(pe, 0)
                wv = w[:, 0].rearrange("p (h n) -> p h n", h=HEADS)[:, :, QK_NOPE:]
                for t in range(4):
                    rows_turned.mark(nc.tensor.matmul(BANK[:, 4 + t].rearrange("p (h n) -> p h n", h=HEADS), ZM[:, 3, t * P:(t + 1) * P], wv,
                                                      start=True, stop=True))
                pe.wait_ge(*inverse_rms(1))
                pe.wait_ge(*h_ready(2))
                for u in range(U + 2):
                    if u < U:
                        t = tq if units[u][0] == "q" else 0
                        if u >= 4:
                            pe.wait_ge(*scaled(u - 3))
                        merged.mark(nc.tensor.matmul(BANK[0:QK, u % 4, t:], spread[:, u], roots[:, t:], start=True, stop=True))
                    if u >= 2:
                        pe.wait_ge(*scaled(u - 1))
                        if u < 6:
                            pe.wait_ge(*slot_used(4))
                        else:
                            pe.wait_ge(*gate_ready(u - 5))
                        turned_out.mark(nc.tensor.matmul(BANK[0:QK, 4 + u % 4, 0:SEQ], rotate, dst(u - 2)[:, CTX:], start=True, stop=True))

            @block.scalar
            def _(act):
                for u in range(U):
                    kind, h = units[u]
                    t = tq if kind == "q" else 0
                    rows = QK if kind == "q" else QK_NOPE
                    act.wait_ge(*product(u + 1))
                    if kind == "k":
                        act.wait_ge(*first_cut(h + 1))
                    evacuated.mark(nc.scalar.activation(dst(u)[0:rows, t:], BANK[0:rows, u % 2, t:], ACT.Copy))
                    act.wait_ge(*evacuated(u + 1))
                    if u >= 2:
                        act.wait_ge(*sums(u - 1))
                    squares.mark(nc.scalar.activation(sq(u)[:, t:], dst(u)[:, t:], ACT.Square))
                act.wait_ge(*dve_sig(2))
                inverse_rms.mark(nc.scalar.activation(roots, roots, ACT.Sqrt))
                for t in range(4):
                    act.wait_ge(*rows_turned(t + 1))
                    slot_used.mark(nc.scalar.activation(VT[:, t], BANK[:, 4 + t], ACT.Copy))

            @block.vector
            def _(dve):
                for h in range(HEADS):
                    first_cut.mark(nc.vector.tensor_copy(KHD[QK_NOPE:QK, h], ZM[0:QK_ROPE, 4]))
                dve.wait_ge(*sums(U))
                dve_sig.mark(nc.vector.tensor_scalar(roots, BANK[0:U, 2], 1.0 / QK, RMS_EPS, ALU.mult, ALU.add))
                dve.wait_ge(*dve_sig(1))
                dve_sig.mark(nc.vector.reciprocal(roots, roots))
                for u in range(U + 2):
                    if u < U:
                        t = tq if units[u][0] == "q" else 0
                        g = 0 if units[u][0] == "q" else 1
                        dve.wait_ge(*merged(u + 1))
                        scaled.mark(nc.vector.scalar_tensor_tensor(dst(u)[:, t:], dst(u)[:, t:], g_head[:, g:g + 1], BANK[0:QK, u % 4, t:],
                                                                   ALU.mult, ALU.mult))
                    if u >= 2:
                        dve.wait_ge(*turned_out(u - 1))
                        if u >= 4:
                            dve.wait_ge(*pool_sig(2 * (u - 4) + 2))
                        gate_ready.mark(nc.vector.tensor_tensor(tmp(u), BANK[0:QK, 4 + u % 4, 0:SEQ], sin, ALU.mult))
        Signal.end_stage()

    def attention(tq, ahead):
        units = [(h, q) for h in range(HEADS) for q in range(tq // P, TOK // P)]
        U = len(units)
        keys = lambda u: TOK if units[u][1] * P >= CTX else CTX
        PR = lambda u: MT[:, u % 2]
        PTR = lambda u: MT[:, 2 + u % 2]
        stat = carve(WORK, M1 + 4 * TOK, 3, 2 * len(units) + 1)
        SCORES = (0, 1, 6, 7)
        with stage() as block:
            @block.sync
            def _(sp):
                ahead.start(sp, len(ahead.sources))

            @block.tensor
            def _(pe):
                for u in range(-2, U + 2):
                    if u + 2 < U:
                        h, q = units[u + 2]
                        if u + 2 >= 4:
                            pe.wait_ge(*squares(u - 1))
                        product.mark(nc.tensor.matmul(BANK[:, SCORES[(u + 2) % 4], 0:keys(u + 2)], QH[0:QK, h, q * P:(q + 1) * P],
                                                      KHD[0:QK, h, 0:keys(u + 2)], start=True, stop=True))
                    if u >= 2:
                        h, q = units[u - 2]
                        rows = slice((h % 2) * VH, (h % 2 + 1) * VH)
                        pe.wait_ge(*turned_out(u - 1))
                        if u >= 4:
                            pe.wait_ge(*evacuated(u - 3))
                        n = keys(u - 2) // P
                        for k in range(n):
                            last = nc.tensor.matmul(BANK[rows, 4 + u % 2, 0:P], VT[:, k, h * VH:(h + 1) * VH], PTR(u - 2)[:, k * P:(k + 1) * P],
                                                    start=(k == 0), stop=(k == n - 1))
                        sums.mark(last)
                    if 1 <= u <= U:
                        pe.wait_ge(*scaled(u))
                        if u >= 3:
                            pe.wait_ge(*turned_out(u - 2))
                        for k in range(keys(u - 1) // P):
                            last = nc.tensor.transpose(BANK[:, 2 + (u - 1) % 2, k * P:(k + 1) * P], PR(u - 1)[:, k * P:(k + 1) * P], ident[:])
                        rows_turned.mark(last)

            @block.vector
            def _(dve):
                c = 0
                for u in range(-1, U + 2):
                    if 1 <= u <= U:
                        dve.wait_ge(*squares(u))
                        c += 1
                        dve_sig.mark(nc.vector.reciprocal(stat[:, 2, 2 * u - 1:2 * u], stat[:, 2, 2 * u - 2:2 * u - 1]))
                        dve.wait_ge(*dve_sig(c))
                        scaled.mark(nc.vector.tensor_scalar(PR(u - 1)[:, 0:keys(u - 1)], PR(u - 1)[:, 0:keys(u - 1)], stat[:, 2, 2 * u - 1:2 * u], None, ALU.mult))
                    if u + 1 < U:
                        dve.wait_ge(*product(u + 2))
                        c += 1
                        dve_sig.mark(nc.vector.reduce_max(stat[:, 0, u + 1:u + 2], BANK[:, SCORES[(u + 1) % 4], 0:keys(u + 1)], AX.X))
                        dve.wait_ge(*dve_sig(c))
                        gate_ready.mark(nc.vector.tensor_scalar(stat[:, 1, u + 1:u + 2], stat[:, 0, u + 1:u + 2], -(QK ** -0.5), None, ALU.mult))
                    if u >= 2:
                        h, q = units[u - 2]
                        rows = slice((h % 2) * VH, (h % 2 + 1) * VH)
                        dve.wait_ge(*sums(u - 1))
                        o = [x[rows, h // 2, q * P:(q + 1) * P] for x in O_M]
                        high_ready.mark(nc.vector.tensor_copy(o[0], BANK[rows, 4 + u % 2, 0:P]))
                        dve.wait_ge(*high_ready(u - 1))
                        evacuated.mark(nc.vector.tensor_tensor(o[1], BANK[rows, 4 + u % 2, 0:P], o[0].bitcast(FP32), ALU.subtract))

            @block.scalar
            def _(act):
                for u in range(U + 1):
                    if u < U:
                        act.wait_ge(*gate_ready(u + 1))
                        if u >= 2:
                            act.wait_ge(*rows_turned(u - 1))
                        squares.mark(nc.scalar.activation(PR(u)[:, 0:keys(u)], BANK[:, SCORES[u % 4], 0:keys(u)], ACT.Exp, bias=stat[:, 1, u:u + 1],
                                                          scale=QK ** -0.5, accum_out=stat[:, 2, 2 * u:2 * u + 1]))
                    if u >= 1:
                        act.wait_ge(*rows_turned(u))
                        if u >= 3:
                            act.wait_ge(*sums(u - 2))
                        turned_out.mark(nc.scalar.activation(PTR(u - 1)[:, 0:keys(u - 1)], BANK[:, 2 + (u - 1) % 2, 0:keys(u - 1)], ACT.Copy))
        Signal.end_stage()

    ZF = carve(WORK, TILES, PAIRS, TOK)
    UF = carve(WORK, 2 * TILES, PAIRS, 4, 2 * P)
    OF0 = 4 * TILES
    O_F = parts("o_fourier", WORK0 + OF0, PAIRS)
    assert OF0 + 2 * TILES <= OM1
    dft_feature = carve(WORK, M1, 2 * P)
    dft_token = carve(WORK, M1 + 2 * P, 2, 2 * SEQ)

    def fourier_weights(l):
        wi = ins["w_in"][l]
        return Chunks([k_tiles(wi, C_FNO, C_FNO + 256), k_tiles(wi, C_FNO + 256, C_FNO + 512)],
                      [(m // 2, 0, DT, (m % 2) * P, P) for m in range(PAIRS)], lambda c: product(c + 1))

    def fourier(l, t0, w, ahead):
        n = TOK - t0
        tiles = list(range(t0 // P, 4))
        with stage() as block:
            @block.sync
            def _(sp):
                sp.dma_start(dft_feature, ins["dft_feature"]).then_inc(dft_in, 16)
                sp.dma_start(dft_token, ins["dft_token"].rearrange("(t p) n -> p t n", p=P)).then_inc(dft_in, 16)
                w.issue(sp, ahead)

            @block.tensor
            def _(pe):
                for m in range(PAIRS):
                    wm = w.arrived(pe, m)
                    for k in range(DT):
                        last = product3(BANK[:, m, 0:n], [x[:, k] for x in wm], [x[:, k, t0:] for x in HS], k == 0, k == DT - 1)
                    product.mark(last)
                pe.wait_ge(dft_in, 32 * (l + 1))
                i = 0
                for m in range(PAIRS):
                    pe.wait_ge(*evacuated(m + 1))
                    for t in tiles:
                        if i >= 4:
                            pe.wait_ge(*turned_out(i - 3))
                        rows_turned.mark(nc.tensor.matmul(BANK[:, 4 + i % 4, 0:2 * P], ZF[:, m, t * P:(t + 1) * P], dft_feature, start=True, stop=True))
                        i += 1
                i = 0
                for m in range(PAIRS):
                    for s in range(t0 // CTX, 2):
                        pe.wait_ge(*turned_out(len(tiles) * m + 2 * (s - t0 // CTX) + 2))
                        if i >= 4:
                            pe.wait_ge(*scaled(i - 3))
                        for part in range(2):
                            for t in range(2):
                                last = nc.tensor.matmul(BANK[:, i % 4, 0:SEQ], UF[:, m, 2 * s + t, part * P:(part + 1) * P],
                                                        dft_token[:, t, part * SEQ:(part + 1) * SEQ],
                                                        start=(part == 0 and t == 0), stop=(part == 1 and t == 1))
                        sums.mark(last)
                        i += 1

            @block.scalar
            def _(act):
                for c in range(PAIRS):
                    w.high(act, c)
                for m in range(PAIRS):
                    act.wait_ge(*product(m + 1))
                    evacuated.mark(nc.scalar.activation(ZF[:, m, t0:], BANK[:, m, 0:n], ACT.Copy))
                i = 0
                for m in range(PAIRS):
                    for t in tiles:
                        act.wait_ge(*rows_turned(i + 1))
                        turned_out.mark(nc.scalar.activation(UF[:, m, t], BANK[:, 4 + i % 4, 0:2 * P], ACT.Copy))
                        i += 1
                ahead.high_ahead(act, w)

            @block.vector
            def _(dve):
                for c in range(PAIRS):
                    w.low(dve, c)
                i = 0
                for m in range(PAIRS):
                    for s in range(t0 // CTX, 2):
                        dve.wait_ge(*sums(i + 1))
                        o = [x[:, m, s * SEQ:(s + 1) * SEQ] for x in O_F]
                        dve_sig.mark(nc.vector.tensor_copy(o[0], BANK[:, i % 4, 0:SEQ]))
                        dve.wait_ge(*dve_sig(i + 1))
                        scaled.mark(nc.vector.tensor_tensor(o[1], BANK[:, i % 4, 0:SEQ], o[0].bitcast(FP32), ALU.subtract))
                        i += 1
                ahead.low_ahead(dve, w)
        ahead.early = CHUNKS
        Signal.end_stage()

    MERGE = [place("merge_high", WORK0 + TILES, DT * TOK, FP32R).rearrange("p (k t) -> p k t", t=TOK),
             place("merge_low", WORK0 + M1, DT * TOK, FP32R).rearrange("p (k t) -> p k t", t=TOK)]
    TMP = place("merge_tiles", WORK0 + 3 * TILES, 4 * TOK).rearrange("p (k t) -> p k t", t=TOK)
    assert WORK0 + M1 + DT * TOK <= W0, (WORK0 + M1 + DT * TOK, W0)

    steps = [(mm, b) for mm in range(DT // 2) for b in range(3)]

    def merge_weights(l):
        wi = ins["w_in"][l]
        sources, chunks = [], []
        for i, (mm, b) in enumerate(steps):
            c = C_GATE + b * D + mm * 2 * P
            wo = ins[("w_rwkv_o", "w_mla_o", "w_fno")[b]][l]
            sources += [k_tiles(wi, c, c + 2 * P), k_tiles(wo, mm * 2 * P, (mm + 1) * 2 * P)]
            chunks += [(2 * i, 0, DT, 0, P), (2 * i, 0, DT, P, P), (2 * i + 1, 0, PAIRS, 0, 2 * P)]
        return Chunks(sources, chunks, lambda c: pe_sig(c // 3 * 2 + c % 3 + 1) if c % 3 < 2 else product(c // 3 * 2 + 2))

    def merge(l, t0, w, ahead):
        n = TOK - t0
        branch = (O_R, O_M, O_F)
        gate = lambda u: TMP[:, u % 2, 0:n]
        total = lambda m: TMP[:, 2 + m, 0:n]
        adds = lambda i: sum(2 for x in steps[:i] if x[1] > 0)
        with stage() as block:
            @block.sync
            def _(sp):
                w.issue(sp, ahead)

            @block.tensor
            def _(pe):
                for i, (mm, b) in enumerate(steps):
                    for m in range(2):
                        u = 2 * i + m
                        wg = w.arrived(pe, 3 * i + m)
                        if i > 0:
                            pe.wait_ge(*gate_ready(u - 1))
                        for k in range(DT):
                            last = product3(BANK[:, m, 0:n], [x[:, k] for x in wg], [x[:, k, t0:] for x in HS], k == 0, k == DT - 1)
                        pe_sig.mark(last)
                    wo = w.arrived(pe, 3 * i + 2)
                    for m in range(2):
                        u = 2 * i + m
                        if i > 0:
                            pe.wait_ge(*scaled(u - 1))
                        for k in range(PAIRS):
                            last = product3(BANK[:, 2 + m, 0:n], [x[:, k, m * P:(m + 1) * P] for x in wo], [x[:, k, t0:] for x in branch[b]],
                                            k == 0, k == PAIRS - 1)
                        product.mark(last)

            @block.scalar
            def _(act):
                for c in range(CHUNKS):
                    w.high(act, c)
                for i, (mm, b) in enumerate(steps):
                    for m in range(2):
                        u = 2 * i + m
                        act.wait_ge(*pe_sig(u + 1))
                        w.high(act, 3 * (i + 1) + m)
                        if u >= 2:
                            act.wait_ge(*scaled(u - 1))
                            if adds(i) and steps[i - 1][1] > 0:
                                act.wait_ge(*pool_sig(adds(i - 1) + m + 1))
                        gate_ready.mark(nc.scalar.activation(gate(u), BANK[:, m, 0:n], ACT.Sigmoid))
                    if b == 2:
                        for m in range(2):
                            act.wait_ge(*pool_sig(adds(i) + m + 1))
                            merged.mark(nc.scalar.activation(MERGE[0][:, 2 * mm + m, t0:], total(m), ACT.Copy))
                    w.high(act, 3 * (i + 1) + 2)
                ahead.high_ahead(act, w)

            @block.vector
            def _(dve):
                for c in range(CHUNKS):
                    w.low(dve, c)
                for i, (mm, b) in enumerate(steps):
                    for m in range(2):
                        w.low(dve, 3 * (i + 1) + m)
                    for m in range(2):
                        u = 2 * i + m
                        dve.wait_ge(*gate_ready(u + 1))
                        dve.wait_ge(*product(u + 1))
                        if b == 0:
                            if mm > 0:
                                dve.wait_ge(*h_ready(2 * (mm - 1) + m + 1))
                            scaled.mark(nc.vector.tensor_tensor(total(m), gate(u), BANK[:, 2 + m, 0:n], ALU.mult))
                        else:
                            scaled.mark(nc.vector.tensor_tensor(gate(u), gate(u), BANK[:, 2 + m, 0:n], ALU.mult))
                    if b == 2:
                        for m in range(2):
                            dve.wait_ge(*merged(2 * mm + m + 1))
                            h_ready.mark(nc.vector.tensor_tensor(MERGE[1][:, 2 * mm + m, t0:], total(m),
                                                                 MERGE[0][:, 2 * mm + m, t0:].bitcast(FP32), ALU.subtract))
                    w.low(dve, 3 * (i + 1) + 2)
                ahead.low_ahead(dve, w)

            @block.gpsimd
            def _(pool):
                for i, (mm, b) in enumerate(steps):
                    for m in range(2):
                        u = 2 * i + m
                        if b > 0:
                            pool.wait_ge(*scaled(u + 1))
                            if b > 1:
                                pool.wait_ge(*pool_sig(adds(i) - 2 + m + 1))
                            pool_sig.mark(nc.gpsimd.tensor_tensor(total(m), total(m), gate(u), ALU.add))
        ahead.early = CHUNKS
        Signal.end_stage()

    def add_to_stream(dve, m, bank, which, t0, mark):
        for s in range(t0 // CTX, 2):
            a = s * CTX
            last = nc.vector.scalar_tensor_tensor(X[:, m, a:a + CTX], BANK[:, bank, a - t0:a - t0 + CTX], mod[:, which, m, s:s + 1],
                                                  X[:, m, a:a + CTX], ALU.mult, ALU.add)
        mark(last)

    def out_weights(l):
        return Chunks([k_tiles(ins["w_out"][l], c, c + 2 * P) for c in range(0, D, 2 * P)],
                      [(m // 2, 0, DT, (m % 2) * P, P) for m in range(DT)], lambda c: product(c + 1))

    def project_out(l, t0, w, ahead):
        n = TOK - t0
        with stage() as block:
            @block.sync
            def _(sp):
                w.issue(sp, ahead)

            @block.tensor
            def _(pe):
                for m in range(DT):
                    wm = w.arrived(pe, m)
                    for k in range(DT):
                        last = product3(BANK[:, m, 0:n], [x[:, k] for x in wm], [x[:, k, t0:] for x in MERGE], k == 0, k == DT - 1)
                    product.mark(last)

            @block.scalar
            def _(act):
                for c in range(DT):
                    w.high(act, c)

            @block.vector
            def _(dve):
                for c in range(CHUNKS):
                    w.low(dve, c)
                for m in range(DT):
                    dve.wait_ge(*product(m + 1))
                    add_to_stream(dve, m, m, 2, t0, evacuated.mark)
                    w.low(dve, m + CHUNKS)
        Signal.end_stage()

    HID = parts("hidden", WORK0, FT)
    FTMP = place("ffn_tiles", WORK0 + 2 * FT * TOK, 2 * TOK).rearrange("p (k t) -> p k t", t=TOK)
    assert WORK0 + 2 * FT * TOK + 2 * TOK <= W0, (W0,)

    def ffn_in_weights(l):
        wi = ins["w_ffn_in"][l]
        sources = []
        for c in range(0, FFN, 2 * P):
            sources += [k_tiles(wi, c, c + 2 * P), k_tiles(wi, FFN + c, FFN + c + 2 * P)]
        return Chunks(sources, [(u // 2 * 2 + g, 0, DT, (u % 2) * P, P) for u in range(FT) for g in range(2)],
                      lambda c: (product if c % 2 else pe_sig)(c // 2 + 1))

    def ffn_in(l, t0, w, ahead):
        n = TOK - t0
        tile = lambda u: FTMP[:, u % 2, 0:n]
        with stage() as block:
            @block.sync
            def _(sp):
                w.issue(sp, ahead)

            @block.tensor
            def _(pe):
                pe_sig.count(pe)
                for u in range(FT):
                    for g in range(2):
                        if u + g == 0:
                            continue
                        wm = w.arrived(pe, 2 * u + g)
                        if u >= 2:
                            pe.wait_ge(*(gate_ready if g == 0 else scaled)(u - 1))
                        for k in range(DT):
                            last = product3(BANK[:, 2 * g + u % 2, 0:n], [x[:, k] for x in wm], [x[:, k, t0:] for x in HS], k == 0, k == DT - 1)
                        (pe_sig if g == 0 else product).mark(last)

            @block.scalar
            def _(act):
                for c in range(CHUNKS):
                    w.high(act, c)
                for u in range(FT):
                    act.wait_ge(*pe_sig(u + 1))
                    w.high(act, 2 * u + CHUNKS)
                    if u >= 2:
                        act.wait_ge(*evacuated(u - 1))
                    gate_ready.mark(nc.scalar.activation(tile(u), BANK[:, u % 2, 0:n], ACT.Silu))
                    w.high(act, 2 * u + 1 + CHUNKS)
                    act.wait_ge(*scaled(u + 1))
                    merged.mark(nc.scalar.activation(HID[0][:, u, t0:], tile(u), ACT.Copy))
                ahead.high_ahead(act, w)

            @block.vector
            def _(dve):
                for c in range(CHUNKS):
                    w.low(dve, c)
                for u in range(FT):
                    w.low(dve, 2 * u + CHUNKS)
                    dve.wait_ge(*gate_ready(u + 1))
                    dve.wait_ge(*product(u + 1))
                    scaled.mark(nc.vector.tensor_tensor(tile(u), tile(u), BANK[:, 2 + u % 2, 0:n], ALU.mult))
                    w.low(dve, 2 * u + 1 + CHUNKS)
                    dve.wait_ge(*merged(u + 1))
                    evacuated.mark(nc.vector.tensor_tensor(HID[1][:, u, t0:], tile(u), HID[0][:, u, t0:].bitcast(FP32), ALU.subtract))
                ahead.low_ahead(dve, w)
        ahead.early = CHUNKS
        Signal.end_stage()

    def ffn_out_weights(l):
        wo = ins["w_ffn_out"][l].rearrange("(k p) n -> p k n", p=P)
        return Chunks([wo[:, k:k + 2, :] for k in range(0, FT, 2)], [(k // 2, k % 2, 1, 0, D) for k in range(FT)],
                      lambda c: slot_used(c + 1) if c < FT - 1 else product(DT))

    def ffn_out(l, t0, w, ahead):
        n = TOK - t0
        with stage() as block:
            @block.sync
            def _(sp):
                w.issue(sp, ahead)

            @block.tensor
            def _(pe):
                for k in range(FT):
                    wk = w.arrived(pe, k)
                    for m in range(DT):
                        last = product3(BANK[:, m, 0:n], [x[:, 0, m * P:(m + 1) * P] for x in wk], [x[:, k, t0:] for x in HID],
                                        k == 0, k == FT - 1)
                        if k == FT - 1:
                            product.mark(last)
                    if k < FT - 1:
                        slot_used.mark(last)

            @block.scalar
            def _(act):
                for c in range(FT):
                    w.high(act, c)
                if ahead:
                    ahead.high_ahead(act, w)

            @block.vector
            def _(dve):
                for c in range(FT):
                    w.low(dve, c)
                for m in range(DT):
                    dve.wait_ge(*product(m + 1))
                    add_to_stream(dve, m, m, 5, t0, evacuated.mark)
                if ahead:
                    ahead.low_ahead(dve, w)
        if ahead:
            ahead.early = CHUNKS
        Signal.end_stage()

    for l in range(DEPTH):
        t0 = CTX if l == DEPTH - 1 else 0
        w_rwkv = rwkv_weights(l)
        modulation(l, w_modulation, w_rwkv)
        norm(scale_1, mod[:, 0], 0, w_rwkv, save=True)
        project_rwkv(l, w_rwkv)
        features()
        scan(l < DEPTH - 1)
        w_mla, w_heads, w_fourier = mla_weights(l), head_weights(l), fourier_weights(l)
        rwkv_output(l, t0, w_mla)
        mla_project(l, w_mla, w_heads)
        mla_heads(l, t0, w_heads)
        attention(t0, w_fourier)
        w_merge, w_out = merge_weights(l), out_weights(l)
        fourier(l, t0, w_fourier, w_merge)
        merge(l, t0, w_merge, w_out)
        w_ffn_in, w_ffn_out = ffn_in_weights(l), ffn_out_weights(l)
        project_out(l, t0, w_out, w_ffn_in)
        norm(scale_2, mod[:, 3], t0, w_ffn_in)
        ffn_in(l, t0, w_ffn_in, w_ffn_out)
        w_modulation = modulation_weights(l + 1) if l + 1 < DEPTH else None
        ffn_out(l, t0, w_ffn_out, w_modulation)

    result = carve(WORK, 0, 2, D)
    with stage() as block:
        @block.tensor
        def _(pe):
            for b in range(4):
                for q in range(4):
                    t, k = b // 2, (b % 2) * 4 + q
                    last = nc.tensor.transpose(BANK[:, b, q * P:(q + 1) * P], X[:, k, CTX + t * P:CTX + (t + 1) * P], ident[:])
                rows_turned.mark(last)

        @block.vector
        def _(dve):
            for b in range(4):
                dve.wait_ge(*rows_turned(b + 1))
                turned_out.mark(nc.vector.tensor_copy(result[:, b // 2, (b % 2) * 512:(b % 2 + 1) * 512], BANK[:, b]))

        @block.sync
        def _(sp):
            sp.wait_ge(*turned_out(4))
            sp.dma_start(out[0].rearrange("(t p) d -> p t d", p=P), result).then_inc(out_stored, 16)
            sp.wait_ge(out_stored, 16)
    Signal.end_stage()


def kernel(**inputs):
    from concourse import bacc
    from concourse.bass_utils import run_bass_kernel_spmd

    nc = bacc.Bacc("TRN2", target_bir_lowering=False, num_devices=1)
    arrays, aps = {}, {}
    for name, a in {**inputs, **shape_constants()}.items():
        a = np.ascontiguousarray(a)
        arrays[f"{name}_dram"] = a
        aps[name] = nc.dram_tensor(f"{name}_dram", a.shape, mybir.dt.from_np(a.dtype), kind="ExternalInput").ap()
    out = nc.dram_tensor("out_dram", (1, SEQ, D), FP32, kind="ExternalOutput").ap()
    build(nc, aps, out)
    result = run_bass_kernel_spmd(nc, [arrays], core_ids=[0])
    return result.results[0]["out_dram"]
```
